# Optimizing a Trainium2 kernel written in Bass

```python
import math
import jax, jax.numpy as jnp
from jax import lax
import numpy as np
import jax
import jax.numpy as jnp

D_MODEL = 1024
BATCH = 1
SEQ = 256
DEPTH = 2

GRID_W = 64
CTX_LEN = 256
N_MIXERS = 2
MIXER_ATTN = 0
MIXER_POOL = 1
N_HEADS = 8
HEAD_DIM = 64
V_DIM = 2 * HEAD_DIM
QK_WIDTH = N_HEADS * 2 * HEAD_DIM
V_WIDTH = N_HEADS * V_DIM
ROPE_BASE = 10000.0
ROPE_PAIRS_PER_AXIS = HEAD_DIM // 4
POOL_WINDOWS = (2, 4, 8, 16)
N_POOL_GROUPS = len(POOL_WINDOWS)
POOL_GROUP = D_MODEL // N_POOL_GROUPS
D_FF = -(-8 * D_MODEL // (3 * 256)) * 256
Q_BLOCK = 128
ALPHA = (2.0 * DEPTH) ** 0.25
BETA = (8.0 * DEPTH) ** -0.25
LN_EPS = 1e-5
N_MOD = 6
N_ATTN_LAYERS = (DEPTH + 1) // 2
N_POOL_LAYERS = DEPTH // 2


def layer_norm(x, g, b):
    xf = x.astype(jnp.float32)
    mu = jnp.mean(xf, axis=-1, keepdims=True)
    var = jnp.mean(jnp.square(xf - mu), axis=-1, keepdims=True)
    return ((xf - mu) * lax.rsqrt(var + LN_EPS) * g + b).astype(x.dtype)

def adaln_params(cond, w_mod, b_mod):
    m = jax.nn.silu(cond) @ w_mod + b_mod
    return jnp.split(m, N_MOD, axis=-1)

def modulate(h, shift, scale):
    return h * (1 + scale) + shift

def axial_rope_tables(rows, dtype):
    row = jnp.repeat(jnp.arange(rows, dtype=jnp.float32), GRID_W)
    col = jnp.tile(jnp.arange(GRID_W, dtype=jnp.float32), rows)
    inv = jnp.power(ROPE_BASE, -jnp.arange(ROPE_PAIRS_PER_AXIS, dtype=jnp.float32) / ROPE_PAIRS_PER_AXIS)
    ang = jnp.concatenate([row[:, None] * inv, col[:, None] * inv], axis=-1)
    cos = jnp.cos(ang)[:, None, None, :].astype(dtype)
    sin = jnp.sin(ang)[:, None, None, :].astype(dtype)
    return cos, sin

def apply_rope(x, cos, sin):
    half = HEAD_DIM // 2
    x1, x2 = x[..., :half], x[..., half:]
    return jnp.concatenate([x1 * cos - x2 * sin, x1 * sin + x2 * cos], axis=-1)

def project_q(h, w_qkv):
    B, S = h.shape[:2]
    return (h @ w_qkv[:, :QK_WIDTH]).reshape(B, S, N_HEADS, 2, HEAD_DIM)

def project_kv(h, w_qkv):
    B, S = h.shape[:2]
    kv = h @ w_qkv[:, QK_WIDTH:]
    k = kv[..., :QK_WIDTH].reshape(B, S, N_HEADS, 2, HEAD_DIM)
    v = kv[..., QK_WIDTH:].reshape(B, S, N_HEADS, V_DIM)
    return k, v

def diff_softmax_mix(q, k, v, lam):
    s = jnp.einsum('bqhmd,bkhmd->bhmqk', q * (HEAD_DIM ** -0.5), k).astype(jnp.float32)
    p = jax.nn.softmax(s, axis=-1)
    a = p[:, :, 0] - lam * p[:, :, 1]
    return jnp.einsum('bhqk,bkhe->bqhe', a.astype(v.dtype), v)

def diff_head_out(o, subln_g, lam_init, w_o):
    B, Q = o.shape[:2]
    of = o.astype(jnp.float32)
    of = of * lax.rsqrt(jnp.mean(of * of, axis=-1, keepdims=True) + LN_EPS) * subln_g * (1.0 - lam_init)
    return of.astype(o.dtype).reshape(B, Q, V_WIDTH) @ w_o

def latent_diff_attention(q_l, k_all, v_all, lam):
    B, S = q_l.shape[:2]
    n_blk = S // Q_BLOCK
    qb = jnp.moveaxis(q_l.reshape(B, n_blk, Q_BLOCK, N_HEADS, 2, HEAD_DIM), 1, 0)
    ob = lax.map(lambda q: diff_softmax_mix(q, k_all, v_all, lam), qb)
    return jnp.moveaxis(ob, 0, 1).reshape(B, S, N_HEADS, V_DIM)

def multiscale_pool(h, w_pool, pool_scale):
    B, S, D = h.shape
    hf = h.astype(jnp.float32)
    cs = jnp.concatenate([jnp.zeros((B, 1, D), jnp.float32), lax.cumsum(hf, axis=1)], axis=1)
    t = jnp.arange(S)
    outs = []
    for g, w in enumerate(POOL_WINDOWS):
        lo = jnp.clip(t - w // 2, 0, S)
        hi = jnp.clip(t + w - w // 2, 0, S)
        cg = cs[..., g * POOL_GROUP:(g + 1) * POOL_GROUP]
        mean = (cg[:, hi] - cg[:, lo]) / (hi - lo).astype(jnp.float32)[None, :, None]
        outs.append(mean - hf[..., g * POOL_GROUP:(g + 1) * POOL_GROUP])
    pooled = jnp.stack(outs, axis=2).astype(h.dtype)
    y = jnp.einsum('bsgi,gio->bsgo', pooled, w_pool).reshape(B, S, D)
    return y * pool_scale

def swiglu(h, w_in, w_out):
    g, u = jnp.split(h @ w_in, 2, axis=-1)
    return (jax.nn.silu(g) * u) @ w_out

def reads_context(layer):
    return (layer % N_MIXERS) == MIXER_ATTN

def first_inputs(seed: int = 0) -> dict:
    key = jax.random.key(seed)
    ks = jax.random.split(key, 16)
    D = D_MODEL
    f32 = jnp.float32
    return {
        "x": jax.random.normal(ks[0], (BATCH, SEQ, D), f32),
        "c": jax.random.normal(ks[1], (BATCH, D), f32),
        "ctx": jax.random.normal(ks[2], (BATCH, CTX_LEN, D), f32),
        "c_ctx": jax.random.normal(ks[3], (D,), f32),
        "w_mod": jax.random.normal(ks[4], (DEPTH, D, N_MOD * D), f32) * (0.5 * D ** -0.5),
        "b_mod": jax.random.normal(ks[5], (DEPTH, N_MOD * D), f32) * 0.01,
        "ln_g": 1.0 + 0.02 * jax.random.normal(ks[6], (DEPTH, 2, D), f32),
        "ln_b": 0.02 * jax.random.normal(ks[7], (DEPTH, 2, D), f32),
        "attn_w_qkv": jax.random.normal(ks[8], (N_ATTN_LAYERS, D, QK_WIDTH + QK_WIDTH + V_WIDTH), f32) * D ** -0.5,
        "attn_lambda": 0.1 * jax.random.normal(ks[9], (N_ATTN_LAYERS, 4, HEAD_DIM), f32),
        "attn_subln_g": 1.0 + 0.02 * jax.random.normal(ks[10], (N_ATTN_LAYERS, V_DIM), f32),
        "attn_w_o": jax.random.normal(ks[11], (N_ATTN_LAYERS, V_WIDTH, D), f32) * (V_WIDTH ** -0.5 * BETA),
        "pool_w": jax.random.normal(ks[12], (N_POOL_LAYERS, N_POOL_GROUPS, POOL_GROUP, POOL_GROUP), f32) * (POOL_GROUP ** -0.5 * BETA),
        "pool_scale": 0.5 + 0.05 * jax.random.normal(ks[13], (N_POOL_LAYERS, D), f32),
        "ffn_w_in": jax.random.normal(ks[14], (DEPTH, D, 2 * D_FF), f32) * D ** -0.5,
        "ffn_w_out": jax.random.normal(ks[15], (DEPTH, D_FF, D), f32) * (D_FF ** -0.5 * BETA),
    }

def first_block(x, c, ctx, c_ctx, w_mod, b_mod, ln_g, ln_b, attn_w_qkv, attn_lambda, attn_subln_g,
              attn_w_o, pool_w, pool_scale, ffn_w_in, ffn_w_out):
    n_lat = x.shape[1]
    rows = n_lat // GRID_W
    cos, sin = axial_rope_tables(rows, x.dtype)
    h_ctx = ctx
    for i in range(DEPTH):
        mixer = i % N_MIXERS
        ctx_later = any(reads_context(j) for j in range(i + 1, DEPTH))
        sh1, sc1, g1, sh2, sc2, g2 = adaln_params(c[:, None, :], w_mod[i], b_mod[i])
        csh1, csc1, cg1, csh2, csc2, cg2 = adaln_params(c_ctx, w_mod[i], b_mod[i])
        hx = modulate(x, sh1, sc1)
        hc = modulate(h_ctx, csh1, csc1)
        if mixer == MIXER_ATTN:
            a = i // N_MIXERS
            lam_init = 0.8 - 0.6 * math.exp(-0.3 * i)
            lp = attn_lambda[a].astype(jnp.float32)
            lam = jnp.exp(jnp.sum(lp[0] * lp[1])) - jnp.exp(jnp.sum(lp[2] * lp[3])) + lam_init
            w_qkv = attn_w_qkv[a]
            k_c, v_c = project_kv(hc, w_qkv)
            q_l = apply_rope(project_q(hx, w_qkv), cos, sin)
            k_l, v_l = project_kv(hx, w_qkv)
            k_l = apply_rope(k_l, cos, sin)
            k_all = jnp.concatenate([k_c, k_l], axis=1)
            v_all = jnp.concatenate([v_c, v_l], axis=1)
            y_lat = diff_head_out(latent_diff_attention(q_l, k_all, v_all, lam),
                                  attn_subln_g[a], lam_init, attn_w_o[a])
            if ctx_later:
                q_c = project_q(hc, w_qkv)
                y_ctx = diff_head_out(diff_softmax_mix(q_c, k_c, v_c, lam),
                                      attn_subln_g[a], lam_init, attn_w_o[a])
        else:
            p = i // N_MIXERS
            y_lat = multiscale_pool(hx, pool_w[p], pool_scale[p])
            if ctx_later:
                y_ctx = multiscale_pool(hc, pool_w[p], pool_scale[p])
        x = layer_norm(ALPHA * x + g1 * y_lat, ln_g[i, 0], ln_b[i, 0])
        x = layer_norm(ALPHA * x + g2 * swiglu(modulate(x, sh2, sc2), ffn_w_in[i], ffn_w_out[i]),
                       ln_g[i, 1], ln_b[i, 1])
        if ctx_later:
            h_ctx = layer_norm(ALPHA * h_ctx + cg1 * y_ctx, ln_g[i, 0], ln_b[i, 0])
            h_ctx = layer_norm(ALPHA * h_ctx + cg2 * swiglu(modulate(h_ctx, csh2, csc2), ffn_w_in[i], ffn_w_out[i]),
                               ln_g[i, 1], ln_b[i, 1])
    return x


DEPTH_2 = 1

NORM_EPS = 1e-6

REL_BUCKETS = 32
REL_MAX_DIST = 2048

A_HEADS = 8
A_IDX_HEADS = 4
A_IDX_DIM = 64
A_TOPK_MAX = 256

B_HEADS = 8
B_KV_HEADS = 2
B_GROUP = B_HEADS // B_KV_HEADS
B_CMP_LEN = 32
B_CMP_STRIDE = 16
B_SEL_LEN = 64
B_SEL_TOPK_MAX = 16
B_WINDOW = 512
B_Q_BLOCK = 64

C_GROUPS = ((128, 1), (512, 4), (2048, 16))
C_HEADS_PER_GROUP = 4
C_HEADS = C_HEADS_PER_GROUP * len(C_GROUPS)
C_PAD = 2048

REL_HEADS = A_HEADS + B_HEADS + C_HEADS

D_FF_2 = ((8 * D_MODEL + 3 * 256 - 1) // (3 * 256)) * 256

IN_SIZES = (
    A_HEADS * HEAD_DIM,
    HEAD_DIM,
    HEAD_DIM,
    A_IDX_HEADS * A_IDX_DIM,
    A_IDX_DIM,
    A_IDX_HEADS,
    B_HEADS * HEAD_DIM,
    6 * B_KV_HEADS * HEAD_DIM,
    3 * B_HEADS,
    3 * C_HEADS * HEAD_DIM,
    3 * D_MODEL,
)
IN_TOTAL = sum(IN_SIZES)


def _rms(x, g):
    xf = x.astype(jnp.float32)
    y = xf * lax.rsqrt(jnp.mean(xf * xf, axis=-1, keepdims=True) + NORM_EPS)
    return (y * g.astype(jnp.float32)).astype(x.dtype)

def _split_last(y, sizes):
    out, off = [], 0
    for n in sizes:
        out.append(y[..., off:off + n])
        off += n
    return out

def _rel_bucket(dist):
    n = jnp.maximum(dist, 0)
    exact = REL_BUCKETS // 2
    nf = jnp.maximum(n, 1).astype(jnp.float32)
    large = exact + (jnp.log(nf / exact) / math.log(REL_MAX_DIST / exact)
                     * (REL_BUCKETS - exact)).astype(jnp.int32)
    return jnp.where(n < exact, n, jnp.minimum(large, REL_BUCKETS - 1))

def _masked_softmax(logits, mask):
    s = jnp.where(mask, logits, -jnp.inf)
    m = jnp.max(s, axis=-1, keepdims=True)
    m = jnp.where(jnp.isfinite(m), m, 0.0)
    e = jnp.exp(s - m)
    den = jnp.sum(e, axis=-1, keepdims=True)
    p = e / jnp.maximum(den, 1e-30)
    lse = (m + jnp.log(den))[..., 0]
    return p, lse

def _sweep(fn, seq, block):
    out = lax.map(fn, jnp.arange(seq // block))
    out = jnp.moveaxis(out, 0, 1)
    return out.reshape((out.shape[0], seq) + out.shape[3:])

_gather_rows = jax.vmap(lambda a, i: a[i])

def _dsa_attention(q, k, v, iq, ik, iw, rel_tab):
    seq = q.shape[1]
    topk = min(A_TOPK_MAX, seq // 4)
    scale = HEAD_DIM ** -0.5
    keys = jnp.arange(seq)

    def block(i):
        q0 = i * Q_BLOCK
        t = q0 + jnp.arange(Q_BLOCK)
        qb = lax.dynamic_slice_in_dim(q, q0, Q_BLOCK, axis=1)
        iqb = lax.dynamic_slice_in_dim(iq, q0, Q_BLOCK, axis=1)
        iwb = lax.dynamic_slice_in_dim(iw, q0, Q_BLOCK, axis=1).astype(jnp.float32)
        rel = jax.nn.relu(jnp.einsum("bqhd,bsd->bqhs", iqb, ik, preferred_element_type=jnp.float32))
        score = jnp.einsum("bqhs,bqh->bqs", rel, iwb)
        score = jnp.where(keys[None, None, :] <= t[None, :, None], score, -jnp.inf)
        _, idx = lax.top_k(score, topk)
        kg = _gather_rows(k, idx)
        vg = _gather_rows(v, idx)
        dist = t[None, :, None] - idx
        bias = jnp.moveaxis(rel_tab[_rel_bucket(dist)], -1, 1)
        logits = jnp.einsum("bqhd,bqkd->bhqk", qb, kg, preferred_element_type=jnp.float32) * scale + bias
        p, _ = _masked_softmax(logits, (dist >= 0)[:, None])
        return jnp.einsum("bhqk,bqkd->bqhd", p.astype(vg.dtype), vg).astype(q.dtype)

    o = _sweep(block, seq, Q_BLOCK)
    return o.reshape(o.shape[:2] + (A_HEADS * HEAD_DIM,))

def _nsa_attention(q, kc, vc, ks, vs, kw, vw, gates, cmp_pos, cmp_w, k_gain, rel_tab):
    bsz, seq = q.shape[:2]
    G, Hg, Dh = B_KV_HEADS, B_GROUP, HEAD_DIM
    scale = Dh ** -0.5
    n_cmp = (seq - B_CMP_LEN) // B_CMP_STRIDE + 1
    n_sel = seq // B_SEL_LEN
    n_top = min(B_SEL_TOPK_MAX, n_sel)

    cidx = jnp.arange(n_cmp)[:, None] * B_CMP_STRIDE + jnp.arange(B_CMP_LEN)[None, :]

    def compress(src, pos, w):
        blk = src[:, cidx] + pos[:, None, :]
        return jnp.einsum("bnlgd,lde->bnge", blk, w)

    kcmp = _rms(compress(kc, cmp_pos[0], cmp_w[0]), k_gain)
    vcmp = compress(vc, cmp_pos[1], cmp_w[1])
    cstart = cidx[:, 0]
    cend = cidx[:, -1]
    sstart = jnp.arange(n_sel) * B_SEL_LEN
    overlap = ((cstart[:, None] < sstart[None, :] + B_SEL_LEN)
               & (cstart[:, None] + B_CMP_LEN > sstart[None, :])).astype(jnp.float32)
    ksb = jnp.moveaxis(ks.reshape(bsz, n_sel, B_SEL_LEN, G, Dh), 3, 1)
    vsb = jnp.moveaxis(vs.reshape(bsz, n_sel, B_SEL_LEN, G, Dh), 3, 1)
    wpad = ((0, 0), (B_WINDOW, 0), (0, 0), (0, 0))
    kw_pad = jnp.pad(kw, wpad)
    vw_pad = jnp.pad(vw, wpad)
    tab = rel_tab.reshape(REL_BUCKETS, G, Hg)
    sel_blocks = jnp.arange(n_sel)
    gather_blocks = jax.vmap(jax.vmap(lambda a, i: a[i]))
    bias_per_group = jax.vmap(lambda tb, bk: tb[bk], in_axes=(1, 1), out_axes=1)

    def block(i):
        q0 = i * B_Q_BLOCK
        t = q0 + jnp.arange(B_Q_BLOCK)
        qb = lax.dynamic_slice_in_dim(q, q0, B_Q_BLOCK, axis=1).reshape(bsz, B_Q_BLOCK, G, Hg, Dh)
        gb = lax.dynamic_slice_in_dim(gates, q0, B_Q_BLOCK, axis=1).reshape(bsz, B_Q_BLOCK, G, Hg, 3)
        lc = jnp.einsum("bqghd,bngd->bghqn", qb, kcmp, preferred_element_type=jnp.float32) * scale
        pc, _ = _masked_softmax(lc, cend[None, :] <= t[:, None])
        oc = jnp.einsum("bghqn,bngd->bqghd", pc.astype(vcmp.dtype), vcmp)
        imp = jnp.einsum("bghqn,nm->bgqm", pc, overlap)
        jt = (t // B_SEL_LEN)[:, None]
        forced = (sel_blocks[None] == 0) | (sel_blocks[None] == jt) | (sel_blocks[None] == jt - 1)
        imp = jnp.where(forced, jnp.inf, jnp.where(sel_blocks[None] <= jt, imp, -jnp.inf))
        _, sel = lax.top_k(imp, n_top)
        kg = gather_blocks(ksb, sel).reshape(bsz, G, B_Q_BLOCK, n_top * B_SEL_LEN, Dh)
        vg = gather_blocks(vsb, sel).reshape(bsz, G, B_Q_BLOCK, n_top * B_SEL_LEN, Dh)
        pos = (sel[..., None] * B_SEL_LEN + jnp.arange(B_SEL_LEN)).reshape(bsz, G, B_Q_BLOCK, -1)
        dist = t[None, None, :, None] - pos
        bias_s = jnp.moveaxis(bias_per_group(tab, _rel_bucket(dist)), -1, 2)
        ls = jnp.einsum("bqghd,bgqkd->bghqk", qb, kg, preferred_element_type=jnp.float32) * scale + bias_s
        ps, _ = _masked_softmax(ls, (dist >= 0)[:, :, None])
        osel = jnp.einsum("bghqk,bgqkd->bqghd", ps.astype(vg.dtype), vg)
        kwb = lax.dynamic_slice_in_dim(kw_pad, q0, B_Q_BLOCK + B_WINDOW, axis=1)
        vwb = lax.dynamic_slice_in_dim(vw_pad, q0, B_Q_BLOCK + B_WINDOW, axis=1)
        kpos = q0 - B_WINDOW + jnp.arange(B_Q_BLOCK + B_WINDOW)
        dw = t[:, None] - kpos[None, :]
        mw = (dw >= 0) & (dw < B_WINDOW) & (kpos[None, :] >= 0)
        bias_w = jnp.transpose(tab[_rel_bucket(dw)], (2, 3, 0, 1))
        lw = jnp.einsum("bqghd,bkgd->bghqk", qb, kwb, preferred_element_type=jnp.float32) * scale + bias_w
        pw, _ = _masked_softmax(lw, mw)
        ow = jnp.einsum("bghqk,bkgd->bqghd", pw.astype(vwb.dtype), vwb)
        o = gb[..., 0:1] * oc + gb[..., 1:2] * osel + gb[..., 2:3] * ow
        return o.reshape(bsz, B_Q_BLOCK, G * Hg * Dh).astype(q.dtype)

    return _sweep(block, seq, B_Q_BLOCK)

def _dilated_attention(q, k, v, rel_tab):
    bsz, seq = q.shape[:2]
    scale = HEAD_DIM ** -0.5
    pad = ((0, 0), (C_PAD, 0), (0, 0), (0, 0))
    hsl = [slice(g * C_HEADS_PER_GROUP, (g + 1) * C_HEADS_PER_GROUP) for g in range(len(C_GROUPS))]
    kps = [jnp.pad(k[:, :, hs], pad) for hs in hsl]
    vps = [jnp.pad(v[:, :, hs], pad) for hs in hsl]

    def block(i):
        q0 = i * Q_BLOCK
        t = q0 + jnp.arange(Q_BLOCK)
        qb = lax.dynamic_slice_in_dim(q, q0, Q_BLOCK, axis=1)
        outs, lses = [], []
        for gi, (win, dil) in enumerate(C_GROUPS):
            steps = jnp.arange(win // dil + 1) * dil
            pos = t[:, None] - steps[None, :]
            kg = jnp.take(kps[gi], pos + C_PAD, axis=1)
            vg = jnp.take(vps[gi], pos + C_PAD, axis=1)
            bias = rel_tab[_rel_bucket(steps), hsl[gi]].T[None, :, None, :]
            logits = jnp.einsum("bqhd,bqkhd->bhqk", qb[:, :, hsl[gi]], kg,
                                preferred_element_type=jnp.float32) * scale + bias
            p, lse = _masked_softmax(logits, (pos >= 0)[None, None])
            outs.append(jnp.einsum("bhqk,bqkhd->bqhd", p.astype(vg.dtype), vg))
            lses.append(lse)
        w = jax.nn.softmax(jnp.stack(lses), axis=0)
        w = jnp.transpose(w, (0, 1, 3, 2))[..., None]
        o = w[0] * outs[0]
        for gi in range(1, len(C_GROUPS)):
            o = o + w[gi] * outs[gi]
        return o.reshape(bsz, Q_BLOCK, C_HEADS_PER_GROUP * HEAD_DIM).astype(q.dtype)

    return _sweep(block, seq, Q_BLOCK)

def second_inputs(seed: int = 0) -> dict:
    key = jax.random.key(seed)
    ks = jax.random.split(key, 14)

    def nrm(k, shape, scale):
        return jax.random.normal(k, shape, jnp.float32) * scale

    return {
        "x": nrm(ks[0], (BATCH, SEQ, D_MODEL), 1.0),
        "norm1_g": 1.0 + nrm(ks[1], (DEPTH_2, D_MODEL), 0.1),
        "norm2_g": 1.0 + nrm(ks[2], (DEPTH_2, D_MODEL), 0.1),
        "w_in": nrm(ks[3], (DEPTH_2, D_MODEL, IN_TOTAL), D_MODEL ** -0.5),
        "qk_norm_g": 1.0 + nrm(ks[4], (DEPTH_2, 6, HEAD_DIM), 0.1),
        "nsa_cmp_pos": nrm(ks[5], (DEPTH_2, 2, B_CMP_LEN, HEAD_DIM), 0.5),
        "nsa_cmp_w": nrm(ks[6], (DEPTH_2, 2, B_CMP_LEN, HEAD_DIM, HEAD_DIM), (B_CMP_LEN * HEAD_DIM) ** -0.5),
        "w_branch_a": nrm(ks[7], (DEPTH_2, A_HEADS * HEAD_DIM, D_MODEL), (A_HEADS * HEAD_DIM) ** -0.5),
        "w_branch_b": nrm(ks[8], (DEPTH_2, B_HEADS * HEAD_DIM, D_MODEL), (B_HEADS * HEAD_DIM) ** -0.5),
        "w_branch_c": nrm(ks[9], (DEPTH_2, C_HEADS_PER_GROUP * HEAD_DIM, D_MODEL), (C_HEADS_PER_GROUP * HEAD_DIM) ** -0.5),
        "w_out": nrm(ks[10], (DEPTH_2, D_MODEL, D_MODEL), D_MODEL ** -0.5),
        "w_ffn_in": nrm(ks[11], (DEPTH_2, D_MODEL, 2 * D_FF_2), D_MODEL ** -0.5),
        "w_ffn_out": nrm(ks[12], (DEPTH_2, D_FF_2, D_MODEL), D_FF_2 ** -0.5),
        "rel_bias": nrm(ks[13], (REL_BUCKETS, REL_HEADS), 0.5),
    }

def second_block(x, norm1_g, norm2_g, w_in, qk_norm_g, nsa_cmp_pos, nsa_cmp_w, w_branch_a, w_branch_b,
              w_branch_c, w_out, w_ffn_in, w_ffn_out, rel_bias):
    bsz, seq, _ = x.shape
    rel_a = rel_bias[:, :A_HEADS]
    rel_b = rel_bias[:, A_HEADS:A_HEADS + B_HEADS]
    rel_c = rel_bias[:, A_HEADS + B_HEADS:]
    for layer in range(DEPTH_2):
        h = _rms(x, norm1_g[layer])
        (a_q, a_k, a_v, i_q, i_k, i_w, b_q, b_kv, b_g, c_qkv, mix_g) = _split_last(h @ w_in[layer], IN_SIZES)
        qk = qk_norm_g[layer]
        a_q = _rms(a_q.reshape(bsz, seq, A_HEADS, HEAD_DIM), qk[0])
        a_k = _rms(a_k, qk[1])
        y_a = _dsa_attention(a_q, a_k, a_v, i_q.reshape(bsz, seq, A_IDX_HEADS, A_IDX_DIM), i_k, i_w,
                             rel_a) @ w_branch_a[layer]
        b_q = _rms(b_q.reshape(bsz, seq, B_HEADS, HEAD_DIM), qk[2])
        b_kv = b_kv.reshape(bsz, seq, 6, B_KV_HEADS, HEAD_DIM)
        b_gates = jax.nn.sigmoid(b_g).reshape(bsz, seq, B_HEADS, 3)
        y_b = _nsa_attention(b_q, b_kv[:, :, 0], b_kv[:, :, 1], _rms(b_kv[:, :, 2], qk[3]), b_kv[:, :, 3],
                             _rms(b_kv[:, :, 4], qk[3]), b_kv[:, :, 5], b_gates, nsa_cmp_pos[layer],
                             nsa_cmp_w[layer], qk[3], rel_b) @ w_branch_b[layer]
        c_qkv = c_qkv.reshape(bsz, seq, 3, C_HEADS, HEAD_DIM)
        y_c = _dilated_attention(_rms(c_qkv[:, :, 0], qk[4]), _rms(c_qkv[:, :, 1], qk[5]), c_qkv[:, :, 2],
                                 rel_c) @ w_branch_c[layer]
        g = jax.nn.sigmoid(mix_g).reshape(bsz, seq, 3, D_MODEL)
        x = x + (g[:, :, 0] * y_a + g[:, :, 1] * y_b + g[:, :, 2] * y_c) @ w_out[layer]
        h = _rms(x, norm2_g[layer])
        gate, up = jnp.split(h @ w_ffn_in[layer], 2, axis=-1)
        x = x + (jax.nn.silu(gate) * up) @ w_ffn_out[layer]
    return x


def setup_inputs(seed=0):
    out = dict(first_inputs(seed))
    for name, value in second_inputs(seed + 1).items():
        if name != "x":
            out[name + "_2"] = value
    return out


def reference(
    x, c, ctx, c_ctx, w_mod, b_mod, ln_g, ln_b, attn_w_qkv, attn_lambda, attn_subln_g, attn_w_o,
    pool_w, pool_scale, ffn_w_in, ffn_w_out, norm1_g_2, norm2_g_2, w_in_2, qk_norm_g_2,
    nsa_cmp_pos_2, nsa_cmp_w_2, w_branch_a_2, w_branch_b_2, w_branch_c_2, w_out_2, w_ffn_in_2,
    w_ffn_out_2, rel_bias_2,
):
    x = first_block(
        x, c, ctx, c_ctx, w_mod, b_mod, ln_g, ln_b, attn_w_qkv, attn_lambda, attn_subln_g,
        attn_w_o, pool_w, pool_scale, ffn_w_in, ffn_w_out,
    )
    return second_block(
        x, norm1_g_2, norm2_g_2, w_in_2, qk_norm_g_2, nsa_cmp_pos_2, nsa_cmp_w_2, w_branch_a_2,
        w_branch_b_2, w_branch_c_2, w_out_2, w_ffn_in_2, w_ffn_out_2, rel_bias_2,
    )


_drawn_inputs = setup_inputs


def setup_inputs(seed=0):
    import zlib

    import numpy as np

    out = dict(_drawn_inputs(seed))
    spreads = {}
    factors = {'b_mod': 4.26,
     'attn_lambda': 8.0,
     'attn_subln_g': 22.889,
     'pool_scale': 20.444,
     'qk_norm_g_2': 3.462}
    for name, (base, spread) in spreads.items():
        noise = np.random.default_rng([zlib.crc32(name.encode()), seed]).standard_normal(out[name].shape)
        drawn = base * np.exp(spread * noise) if base else spread * noise
        out[name] = jnp.asarray(drawn.astype(out[name].dtype))
    for name, factor in factors.items():
        out[name] = (out[name] * factor).astype(out[name].dtype)
    return out
```

```python
from contextlib import ExitStack

import numpy as np

import concourse.bass as bass
from concourse import mybir

F32 = mybir.dt.float32
ALU = mybir.AluOpType
ACT = mybir.ActivationFunctionType
AX = mybir.AxisListType.X

P = 128
SEQ = 256
TT = SEQ // P
D = 1024
KC = D // P
NB = 512
PK = 4
HEADS = 8
HD = 64
DEPTH = 2
ALPHA = (2.0 * DEPTH) ** 0.25
LN_EPS = 1e-5
RMS_EPS = 1e-6
LAM_INIT = 0.8 - 0.6
D_FF = -(-8 * D // (3 * 256)) * 256
FC = D_FF // P
FNB = D_FF // 256
POOL_WINDOWS = (2, 4, 8, 16)
GRID_W = 64
NEG = -1.0e30
TAKEN = -3.0e38
TOPK = min(256, SEQ // 4)

AQ, AK, AV, IQ, IK, IW = 0, 512, 576, 640, 896, 960
BQ, BKC, BVC, BKS, BVS, BKW, BVW, BG = 964, 1476, 1604, 1732, 1860, 1988, 2116, 2244
CQ, CK, CV, MIX = 2268, 3036, 3804, 4572
ZW = MIX
Z_BLOCKS = [(0, 512), (512, 964), (964, 1476), (1476, 1860), (1860, 2268),
            (2268, 2780), (2780, 3292), (3292, 3804), (3804, 4316), (4316, 4572)]
CMP_LEN, CMP_STRIDE = 32, 16
N_CMP = (SEQ - CMP_LEN) // CMP_STRIDE + 1
C_GROUPS = ((128, 1), (512, 4), (2048, 16))
BUCKETS, MAX_DIST = 32, 2048
REL_HEADS = 28
SROW = 384

COL_BMOD, COL_N1, COL_N2, COL_SUB, COL_QK = 0, 96, 104, 112, 113
N_COLS = 119

SS_AQ, SS_AK, SS_BQ, SS_KS, SS_KW, SS_CQ, SS_CK, SS_N = 0, 8, 9, 17, 19, 21, 33, 45

RING = 6
AHEAD = 3
MODS = 2


def shape_constants():
    t = np.arange(SEQ)
    inv = np.power(np.float32(10000.0), -np.arange(16, dtype=np.float32) / np.float32(16))
    row = np.repeat(np.arange(SEQ // GRID_W, dtype=np.float32), GRID_W)
    col = np.tile(np.arange(GRID_W, dtype=np.float32), SEQ // GRID_W)
    ang = np.concatenate([row[:, None] * inv, col[:, None] * inv], axis=-1).astype(np.float32)
    cos, sin = np.cos(ang), np.sin(ang)
    rope = np.stack([np.concatenate([cos, cos], 1), np.concatenate([-sin, sin], 1)], 1)
    rope = rope.reshape(TT, P, 2 * HD).transpose(1, 0, 2).reshape(P, -1)
    dist = P + np.arange(P)[:, None] - np.arange(SEQ)[None, :]
    causal = np.where(dist >= 0, 0.0, NEG)
    cend = np.arange(N_CMP) * CMP_STRIDE + CMP_LEN - 1
    cmp_mask = np.where(cend[None, :] <= t[:, None], 0.0, NEG).reshape(TT, P, N_CMP)
    cmp_mask = cmp_mask.transpose(1, 0, 2).reshape(P, -1)
    table = np.concatenate([np.eye(P), rope, causal, cmp_mask], axis=1).astype(np.float32)

    d = SEQ - 1 - np.arange(SROW)
    n = np.maximum(d, 0)
    exact = BUCKETS // 2
    nf = np.maximum(n, 1).astype(np.float32)
    large = exact + (np.log(nf / np.float32(exact)) / np.float32(np.log(MAX_DIST / exact))
                     * np.float32(BUCKETS - exact)).astype(np.int32)
    bucket = np.where(n < exact, n, np.minimum(large, BUCKETS - 1))
    onehot = ((bucket[None, :] == np.arange(BUCKETS)[:, None]) & (d >= 0)).astype(np.float32)
    rowmask = np.zeros((REL_HEADS, SROW), np.float32)
    rowmask[:, d < 0] = NEG
    for g, (win, dil) in enumerate(C_GROUPS):
        rowmask[16 + 4 * g:20 + 4 * g, (d % dil != 0) | (d > win)] = NEG

    pool = np.zeros((len(POOL_WINDOWS), SEQ, SEQ), np.float32)
    for g, w in enumerate(POOL_WINDOWS):
        lo, hi = np.clip(t - w // 2, 0, SEQ), np.clip(t + w - w // 2, 0, SEQ)
        inside = (t[:, None] >= lo[None, :]) & (t[:, None] < hi[None, :])
        pool[g] = inside / (hi - lo)[None, :].astype(np.float32) - np.eye(SEQ)
    pool = pool.reshape(len(POOL_WINDOWS), TT, P, SEQ).transpose(2, 1, 0, 3)
    return {"const_table": table, "const_onehot": onehot, "const_rowmask": rowmask,
            "const_pool": np.ascontiguousarray(pool.reshape(P, -1)).astype(np.float32)}


def w_panels(a):
    out = []

    def add(key, w, kg, chunks, lo, hi):
        src = w[kg * PK * P:(kg * PK + chunks) * P, lo:hi].rearrange("(c p) n -> p c n", p=P)
        out.append((key, [(src, 0, hi - lo)], chunks, hi - lo))

    def ffn(name, w_in, w_out):
        for nb in range(FNB):
            for kg in range(2):
                rows = w_in[kg * PK * P:(kg + 1) * PK * P, :]
                parts = [(rows[:, h * D_FF + nb * 256:h * D_FF + nb * 256 + 256]
                          .rearrange("(c p) n -> p c n", p=P), h * 256, 256) for h in range(2)]
                out.append(((name + "_in", nb, kg), parts, PK, 512))
        for nb in range(2):
            for kg in range(-(-FC // PK)):
                add((name + "_out", nb, kg), w_out, kg, min(PK, FC - kg * PK), nb * NB, nb * NB + NB)

    for nb in range(6):
        for kg in range(2):
            add(("qkv", nb, kg), a["attn_w_qkv"][0], kg, PK, nb * NB, nb * NB + NB)
    for nb in range(2):
        for kg in range(2):
            add(("wo", nb, kg), a["attn_w_o"][0], kg, PK, nb * NB, nb * NB + NB)
    ffn("ffn0", a["ffn_w_in"][0], a["ffn_w_out"][0])
    out.append((("pool", 0, 0), [(a["pool_w"][0].rearrange("g (c p) n -> p (g c) n", p=P), 0, 256)], 8, 256))
    ffn("ffn1", a["ffn_w_in"][1], a["ffn_w_out"][1])
    w_in = a["w_in_2"][0]
    for nb, (lo, hi) in enumerate(Z_BLOCKS):
        for kg in range(2):
            add(("z", nb, kg), w_in, kg, PK, lo, hi)
    out.append((("cmp", 0, 0), [(a["nsa_cmp_w_2"][0].rearrange("v (l j) d e -> (j d) (v l) e", j=2), 0, HD)],
                32, HD))
    for nb in range(2):
        for br in range(3):
            for kg in range(2):
                lo = MIX + br * D + nb * NB
                add(("mix", nb * 3 + br, kg), w_in, kg, PK, lo, lo + NB)
    for nb in range(2):
        for br, w in enumerate(("w_branch_a_2", "w_branch_b_2", "w_branch_c_2")):
            add((f"branch{br}", nb, 0), a[w][0], 0, 2 if br == 2 else 4, nb * NB, nb * NB + NB)
    for nb in range(2):
        for kg in range(2):
            add(("w_out", nb, kg), a["w_out_2"][0], kg, PK, nb * NB, nb * NB + NB)
    ffn("ffn2", a["w_ffn_in_2"][0], a["w_ffn_out_2"][0])
    return out


def build(nc, a, out, scratch):
    panels = w_panels(a)
    panel_at = {key: i for i, (key, *_) in enumerate(panels)}

    with ExitStack() as ctx:
        def sb(name, cols, parts=P):
            return ctx.enter_context(nc.sbuf_tensor(name, [parts, cols], F32))

        def sem(name):
            return ctx.enter_context(nc.semaphore(name))

        def v3(ap, a_):
            return ap.rearrange("p (a b) -> p a b", a=a_)

        ring = [sb(f"ring{i}", PK * NB) for i in range(RING)]
        big = sb("big", 16384)
        aux = sb("aux", 12288)
        x_tok = sb("x_tok", TT * D)[:].rearrange("p (t n) -> p t n", t=TT)
        y_tok = sb("y_tok", TT * D)[:].rearrange("p (t n) -> p t n", t=TT)
        hT_raw = sb("hT", KC * 512)
        hT = v3(hT_raw[:], KC)
        table = sb("table", P + TT * 2 * HD + SEQ + TT * N_CMP)
        ident = table[:, 0:P]
        rope = v3(table[:, P:P + TT * 2 * HD], TT * 2)
        causal = table[:, P + 4 * HD:P + 4 * HD + SEQ]
        cmp_mask = v3(table[:, P + 4 * HD + SEQ:], TT)
        ones = sb("ones", P)
        neghalf = sb("neghalf", 96)
        cols = sb("cols", N_COLS)
        modcol = v3(sb("modcol", 64)[:], 8)
        cs_in = v3(sb("cs_in", 16)[:], 2)
        cs = sb("cs", 16)
        modacc_raw = sb("modacc", MODS * NB)
        modacc = v3(modacc_raw[:], MODS)
        tmp = v3(sb("tmp", 2 * NB)[:], 2)
        small = sb("small", 368)
        gates = small[:, 320:368].rearrange("p (t h g) -> p t h g", t=TT, h=8)
        srow = sb("srow", SROW, REL_HEADS)
        posT = sb("posT", 32)
        lam = sb("lam", 8)

        q_tok = v3(big[:, 0:2048], TT)
        k_tok = v3(big[:, 2048:6144], 4)
        v_tok = v3(big[:, 6144:10240], 4)
        qT = v3(big[:, 10240:12288], HEADS)
        kT = v3(big[:, 12288:16384], HEADS)
        oT = qT
        ffT = v3(big[:, 0:FC * SEQ], FC)
        mod_rows = v3(big[:, 5632:7680], 2)
        pool_m = v3(big[:, 7680:9728], TT * 4)
        pscale = big[:, 9728:10752]
        hx_tok = v3(big[:, 10752:12800], TT)
        pooledT = v3(big[:, 12800:14848], KC)
        modring = [v3(aux[:, 4096 * i:4096 * i + 4096], KC) for i in range(MODS)]
        g1row, g2row = aux[:, 8192:9216], aux[:, 9216:10240]
        ln_rows = v3(aux[:, 10240:12288], 2)
        prob = hT_raw[:, 0:4096].rearrange("p (b m n) -> p b m n", b=AHEAD + 1, m=2)
        aT = v3(big[:, 0:1024], 2)
        z = v3(big[:, 0:TT * ZW], TT)
        ft = v3(big[:, TT * ZW:TT * ZW + 28 * SEQ], 28)
        oT2 = ft[:, 0:10, :]
        bias = v3(aux[:, 0:REL_HEADS * SEQ], REL_HEADS)
        kdup = aux[:, 7168:9728].rearrange("p (t b n) -> p t b n", t=TT, b=10)
        lbuf = v3(aux[:, 9216:12288], AHEAD + 1)
        score = [tmp[:, 0, 0:128], tmp[:, 0, 128:384]]
        work = [tmp[:, 1, 0:128], tmp[:, 1, 128:384]]
        selmask = [aux[:, 7168:7296], aux[:, 7296:7552]]
        pT = v3(aux[:, 7680:9216], 2)
        rel = hT[:, 0:4, 256:512]
        o_c = hT[:, 4:6, 256:512]
        xc = modacc_raw[:, 0:4 * 16 * N_CMP].rearrange("p (k l n) -> p k l n", k=4, l=16)
        cmp_k = srow[0:N_CMP, :]
        ckd = v3(cmp_k[:, 0:2 * P], 2)
        vcmp = v3(cmp_k[:, 2 * P:], 2)
        kcT = v3(sb("kcT", 2 * N_CMP)[:], 2)
        pcT = v3(table[0:N_CMP, P:P + 2 * P], 2)
        colsrc, possrc, oh_sb, rm_sb, rel_sb = (
            big[0:N_COLS, 0:P], big[0:32, 128:256], big[0:32, 256:640], big[0:REL_HEADS, 640:1024],
            big[0:32, 1024:1024 + REL_HEADS])
        lam_in = v3(big[:, 1100:1356], 4)

        psum = [ctx.enter_context(nc.psum_tensor(f"bank{i}", [P, NB], F32)) for i in range(8)]

        filled = [sem(f"bank_filled{i}") for i in range(8)]
        emptied = [sem(f"bank_emptied{i}") for i in range(8)]
        w_landed = [sem(f"w_landed{i}") for i in range(RING)]
        w_used = sem("w_used")
        mod_landed = [sem(f"mod_landed{i}") for i in range(MODS)]
        mod_acc = sem("mod_acc")
        x_landed, ctx_landed, c_landed = sem("x_landed"), sem("ctx_landed"), sem("c_landed")
        table_landed, cols_landed, lam_landed = sem("table_landed"), sem("cols_landed"), sem("lam_landed")
        ln_landed, g_landed = sem("ln_landed"), {2: sem("g1_bias_landed"), 5: sem("g2_bias_landed")}
        lam_sum, lam_exp, gates_done, sig_done = sem("lam_sum"), sem("lam_exp"), sem("gates_done"), sem("sig_done")
        rows_landed, poolm_landed, psc_landed = sem("rows_landed"), sem("pool_m_landed"), sem("pscale_landed")
        srow_done, srow_stored, bias_landed = sem("srow_done"), sem("srow_stored"), sem("bias_landed")
        consts_done, csil_done = sem("consts_done"), sem("csil_done")
        dve_step, act_step = sem("dve_step"), sem("act_step")
        rope_done, x_done, g1_used, g2_used, ln_used = (
            sem("rope_done"), sem("x_done"), sem("g1_used"), sem("g2_used"), sem("ln_rows_used"))
        var_done, rstd_done = sem("var_done"), sem("rstd_done")
        nmax_done, exp_done, probs_done, o_done = (
            sem("nmax_done"), sem("exp_done"), sem("probs_done"), sem("o_done"))
        sq_done, hx_done, mix_done = sem("sq_done"), sem("hx_done"), sem("mix_done")
        xn_done, zsrc_done, xc_done, ckd_done = sem("xn_done"), sem("zsrc_done"), sem("xc_done"), sem("ckd_done")
        rel_done, rel_used, l_done, exp2_done, p_done = (
            sem("rel_done"), sem("rel_used"), sem("logits_done"), sem("exp2_done"), sem("p_done"))
        attn_done, out_stored = sem("attn_done"), sem("out_stored")

        block = ctx.enter_context(nc.Block())

        uses, where = [0] * 8, {}
        turn = {"gemm": 0, "misc": 0, "unit": 0, "mix": 0}
        POOLS = {"gemm": (0, 1, 2, 3, 4, 5), "misc": (6, 7), "unit": (0, 1, 2, 3, 4), "mix": (5,)}

        def result(eng, key):
            b, n = where[key]
            eng.wait_ge(filled[b], n)
            return psum[b]

        def empties(ins, key):
            ins.then_inc(emptied[where[key][0]], 1)

        def wait_emptied(eng, key):
            b, n = where[key]
            eng.wait_ge(emptied[b], n)

        def landings(i):
            return sum(len(panels[j][1]) for j in range(i % RING, i + 1, RING))

        def mod_is_row(e):
            comp = (e % 12) // 2
            return comp in ((2, 5) if e < 12 else (0, 1, 2, 5))

        QKV_EVENTS = {0: [4], 1: [5], 2: [6, 7], 3: [8, 9], 4: [10, 11], 5: []}
        FFN_EVENTS = {"ffn0": {nb: [12 + nb] for nb in range(10)}, "ffn1": {0: [22], 1: [23]}, "ffn2": {}}
        FIRST_DVE_EVENT, N_EVENTS = 4, 24
        UNITS0 = [(qt, h) for qt in range(TT) for h in range(HEADS)]
        UNITS2 = [("B", qt, h) for qt in range(TT) for h in range(8)] + \
                 [("C", qt, h) for qt in range(TT) for h in range(4)] + \
                 [("A", qt, h) for qt in range(TT) for h in range(8)]
        MIX_PIECES = 2 * 3 * TT * 2
        MIX_AT = {u: range(u * MIX_PIECES // len(UNITS2), (u + 1) * MIX_PIECES // len(UNITS2))
                  for u in range(len(UNITS2))}
        MIX_Z = [[(0, 0, 512)], [(964, 0, 512)], [(2268, 0, 512)], [(2780, 0, 512)], [(3292, 0, 512)],
                 [(1476, 0, 384), (640, 384, 128)]]
        FT_PAIRS = [(0, 2), (2, 2), (4, 1), (5, 2), (7, 1), (8, 2), (10, 2), (12, 2), (14, 2),
                    (16, 2), (18, 2), (20, 2), (22, 2), (24, 2), (26, 2)]
        FT_GAIN = {0: 0, 2: 0, 4: 1, 8: 2, 10: 2, 12: 3, 14: 3, 16: 4, 18: 4, 20: 4, 22: 5, 24: 5, 26: 5}
        FT_ON_ACT = {0, 4, 7, 10, 14, 18, 22, 26}

        def ft_source(b, tt):
            if b < 4:
                return z[:, tt, AQ + b * P:AQ + (b + 1) * P]
            if b in (5, 6):
                return z[:, tt, IQ + (b - 5) * P:IQ + (b - 4) * P]
            if 8 <= b < 12:
                return z[:, tt, BQ + (b - 8) * P:BQ + (b - 7) * P]
            if 16 <= b < 22:
                return z[:, tt, CQ + (b - 16) * P:CQ + (b - 15) * P]
            if b >= 22:
                return z[:, tt, CK + (b - 22) * P:CK + (b - 21) * P]
            return kdup[:, tt, {4: 0, 7: 1, 12: 2, 13: 3, 14: 4, 15: 5}[b], :]

        def unit_segments(kind, h):
            if kind == "A":
                return [(h // 2, 4, h, AV)]
            if kind == "B":
                g = h // 4
                return [(8 + h // 2, 12 + g, 8 + h, BVS + g * HD), (8 + h // 2, 14 + g, 8 + h, BVW + g * HD)]
            return [(16 + (4 * g + h) // 2, 22 + (4 * g + h) // 2, 16 + 4 * g + h, CV + (4 * g + h) * HD)
                    for g in range(3)]

        def o2_tok(kind, qt):
            return {"A": y_tok[:, qt, 0:512], "B": y_tok[:, qt, 512:1024], "C": o_c[:, qt, :]}[kind]

        @block.tensor
        def _(pe):
            unreleased = [False]
            next_panel = [0]

            def take(key, pool="gemm"):
                b = POOLS[pool][turn[pool] % len(POOLS[pool])]
                turn[pool] += 1
                if uses[b]:
                    pe.wait_ge(emptied[b], uses[b])
                uses[b] += 1
                where[key] = (b, uses[b])
                return psum[b]

            def fills(ins, key):
                ins.then_inc(filled[where[key][0]], 1)

            def panel(key):
                i = panel_at[key]
                assert i == next_panel[0], key
                next_panel[0] += 1
                pe.wait_ge(w_landed[i % RING], 16 * landings(i))
                _, _, chunks, width = panels[i]
                return ring[i % RING][:, 0:chunks * width].rearrange("p (c n) -> p c n", c=chunks)

            def mm(o, l, r, start, stop, **kw):
                ins = nc.tensor.matmul(o, l, r, start=start, stop=stop, **kw)
                if unreleased[0] and not stop:
                    ins.then_inc(w_used, 1)
                    unreleased[0] = False
                return ins

            def release():
                assert not unreleased[0]
                unreleased[0] = True

            def gemm(stage, lhs, tts, nb, width, groups):
                banks = {tt: take((stage, nb, tt)) for tt in tts}
                last = groups[-1][1] - 1
                for kg, (lo, hi) in enumerate(groups):
                    w = panel((stage, nb, kg))
                    for tt in tts:
                        for c in range(lo, hi):
                            ins = mm(banks[tt][:, 0:width], lhs(tt, c), w[:, c - lo, :], c == 0, c == last)
                        if hi - 1 == last:
                            fills(ins, (stage, nb, tt))
                    release()

            HALVES = [(0, 4), (4, 8)]

            def transposes(key, sources, pool="gemm"):
                bank = take(key, pool)
                for i, src in enumerate(sources):
                    ins = nc.tensor.transpose(bank[0:src.shape[1], i * P:i * P + src.shape[0]], src,
                                              ident[0:src.shape[0], 0:src.shape[0]])
                    if unreleased[0] and i == 0 and len(sources) > 1:
                        ins.then_inc(w_used, 1)
                        unreleased[0] = False
                fills(ins, key)

            def mod_reduce(e):
                pe.wait_ge(mod_acc, e - FIRST_DVE_EVENT + 1)
                acc = modacc[:, e % MODS, :]
                bank = take(("mod", e), "misc")
                if mod_is_row(e):
                    ins = mm(bank[:, :], ones[:, :], acc, True, True)
                else:
                    for j in range(4):
                        ins = mm(bank[:, j:j + 1], acc[:, j * P:(j + 1) * P], ones[:, 0:1], True, True)
                fills(ins, ("mod", e))

            def x_transposes(stage, tok, ready, version):
                for ch in range(KC):
                    if ch == 0:
                        pe.wait_ge(ready, version)
                    transposes((stage, ch), [tok[:, tt, ch * P:(ch + 1) * P] for tt in range(TT)])

            def ffn(name):
                wait_emptied(pe, (name + "_h", KC - 2))
                wait_emptied(pe, (name + "_h", KC - 1))
                for nb in range(FNB):
                    banks = [take((name, "g", nb)), take((name, "u", nb))]
                    for kg in range(2):
                        w = panel((name + "_in", nb, kg))
                        for half in range(2):
                            for s in range(2):
                                for c in range(PK):
                                    lo = half * 256 + s * P
                                    ins = mm(banks[half][:, s * 256:s * 256 + 256], w[:, c, lo:lo + P],
                                             hT[:, kg * PK + c, 0:SEQ], kg == 0 and c == 0 and s == 0,
                                             kg == 1 and c == PK - 1, skip_group_check=True)
                            if kg == 1:
                                fills(ins, (name, "gu"[half], nb))
                        release()
                    for e in FFN_EVENTS[name].get(nb, []):
                        mod_reduce(e)
                wait_emptied(pe, (name, "u", FNB - 1))
                groups = [(k, min(k + PK, FC)) for k in range(0, FC, PK)]
                for nb in range(2):
                    gemm(name + "_out", lambda tt, c: ffT[:, c, tt * P:(tt + 1) * P], range(TT), nb, NB, groups)

            pe.wait_ge(table_landed, 16)
            pe.wait_ge(cols_landed, 16 * 10)
            transposes("cols", [colsrc])
            transposes("pos", [possrc])
            fills(mm(take("srow")[0:REL_HEADS, 0:SROW], rel_sb, oh_sb, True, True), "srow")

            pe.wait_ge(csil_done, 1)
            for e in range(FIRST_DVE_EVENT):
                pe.wait_ge(mod_landed[e % MODS], 16 * (e // MODS + 1))
                bank = take(("mod", e), "misc")
                for s in range(4):
                    for j in range(KC):
                        ins = mm(bank[:, 2 * s:2 * s + 2], modring[e % MODS][:, j, s * P:(s + 1) * P],
                                 cs[:, 2 * j:2 * j + 2], j == 0, j == KC - 1)
                fills(ins, ("mod", e))

            pe.wait_ge(x_landed, 16)
            pe.wait_ge(ctx_landed, 16)
            for ch in range(KC):
                transposes(("lat", ch), [x_tok[:, tt, ch * P:(ch + 1) * P] for tt in range(TT)])
                transposes(("con", ch), [y_tok[:, tt, ch * P:(ch + 1) * P] for tt in range(TT)])

            for ch in (KC - 1,):
                wait_emptied(pe, ("lat", ch))
                wait_emptied(pe, ("con", ch))
            for nb in range(6):
                gemm("qkv", lambda tt, c: hT[:, c, tt * P:(tt + 1) * P], range(2 if nb < 2 else 4), nb, NB, HALVES)
                for e in QKV_EVENTS[nb]:
                    mod_reduce(e)

            for h in range(HEADS):
                pe.wait_ge(rope_done, 6 if h < 4 else 8)
                for tt in (2, 3):
                    wait_emptied(pe, ("qkv", 2 + h // 4, tt))
                transposes(("qT", h), [q_tok[:, tt, h * P:(h + 1) * P] for tt in range(TT)])
                transposes(("kT", h), [k_tok[:, tt, h * P:(h + 1) * P] for tt in range(4)])
            for tt in range(4):
                wait_emptied(pe, ("qkv", 5, tt))

            def scores(u):
                qt, h = UNITS0[u]
                wait_emptied(pe, ("qT", h))
                wait_emptied(pe, ("kT", h))
                for m in range(2):
                    rows = slice(m * HD, (m + 1) * HD)
                    fills(mm(take(("S", u, m))[:, :], qT[rows, h, qt * P:(qt + 1) * P], kT[rows, h, :],
                             True, True), ("S", u, m))

            def turn_probs(u):
                pe.wait_ge(probs_done, u + 1)
                transposes(("PT", u), [prob[:, u % 4, 0, kb * P:(kb + 1) * P] for kb in range(4)])

            def values(u):
                qt, h = UNITS0[u]
                if u % 4 == 0:
                    take(("O", u // 4), "misc")
                o = psum[where[("O", u // 4)][0]]
                wait_emptied(pe, ("PT", u))
                for kb in range(4):
                    ins = mm(o[:, (u % 4) * P:(u % 4 + 1) * P], aT[:, u % 2, kb * P:(kb + 1) * P],
                             v_tok[:, kb, h * P:(h + 1) * P], kb == 0, kb == 3)
                if u % 4 == 3:
                    fills(ins, ("O", u // 4))

            for u in range(AHEAD):
                scores(u)
            for u in range(len(UNITS0)):
                turn_probs(u)
                if u + AHEAD < len(UNITS0):
                    scores(u + AHEAD)
                values(u)

            pe.wait_ge(o_done, 4)
            for h in range(HEADS):
                transposes(("oT", h), [y_tok[:, tt, h * P:(h + 1) * P] for tt in range(TT)])
            wait_emptied(pe, ("oT", HEADS - 1))
            for nb in range(2):
                gemm("wo", lambda tt, c: oT[:, c, tt * P:(tt + 1) * P], range(TT), nb, NB, HALVES)
            x_transposes("ffn0_h", x_tok, x_done, 2)
            ffn("ffn0")

            pe.wait_ge(hx_done, 2)
            pe.wait_ge(poolm_landed, 16)
            for ch in range(KC):
                bank = take(("pl", ch))
                for kt in range(TT):
                    ins = mm(bank[:, 0:SEQ], hx_tok[:, kt, ch * P:(ch + 1) * P],
                             pool_m[:, kt * 4 + ch // 2, :], kt == 0, kt == TT - 1)
                fills(ins, ("pl", ch))
            wait_emptied(pe, ("pl", KC - 1))
            w = panel(("pool", 0, 0))
            for nb in range(2):
                for tt in range(TT):
                    bank = take(("poolw", nb, tt))
                    for g in (2 * nb, 2 * nb + 1):
                        for c in range(2):
                            ins = mm(bank[:, (g % 2) * 256:(g % 2) * 256 + 256],
                                     pooledT[:, 2 * g + c, tt * P:(tt + 1) * P], w[:, 2 * g + c, :],
                                     c == 0, c == 1)
                    fills(ins, ("poolw", nb, tt))
            release()
            x_transposes("ffn1_h", x_tok, x_done, 6)
            ffn("ffn1")

            x_transposes("z_h", y_tok, xn_done, 2)
            wait_emptied(pe, ("z_h", KC - 2))
            wait_emptied(pe, ("z_h", KC - 1))
            for nb, (lo, hi) in enumerate(Z_BLOCKS):
                gemm("z", lambda tt, c: hT[:, c, tt * P:(tt + 1) * P], range(TT), nb, hi - lo, HALVES)

            pe.wait_ge(zsrc_done, 1)
            for tt in range(TT):
                wait_emptied(pe, ("z", len(Z_BLOCKS) - 1, tt))
            for i in range(4):
                transposes(("dupT", i), [kdup[:, tt, 6 + i, :] for tt in range(TT)])
            for b0, n in FT_PAIRS:
                transposes(("ft", b0), [ft_source(b0 + j, tt) for j in range(n) for tt in range(TT)])

            w = panel(("cmp", 0, 0))
            pe.wait_ge(xc_done, 1)
            bank = take("cmp")
            for i in range(4):
                kv = i // 2
                for l in range(16):
                    ins = mm(bank[0:N_CMP, i * HD:(i + 1) * HD], xc[:, i, l, :], w[:, kv * 16 + l, :], l == 0, l == 15)
            fills(ins, "cmp")
            release()
            pe.wait_ge(ckd_done, 1)
            transposes("kcT", [ckd[:, 0, :], ckd[:, 1, :]])
            for b0, _ in FT_PAIRS[-2:]:
                wait_emptied(pe, ("ft", b0))

            for qt in range(TT):
                nk = (qt + 1) * P
                for j in range(2):
                    rows = slice(j * HD, (j + 1) * HD)
                    bank = take(("I", qt, j))
                    for pr in range(2):
                        ins = mm(bank[:, pr * 256:pr * 256 + nk], ft[rows, 5 + pr, qt * P:(qt + 1) * P],
                                 ft[rows, 7, 0:nk], True, True)
                    fills(ins, ("I", qt, j))

            def scores2(u):
                kind, qt, h = UNITS2[u]
                nk = (qt + 1) * P
                rows = slice((h % 2) * HD, (h % 2 + 1) * HD)
                segs = unit_segments(kind, h)
                for s, (qb, kb, _, _) in enumerate(segs):
                    if s % 2 == 0:
                        bank = take(("S2", u, s // 2), "unit")
                    ins = mm(bank[:, (s % 2) * 256:(s % 2) * 256 + nk], ft[rows, qb, qt * P:(qt + 1) * P],
                             ft[rows, kb, 0:nk], True, True)
                    if s % 2 == 1 or s == len(segs) - 1:
                        fills(ins, ("S2", u, s // 2))
                if kind == "B":
                    fills(mm(take(("S2", u, "c"), "unit")[:, 0:N_CMP], ft[rows, segs[0][0], qt * P:(qt + 1) * P],
                             kcT[rows, h // 4, :], True, True), ("S2", u, "c"))

            def turn_probs2(u):
                kind, qt, h = UNITS2[u]
                nblk = (qt + 1) * len(unit_segments(kind, h))
                pe.wait_ge(p_done, u + 1)
                p = lbuf[:, u % 4, :]
                for i in range(0, nblk, 4):
                    transposes(("PT2", u, i // 4), [p[:, b * P:(b + 1) * P] for b in range(i, min(i + 4, nblk))],
                               "unit")
                if kind == "B":
                    transposes(("PT2", u, "c"), [p[:, nblk * P:nblk * P + N_CMP]], "unit")

            def values2(u):
                kind, qt, h = UNITS2[u]
                segs = unit_segments(kind, h)
                nkb = qt + 1
                nblk = nkb * len(segs)
                group = (kind, qt)
                if h == 0:
                    take(("O2",) + group, "misc")
                o = psum[where[("O2",) + group][0]][:, h * HD:(h + 1) * HD]
                for i in range(0, nblk, 4):
                    wait_emptied(pe, ("PT2", u, i // 4))
                last = nblk - 1 if kind != "B" else nblk
                for b in range(nblk):
                    v = z[:, b % nkb, segs[b // nkb][3]:segs[b // nkb][3] + HD]
                    ins = mm(o, pT[:, u % 2, b * P:(b + 1) * P], v, b == 0, b == last)
                if kind == "B":
                    wait_emptied(pe, ("PT2", u, "c"))
                    ins = mm(o, pcT[:, u % 2, :], vcmp[:, h // 4, :], False, True)
                if h == (3 if kind == "C" else 7):
                    fills(ins, ("O2",) + group)

            mix_w = {}

            def mix_piece(i):
                b, tt, kg = i // 4, i % 4 // 2, i % 2
                if tt == 0:
                    mix_w[kg] = panel(("mix", b, kg))
                if kg == 0:
                    take(("mix", b, tt), "mix")
                bank = psum[where[("mix", b, tt)][0]]
                for c in range(PK):
                    ins = mm(bank[:, :], hT[:, kg * PK + c, tt * P:(tt + 1) * P], mix_w[kg][:, c, :],
                             kg == 0 and c == 0, kg == 1 and c == PK - 1)
                if kg == 1:
                    fills(ins, ("mix", b, tt))
                if tt == TT - 1:
                    release()

            for u in range(AHEAD):
                scores2(u)
            for u in range(len(UNITS2)):
                turn_probs2(u)
                if u + AHEAD < len(UNITS2):
                    scores2(u + AHEAD)
                for i in MIX_AT[u]:
                    mix_piece(i)
                values2(u)

            for kind, n in (("A", 4), ("B", 4), ("C", 2)):
                for qt in range(TT):
                    wait_emptied(pe, ("O2", kind, qt))
                for i in range(n):
                    transposes(("oT2", kind, i), [o2_tok(kind, qt)[:, i * P:(i + 1) * P] for qt in range(TT)])
            wait_emptied(pe, ("oT2", "C", 1))
            for nb in range(2):
                for br in range(3):
                    n = 2 if br == 2 else 4
                    gemm(f"branch{br}", lambda tt, c: oT2[:, 4 * br + c, tt * P:(tt + 1) * P], range(TT), nb, NB,
                         [(0, n)])
            x_transposes("mixed", y_tok, mix_done, 1)
            wait_emptied(pe, ("mixed", KC - 1))
            for nb in range(2):
                gemm("w_out", lambda tt, c: hT[:, c, tt * P:(tt + 1) * P], range(TT), nb, NB, HALVES)
            x_transposes("ffn2_h", y_tok, xn_done, 4)
            ffn("ffn2")
            assert next_panel[0] == len(panels)

        @block.scalar
        def _(act):
            steps = [0]

            def step(ins):
                ins.then_inc(act_step, 1)
                steps[0] += 1

            def settle():
                act.wait_ge(act_step, steps[0])

            act.dma_start(cs_in[:, 0, :], a["c"].rearrange("a (p j) -> p (a j)", p=P)).then_inc(c_landed, 16)
            act.dma_start(cs_in[:, 1, :], a["c_ctx"].rearrange("(p j) -> p j", p=P)).then_inc(c_landed, 16)
            act.wait_ge(c_landed, 32)
            nc.scalar.activation(cs[:, :].rearrange("p (j c) -> p c j", c=2), cs_in, ACT.Silu).then_inc(csil_done, 1)
            act.wait_ge(lam_sum, 1)
            nc.scalar.activation(lam[:, 2:4], lam[:, 0:2], ACT.Exp).then_inc(lam_exp, 1)

            for ch in range(KC):
                bank = result(act, ("lat", ch))
                if ch == 0:
                    for e in range(4):
                        wait_emptied(act, ("mod", e))
                empties(nc.scalar.activation(hT[:, ch, 0:SEQ], bank[:, 0:SEQ], ACT.Identity,
                                             bias=modcol[:, 0, ch:ch + 1], scale=modcol[:, 1, ch:ch + 1]),
                        ("lat", ch))

            for nb in range(6):
                for tt in range(2 if nb < 2 else 4):
                    dst = (q_tok, k_tok, v_tok)[nb // 2][:, tt, (nb % 2) * NB:(nb % 2) * NB + NB]
                    empties(nc.scalar.activation(dst, result(act, ("qkv", nb, tt))[:, :], ACT.Copy),
                            ("qkv", nb, tt))
            for h in range(HEADS):
                empties(nc.scalar.activation(kT[:, h, :], result(act, ("kT", h))[:, :], ACT.Copy), ("kT", h))

            act.wait_ge(srow_done, 1)
            act.dma_start(scratch, srow[:, :].unsqueeze(1).broadcast_to([REL_HEADS, P, SROW])).then_inc(srow_stored, 16)
            def exps(u):
                act.wait_ge(nmax_done, u + 1)
                if u > AHEAD:
                    b, n = where[("PT", u - AHEAD - 1)]
                    act.wait_ge(filled[b], n)
                for m in range(2):
                    ins = nc.scalar.activation(prob[:, u % 4, m, :], result(act, ("S", u, m))[:, :], ACT.Exp,
                                               bias=small[:, 8 * (u % 4) + m:8 * (u % 4) + m + 1], scale=HD ** -0.5,
                                               accum_out=small[:, 8 * (u % 4) + 2 + m:8 * (u % 4) + 3 + m])
                    empties(ins, ("S", u, m))

            for u in range(AHEAD):
                exps(u)
            for u in range(len(UNITS0)):
                bank = result(act, ("PT", u))
                empties(nc.scalar.activation(aT[:, u % 2, :], bank[:, :], ACT.Copy), ("PT", u))
                if u + AHEAD < len(UNITS0):
                    exps(u + AHEAD)
                if u % 4 == 3:
                    b = result(act, ("O", u // 4))
                    if u // 4:
                        act.wait_ge(o_done, u // 4)
                    nc.scalar.activation(tmp[:, 0, :], b[:, :], ACT.Square).then_inc(sq_done, 1)
            for h in range(HEADS):
                empties(nc.scalar.activation(oT[:, h, :], result(act, ("oT", h))[:, 0:SEQ], ACT.Copy,
                                             scale=cols[:, COL_SUB:COL_SUB + 1]), ("oT", h))

            def modulated(stage, shift, scale):
                for ch in range(0, KC, 2):
                    empties(nc.scalar.activation(hT[:, ch, 0:SEQ], result(act, (stage, ch))[:, 0:SEQ], ACT.Identity,
                                                 bias=modcol[:, shift, ch:ch + 1], scale=modcol[:, scale, ch:ch + 1]),
                            (stage, ch))

            def gained(stage, col):
                for ch in range(0, KC, 2):
                    empties(nc.scalar.activation(hT[:, ch, 0:SEQ], result(act, (stage, ch))[:, 0:SEQ], ACT.Copy,
                                                 scale=cols[:, col + ch:col + ch + 1]), (stage, ch))

            def ffn(name):
                for nb in range(FNB):
                    bank = result(act, (name, "g", nb))
                    if nb >= 2:
                        wait_emptied(act, (name, "u", nb - 2))
                    empties(nc.scalar.activation(tmp[:, nb % 2, :], bank[:, :], ACT.Silu), (name, "g", nb))

            modulated("ffn0_h", 4, 5)
            ffn("ffn0")
            for ch in range(KC):
                empties(nc.scalar.activation(pooledT[:, ch, :], result(act, ("pl", ch))[:, 0:SEQ], ACT.Copy),
                        ("pl", ch))
            modulated("ffn1_h", 6, 7)
            ffn("ffn1")

            gained("z_h", COL_N1)
            for nb, (lo, hi) in enumerate(Z_BLOCKS):
                for tt in range(TT):
                    empties(nc.scalar.activation(z[:, tt, lo:hi], result(act, ("z", nb, tt))[:, 0:hi - lo], ACT.Copy),
                            ("z", nb, tt))
                if nb == 4:
                    for tt in range(TT):
                        wait_emptied(act, ("z", 4, tt))
                        g = v3(z[:, tt, BG:BG + 24], 8)
                        nc.scalar.activation(gates[:, tt, :, 0:2], g[:, :, 1:3], ACT.Sigmoid).then_inc(gates_done, 1)
                        nc.scalar.activation(gates[:, tt, :, 2:3], g[:, :, 0:1], ACT.Sigmoid).then_inc(gates_done, 1)
            for b0, n in FT_PAIRS:
                if b0 in FT_ON_ACT:
                    src = v3(result(act, ("ft", b0))[:, 0:n * SEQ], n)
                    if b0 in FT_GAIN:
                        g = COL_QK + FT_GAIN[b0]
                        ins = nc.scalar.activation(ft[:, b0:b0 + n, :], src, ACT.Copy, scale=cols[:, g:g + 1])
                    else:
                        ins = nc.scalar.activation(ft[:, b0:b0 + n, :], src, ACT.Copy)
                    empties(ins, ("ft", b0))

            for qt in range(TT):
                nk = (qt + 1) * P
                for j in range(2):
                    bank = result(act, ("I", qt, j))
                    if j == 0 and qt > 0:
                        act.wait_ge(rel_used, qt)
                    ins = nc.scalar.activation(rel[:, j:4:2, 0:nk], v3(bank[:, :], 2)[:, :, 0:nk], ACT.Relu)
                    empties(ins, ("I", qt, j))

            def exps2(u):
                kind, qt, h = UNITS2[u]
                nk = (qt + 1) * P
                act.wait_ge(l_done, u + 1)
                o = 64 + 16 * (u % 4)
                parts = [(0, nk), (nk, 2 * nk), (2 * nk, 2 * nk + N_CMP)] if kind == "B" else \
                        [(0, nk * (3 if kind == "C" else 1))]
                for i, (lo, hi) in enumerate(parts):
                    ins = nc.scalar.activation(lbuf[:, u % 4, lo:hi], lbuf[:, u % 4, lo:hi], ACT.Exp,
                                               bias=small[:, o + i:o + i + 1],
                                               accum_out=small[:, o + 4 + i:o + 5 + i])
                ins.then_inc(exp2_done, 1)

            for u in range(AHEAD):
                exps2(u)
            for u, (kind, qt, h) in enumerate(UNITS2):
                nblk = (qt + 1) * len(unit_segments(kind, h))
                for i in range(0, nblk, 4):
                    n = min(4, nblk - i)
                    empties(nc.scalar.activation(pT[:, u % 2, i * P:(i + n) * P],
                                                 result(act, ("PT2", u, i // 4))[:, 0:n * P], ACT.Copy),
                            ("PT2", u, i // 4))
                if kind == "B":
                    empties(nc.scalar.activation(pcT[:, u % 2, :], result(act, ("PT2", u, "c"))[0:N_CMP, 0:P], ACT.Copy),
                            ("PT2", u, "c"))
                if u + AHEAD < len(UNITS2):
                    exps2(u + AHEAD)
                for i in MIX_AT[u]:
                    if i % 2 == 1:
                        b, tt = i // 4, i % 4 // 2
                        bank = result(act, ("mix", b, tt))
                        for k, (zc, lo, n) in enumerate(MIX_Z[b]):
                            ins = nc.scalar.activation(z[:, tt, zc:zc + n], bank[:, lo:lo + n], ACT.Copy)
                        empties(ins, ("mix", b, tt))
            for kind, n in (("A", 4), ("B", 4), ("C", 2)):
                for i in range(n):
                    empties(nc.scalar.activation(oT2[:, {"A": 0, "B": 4, "C": 8}[kind] + i, :],
                                                 result(act, ("oT2", kind, i))[:, 0:SEQ], ACT.Copy), ("oT2", kind, i))
            i = 0
            for nb in range(2):
                for br in range(3):
                    for tt in range(TT):
                        wait_emptied(act, ("mix", nb * 3 + br, tt))
                        if i >= 2:
                            n2, b2 = divmod(i - 2, 6)
                            wait_emptied(act, (f"branch{b2 // 2}", n2, b2 % 2))
                        for zc, lo, n in MIX_Z[nb * 3 + br]:
                            ins = nc.scalar.activation(tmp[:, i % 2, lo:lo + n], z[:, tt, zc:zc + n], ACT.Sigmoid)
                        ins.then_inc(sig_done, 1)
                        i += 1
            for ch in range(KC):
                empties(nc.scalar.activation(hT[:, ch, 0:SEQ], result(act, ("mixed", ch))[:, 0:SEQ], ACT.Copy),
                        ("mixed", ch))
            gained("ffn2_h", COL_N2)
            ffn("ffn2")

        @block.vector
        def _(dve):
            steps = [0]
            V = nc.vector

            def step(ins):
                ins.then_inc(dve_step, 1)
                steps[0] += 1

            def settle():
                dve.wait_ge(dve_step, steps[0])

            step(V.memset(ones[:, :], 1.0))
            V.memset(neghalf[:, :], -0.5).then_inc(consts_done, 1)
            bank = result(dve, "cols")
            empties(V.tensor_copy(cols[:, :], bank[:, 0:N_COLS]), "cols")
            wait_emptied(dve, "cols")
            step(V.tensor_scalar(cols[:, COL_SUB:COL_SUB + 1], cols[:, COL_SUB:COL_SUB + 1], 1.0 - LAM_INIT, None,
                                 ALU.mult))
            empties(V.tensor_copy(posT[:, :], result(dve, "pos")[:, 0:32]), "pos")
            bank = result(dve, "srow")
            empties(V.tensor_tensor(srow[:, :], bank[0:REL_HEADS, 0:SROW], rm_sb, ALU.add), "srow")
            wait_emptied(dve, "srow")
            V.memset(lam[:, 7:8], 0.0).then_inc(srow_done, 1)

            dve.wait_ge(lam_landed, 16)
            lp = small[:, 128:256]
            step(V.tensor_tensor(v3(lp, 2), lam_in[:, 0:4:2, :], lam_in[:, 1:4:2, :], ALU.mult))
            settle()
            V.tensor_reduce(lam[:, 0:2], v3(lp, 2), AX, ALU.add).then_inc(lam_sum, 1)
            dve.wait_ge(lam_exp, 1)
            step(V.tensor_tensor(lam[:, 4:5], lam[:, 3:4], lam[:, 2:3], ALU.subtract))
            settle()
            step(V.tensor_scalar(lam[:, 5:6], lam[:, 4:5], -LAM_INIT, None, ALU.add))

            for e in range(4):
                comp, half = divmod(e, 2)
                src = result(dve, ("mod", e))[:, 0:8].rearrange("p (s c) -> p c s", c=2)
                bcol = cols[:, COL_BMOD + comp * KC + half * 4:COL_BMOD + comp * KC + half * 4 + 4]
                step(V.scalar_tensor_tensor(modcol[:, comp, half * 4:half * 4 + 4], src[:, 0, :], float(comp),
                                            bcol, ALU.add, ALU.add))
                empties(V.scalar_tensor_tensor(modcol[:, 2 + comp, half * 4:half * 4 + 4], src[:, 1, :],
                                               float(comp), bcol, ALU.add, ALU.add), ("mod", e))
            wait_emptied(dve, ("mod", 2))
            wait_emptied(dve, ("mod", 3))
            for ch in range(KC):
                bank = result(dve, ("con", ch))
                empties(V.tensor_scalar(hT[:, ch, SEQ:2 * SEQ], bank[:, 0:SEQ], modcol[:, 3, ch:ch + 1],
                                        modcol[:, 2, ch:ch + 1], ALU.mult, ALU.add), ("con", ch))

            def mod_product(e):
                if e >= N_EVENTS:
                    return
                dve.wait_ge(mod_landed[e % MODS], 16 * (e // MODS + 1))
                if e - MODS >= FIRST_DVE_EVENT:
                    result(dve, ("mod", e - MODS))
                acc = modacc[:, e % MODS, :]
                w = modring[e % MODS]
                for j in range(KC):
                    c = cs[:, 2 * j:2 * j + 1]
                    if j == 0:
                        ins = V.tensor_scalar(acc, w[:, j, :], c, None, ALU.mult)
                    else:
                        settle()
                        ins = V.scalar_tensor_tensor(acc, w[:, j, :], c, acc, ALU.mult, ALU.add)
                    if j < KC - 1:
                        step(ins)
                ins.then_inc(mod_acc, 1)

            def mod_finish(e):
                comp, half = divmod(e % 12, 2)
                cols_ = slice(half * NB, half * NB + NB)
                bank = result(dve, ("mod", e))
                if mod_is_row(e):
                    if comp in (0, 1):
                        dst = mod_rows[:, comp, cols_]
                        dve.wait_ge(rows_landed, 32)
                    else:
                        dst = (g1row if comp == 2 else g2row)[:, cols_]
                        dve.wait_ge(g_landed[comp], 16 * (e // 12 + 1))
                    ins = V.scalar_tensor_tensor(dst, bank[:, :], 1.0 if comp == 1 else 0.0, dst, ALU.add, ALU.add)
                else:
                    slot = (4 if e < 12 else 6) + comp - 3
                    b0 = COL_BMOD + (e // 12) * 48 + comp * KC + half * 4
                    ins = V.scalar_tensor_tensor(modcol[:, slot, half * 4:half * 4 + 4], bank[:, 0:4],
                                                 1.0 if comp == 4 else 0.0, cols[:, b0:b0 + 4], ALU.add, ALU.add)
                empties(ins, ("mod", e))

            dve.wait_ge(csil_done, 1)
            mod_product(4)
            mod_product(5)
            for nb in range(6):
                if nb < 4:
                    for tt in range(TT):
                        buf = (q_tok if nb < 2 else k_tok)[:, tt, (nb % 2) * NB:(nb % 2) * NB + NB]
                        wait_emptied(dve, ("qkv", nb, tt))
                        pairs = buf.rearrange("p (h s d) -> p h s d", s=2, d=HD // 2)
                        t0 = tmp[:, 0, :].rearrange("p (h n) -> p h n", n=HD)
                        t1 = tmp[:, 1, :].rearrange("p (h s d) -> p h s d", s=2, d=HD // 2)
                        cos2 = rope[:, 2 * tt, :].unsqueeze(1).broadcast_to([P, 8, HD])
                        sin2 = rope[:, 2 * tt + 1, :]
                        settle()
                        step(V.tensor_tensor(t0, buf.rearrange("p (h n) -> p h n", n=HD), cos2, ALU.mult))
                        for s in range(2):
                            sn = sin2[:, s * 32:(s + 1) * 32].unsqueeze(1).broadcast_to([P, 8, 32])
                            step(V.tensor_tensor(t1[:, :, s, :], pairs[:, :, 1 - s, :], sn, ALU.mult))
                        settle()
                        V.tensor_tensor(buf, tmp[:, 0, :], tmp[:, 1, :], ALU.add).then_inc(rope_done, 1)
                        dve.wait_ge(rope_done, 2 * nb + tt + 1)
                for e in QKV_EVENTS[nb]:
                    mod_finish(e)
                    if e + 2 < 14:
                        mod_product(e + 2)
            for h in range(HEADS):
                empties(V.tensor_copy(qT[:, h, :], result(dve, ("qT", h))[:, 0:SEQ]), ("qT", h))

            def maxima(u):
                s = 8 * (u % 4)
                for m in range(2):
                    step(V.tensor_reduce(small[:, s + 4 + m:s + 5 + m], result(dve, ("S", u, m))[:, :], AX, ALU.max))
                settle()
                V.tensor_scalar(small[:, s:s + 2], small[:, s + 4:s + 6], -HD ** -0.5, None, ALU.mult)\
                    .then_inc(nmax_done, 1)

            def combine(u):
                s = 8 * (u % 4)
                wait_emptied(dve, ("S", u, 0))
                wait_emptied(dve, ("S", u, 1))
                step(V.reciprocal(small[:, s + 6:s + 8], small[:, s + 2:s + 4]))
                settle()
                step(V.tensor_scalar(small[:, 44:45], small[:, s + 7:s + 8], lam[:, 5:6], None, ALU.mult))
                settle()
                p0, p1 = prob[:, u % 4, 0, :], prob[:, u % 4, 1, :]
                step(V.tensor_scalar(p1, p1, small[:, 44:45], None, ALU.mult))
                settle()
                V.scalar_tensor_tensor(p0, p0, small[:, s + 6:s + 7], p1, ALU.mult, ALU.add).then_inc(probs_done, 1)

            rstds = [0]

            def inverse_root(var, n):
                rstds[0] += 1
                dve.wait_ge(rstd_done, rstds[0])
                return small[:, 32:32 + n]

            def head_var(g):
                dve.wait_ge(sq_done, g + 1)
                step(V.tensor_reduce(small[:, 36:40], v3(tmp[:, 0, :], 4), AX, ALU.add))
                settle()
                V.tensor_scalar(small[:, 40:44], small[:, 36:40], 1.0 / P, LN_EPS, ALU.mult, ALU.add)\
                    .then_inc(var_done, 1)

            def head_norm(g):
                r = inverse_root(None, 4)
                qt, h0 = UNITS0[4 * g]
                ins = V.tensor_tensor(v3(y_tok[:, qt, h0 * P:(h0 + 4) * P], 4), v3(result(dve, ("O", g))[:, :], 4),
                                      r.unsqueeze(2).broadcast_to([P, 4, P]), ALU.mult)
                empties(ins, ("O", g))
                wait_emptied(dve, ("O", g))
                V.memset(small[:, 47:48], 0.0).then_inc(o_done, 1)

            for u in range(AHEAD):
                maxima(u)
            combine(0)
            for u in range(len(UNITS0)):
                if u + 1 < len(UNITS0):
                    combine(u + 1)
                if u + AHEAD < len(UNITS0):
                    maxima(u + AHEAD)
                if u and u % 4 == 0:
                    head_var(u // 4 - 1)
                if u > 1 and u % 4 == 1:
                    head_norm(u // 4 - 1)
            head_var(3)
            head_norm(3)

            xs = [0]

            def residual_norm(stage, gate, ln, used):
                for nb in range(2):
                    for tt in range(TT):
                        sl = slice(nb * NB, nb * NB + NB)
                        y = y_tok[:, tt, sl]
                        empties(V.tensor_tensor(y, result(dve, (stage, nb, tt))[:, :], gate[:, sl], ALU.mult),
                                (stage, nb, tt))
                        wait_emptied(dve, (stage, nb, tt))
                        step(V.scalar_tensor_tensor(y, x_tok[:, tt, sl], ALPHA, y, ALU.mult, ALU.add))
                        settle()
                        st = small[:, 100 + 12 * tt + 6 * nb:106 + 12 * tt + 6 * nb]
                        step(V.bn_stats(st, y))
                V.memset(small[:, 47:48], 0.0).then_inc(used, 1)
                settle()
                for tt in range(TT):
                    step(V.bn_aggr(small[:, 124 + 2 * tt:126 + 2 * tt], small[:, 100 + 12 * tt:112 + 12 * tt]))
                settle()
                V.tensor_scalar(small[:, 24:26], small[:, 125:129:2], LN_EPS, None, ALU.add).then_inc(var_done, 1)
                r = inverse_root(None, 2)
                for tt in range(TT):
                    step(V.tensor_scalar(y_tok[:, tt, :], y_tok[:, tt, :], small[:, 124 + 2 * tt:125 + 2 * tt],
                                         r[:, tt:tt + 1], ALU.subtract, ALU.mult))
                    settle()
                    if tt == 0:
                        dve.wait_ge(ln_landed, 32 * (ln + 1))
                    step(V.tensor_tensor(y_tok[:, tt, :], y_tok[:, tt, :], ln_rows[:, 0, :], ALU.mult))
                    settle()
                    V.tensor_tensor(x_tok[:, tt, :], y_tok[:, tt, :], ln_rows[:, 1, :], ALU.add).then_inc(x_done, 1)
                    xs[0] += 1
                dve.wait_ge(x_done, xs[0])
                V.memset(small[:, 47:48], 0.0).then_inc(ln_used, 1)

            def modulated(stage, shift, scale):
                for ch in range(1, KC, 2):
                    empties(V.tensor_scalar(hT[:, ch, 0:SEQ], result(dve, (stage, ch))[:, 0:SEQ],
                                            modcol[:, scale, ch:ch + 1], modcol[:, shift, ch:ch + 1],
                                            ALU.mult, ALU.add), (stage, ch))

            def gained(stage, col):
                for ch in range(1, KC, 2):
                    empties(V.tensor_scalar(hT[:, ch, 0:SEQ], result(dve, (stage, ch))[:, 0:SEQ],
                                            cols[:, col + ch:col + ch + 1], None, ALU.mult), (stage, ch))

            def ffn(name):
                for nb in range(FNB):
                    wait_emptied(dve, (name, "g", nb))
                    bank = result(dve, (name, "u", nb))
                    empties(V.tensor_tensor(ffT[:, 2 * nb:2 * nb + 2, :], v3(tmp[:, nb % 2, :], 2),
                                            v3(bank[:, :], 2), ALU.mult), (name, "u", nb))
                    for e in FFN_EVENTS[name].get(nb, []):
                        mod_finish(e)
                        mod_product(e + 2)

            residual_norm("wo", g1row, 0, g1_used)
            modulated("ffn0_h", 4, 5)
            ffn("ffn0")
            residual_norm("ffn0_out", g2row, 1, g2_used)

            dve.wait_ge(psc_landed, 16)
            step(V.tensor_tensor(g1row, g1row, pscale, ALU.mult))
            for tt in range(TT):
                step(V.tensor_tensor(hx_tok[:, tt, :], x_tok[:, tt, :], mod_rows[:, 1, :], ALU.mult))
                settle()
                V.tensor_tensor(hx_tok[:, tt, :], hx_tok[:, tt, :], mod_rows[:, 0, :], ALU.add).then_inc(hx_done, 1)
            residual_norm("poolw", g1row, 2, g1_used)
            modulated("ffn1_h", 6, 7)
            ffn("ffn1")
            residual_norm("ffn1_out", g2row, 3, g2_used)

            def rms_input():
                for tt in range(TT):
                    step(V.tensor_tensor_reduce(y_tok[:, tt, :], x_tok[:, tt, :], x_tok[:, tt, :], 1.0, 0.0,
                                                ALU.mult, ALU.add, small[:, 20 + tt:21 + tt]))
                settle()
                V.tensor_scalar(small[:, 24:26], small[:, 20:22], 1.0 / D, RMS_EPS, ALU.mult, ALU.add)\
                    .then_inc(var_done, 1)
                r = inverse_root(None, 2)
                for tt in range(TT):
                    V.tensor_scalar(y_tok[:, tt, :], x_tok[:, tt, :], r[:, tt:tt + 1], None, ALU.mult)\
                        .then_inc(xn_done, 1)

            rms_input()
            gained("z_h", COL_N1)

            ss = v3(small[:, 128:128 + 2 * SS_N], TT)
            rs = v3(small[:, 224:224 + 2 * SS_N], TT)
            scr = tmp[:, :, :].rearrange("p a b -> p (a b)")

            def squares(col, heads, idx):
                for tt in range(TT):
                    zz = z[:, tt, col:col + heads * HD]
                    settle()
                    step(V.tensor_tensor(scr[:, 0:heads * HD], zz, zz, ALU.mult))
                    settle()
                    step(V.tensor_reduce(ss[:, tt, idx:idx + heads], v3(scr[:, 0:heads * HD], heads), AX, ALU.add))

            def after_block(nb):
                wait_emptied(dve, ("z", nb, 0))
                wait_emptied(dve, ("z", nb, 1))

            after_block(0)
            squares(AQ, 8, SS_AQ)
            after_block(1)
            squares(AK, 1, SS_AK)
            for tt in range(TT):
                step(V.tensor_copy(v3(kdup[:, tt, 1, :], 2), z[:, tt, IK:IK + HD].unsqueeze(1).broadcast_to([P, 2, HD])))
            after_block(2)
            squares(BQ, 8, SS_BQ)
            after_block(3)
            squares(BKS, 2, SS_KS)
            for tt in range(TT):
                src = z[:, tt, BKC:BKC + 4 * HD].rearrange("p (b n) -> p b n", b=4)
                step(V.tensor_copy(kdup[:, tt, 6:10, :].rearrange("p b (s n) -> p b s n", s=2),
                                   src.unsqueeze(2).broadcast_to([P, 4, 2, HD])))
            after_block(4)
            squares(BKW, 2, SS_KW)
            after_block(5)
            after_block(6)
            squares(CQ, 12, SS_CQ)
            after_block(7)
            squares(CK, 12, SS_CK)
            settle()
            V.tensor_scalar(small[:, 128:128 + 2 * SS_N], small[:, 128:128 + 2 * SS_N], 1.0 / HD, RMS_EPS,
                            ALU.mult, ALU.add).then_inc(var_done, 1)
            rstds[0] += 1
            dve.wait_ge(rstd_done, rstds[0])
            for tt in range(TT):
                for idx, col, slot in ((SS_AK, AK, 0), (SS_KS, BKS, 2), (SS_KS + 1, BKS + HD, 3),
                                       (SS_KW, BKW, 4), (SS_KW + 1, BKW + HD, 5)):
                    step(V.tensor_scalar(v3(kdup[:, tt, slot, :], 2),
                                         z[:, tt, col:col + HD].unsqueeze(1).broadcast_to([P, 2, HD]),
                                         rs[:, tt, idx:idx + 1], None, ALU.mult))
                ck = v3(z[:, tt, CK:CK + 768], 12)
                step(V.tensor_tensor(ck, ck, rs[:, tt, SS_CK:SS_CK + 12].unsqueeze(2).broadcast_to([P, 12, HD]),
                                     ALU.mult))
            settle()
            V.tensor_scalar(small[:, 224:224 + 2 * SS_N], small[:, 224:224 + 2 * SS_N], HD ** -0.5, None, ALU.mult)\
                .then_inc(zsrc_done, 1)

            for i in range(4):
                bank = result(dve, ("dupT", i))
                for half in range(2):
                    rows = slice(half * HD, (half + 1) * HD)
                    for lo in range(2):
                        win = bank[rows, lo * CMP_STRIDE:lo * CMP_STRIDE + N_CMP * CMP_STRIDE]
                        win = win.rearrange("p (n l j) -> p j l n", l=8, j=2)[:, half, :, :]
                        pos = posT[rows, (i // 2) * 16 + lo * 8:(i // 2) * 16 + lo * 8 + 8]
                        ins = V.tensor_tensor(xc[rows, i, lo * 8:lo * 8 + 8, :], win,
                                              pos.unsqueeze(2).broadcast_to([HD, 8, N_CMP]), ALU.add)
                        if half == 1 and lo == 1:
                            empties(ins, ("dupT", i))
                        else:
                            step(ins)
            wait_emptied(dve, ("dupT", 3))
            V.memset(small[:, 47:48], 0.0).then_inc(xc_done, 1)
            for b0, n in FT_PAIRS:
                if b0 not in FT_ON_ACT:
                    src = v3(result(dve, ("ft", b0))[:, 0:n * SEQ], n)
                    if b0 in FT_GAIN:
                        g = COL_QK + FT_GAIN[b0]
                        ins = V.tensor_scalar(ft[:, b0:b0 + n, :], src, cols[:, g:g + 1], None, ALU.mult)
                    else:
                        ins = V.tensor_copy(ft[:, b0:b0 + n, :], src)
                    empties(ins, ("ft", b0))

            bank = result(dve, "cmp")
            step(V.tensor_copy(ckd[:, :, 0:HD], v3(bank[0:N_CMP, 0:2 * HD], 2)))
            empties(V.tensor_copy(vcmp, v3(bank[0:N_CMP, 2 * HD:4 * HD], 2)), "cmp")
            settle()
            sq = v3(scr[0:N_CMP, 0:2 * HD], 2)
            step(V.tensor_tensor(sq, ckd[:, :, 0:HD], ckd[:, :, 0:HD], ALU.mult))
            settle()
            step(V.memset(small[:, 20:22], 1.0))
            settle()
            step(V.tensor_reduce(small[0:N_CMP, 20:22], sq, AX, ALU.add))
            settle()
            V.tensor_scalar(small[:, 24:26], small[:, 20:22], 1.0 / HD, RMS_EPS, ALU.mult, ALU.add)\
                .then_inc(var_done, 1)
            r = inverse_root(None, 2)
            step(V.tensor_tensor(ckd[:, :, 0:HD], ckd[:, :, 0:HD],
                                 r[0:N_CMP, :].unsqueeze(2).broadcast_to([N_CMP, 2, HD]), ALU.mult))
            settle()
            V.tensor_copy(ckd[:, :, HD:P], ckd[:, :, 0:HD]).then_inc(ckd_done, 1)
            bank = result(dve, "kcT")
            src = bank[:, 0:2 * P].rearrange("p (g n) -> p g n", g=2)[:, :, 0:N_CMP]
            empties(V.tensor_scalar(kcT, src, cols[:, COL_QK + 3:COL_QK + 4], None, ALU.mult), "kcT")

            dve.wait_ge(bias_landed, 16)
            for qt in range(TT):
                nk = (qt + 1) * P
                for h in range(4):
                    wait_emptied(dve, ("I", qt, h % 2))
                    settle()
                    ins = V.scalar_tensor_tensor(score[qt], rel[:, h, 0:nk], z[:, qt, IW + h:IW + h + 1],
                                                 causal[:, SEQ - nk:SEQ] if h == 0 else score[qt],
                                                 ALU.mult, ALU.add)
                    if h < 3:
                        step(ins)
                ins.then_inc(rel_used, 1)
                dve.wait_ge(rel_used, qt + 1)

            def top_keys(i):
                qt, it = divmod(i, TOPK // 8)
                src = score[qt] if it == 0 else work[qt]
                settle()
                step(V.max(small[:, 40:48], src))
                settle()
                step(V.match_replace(work[qt], small[:, 40:48], src, TAKEN))
                if it == TOPK // 8 - 1:
                    settle()
                    step(V.tensor_scalar(selmask[qt], work[qt], 0.5 * TAKEN, NEG, ALU.is_gt, ALU.mult))

            dve.wait_ge(gates_done, 2 * TT)

            def logits(u):
                kind, qt, h = UNITS2[u]
                nk = (qt + 1) * P
                L = lbuf[:, u % 4, :]
                o = 64 + 16 * (u % 4)
                segs = unit_segments(kind, h)
                v = u - AHEAD - 1
                if v >= 0:
                    kk, q2, h2 = UNITS2[v]
                    nb2 = (q2 + 1) * len(unit_segments(kk, h2))
                    result(dve, ("PT2", v, "c" if kk == "B" else (nb2 - 1) // 4))
                for s, (qb, kb, bh, _) in enumerate(segs):
                    idx = {"A": SS_AQ + h, "B": SS_BQ + h, "C": SS_CQ + 4 * s + h}[kind]
                    bank = result(dve, ("S2", u, s // 2))
                    ins = V.scalar_tensor_tensor(L[:, s * nk:(s + 1) * nk], bank[:, (s % 2) * 256:(s % 2) * 256 + nk],
                                                 rs[:, qt, idx:idx + 1], bias[:, bh, SEQ - nk:SEQ], ALU.mult, ALU.add)
                    if s % 2 == 1 or s == len(segs) - 1:
                        empties(ins, ("S2", u, s // 2))
                        wait_emptied(dve, ("S2", u, s // 2))
                    else:
                        step(ins)
                if kind == "A":
                    step(V.tensor_tensor(L[:, 0:nk], L[:, 0:nk], selmask[qt], ALU.add))
                    settle()
                if kind == "B":
                    end = 2 * nk + N_CMP
                    empties(V.scalar_tensor_tensor(L[:, 2 * nk:end], result(dve, ("S2", u, "c"))[:, 0:N_CMP],
                                                   rs[:, qt, SS_BQ + h:SS_BQ + h + 1], cmp_mask[:, qt, :],
                                                   ALU.mult, ALU.add), ("S2", u, "c"))
                    step(V.tensor_reduce(small[:, o + 8:o + 10], v3(L[:, 0:2 * nk], 2), AX, ALU.max))
                    wait_emptied(dve, ("S2", u, "c"))
                    step(V.tensor_reduce(small[:, o + 10:o + 11], L[:, 2 * nk:end], AX, ALU.max))
                    settle()
                    V.tensor_scalar(small[:, o:o + 3], small[:, o + 8:o + 11], 0.1 * NEG, -1.0, ALU.max, ALU.mult)\
                        .then_inc(l_done, 1)
                else:
                    step(V.tensor_reduce(small[:, o + 8:o + 9], L[:, 0:len(segs) * nk], AX, ALU.max))
                    settle()
                    V.tensor_scalar(small[:, o:o + 1], small[:, o + 8:o + 9], -1.0, None, ALU.mult).then_inc(l_done, 1)

            def inv_sum(u):
                kind, qt, h = UNITS2[u]
                return 48 + 8 * qt + h

            def weigh(u):
                kind, qt, h = UNITS2[u]
                nk = (qt + 1) * P
                L = lbuf[:, u % 4, :]
                o = 64 + 16 * (u % 4)
                dve.wait_ge(exp2_done, u + 1)
                if kind != "B":
                    V.reciprocal(small[:, inv_sum(u):inv_sum(u) + 1], small[:, o + 4:o + 5]).then_inc(p_done, 1)
                    return
                step(V.tensor_scalar(small[:, o + 12:o + 15], small[:, o + 4:o + 7], 1e-30, None, ALU.max))
                settle()
                step(V.reciprocal(small[:, o + 8:o + 11], small[:, o + 12:o + 15]))
                settle()
                step(V.tensor_tensor(small[:, o + 12:o + 15], small[:, o + 8:o + 11], gates[:, qt, h, :], ALU.mult))
                settle()
                step(V.tensor_scalar(L[:, 0:nk], L[:, 0:nk], small[:, o + 12:o + 13], None, ALU.mult))
                step(V.tensor_scalar(L[:, nk:2 * nk], L[:, nk:2 * nk], small[:, o + 13:o + 14], None, ALU.mult))
                V.tensor_scalar(L[:, 2 * nk:2 * nk + N_CMP], L[:, 2 * nk:2 * nk + N_CMP], small[:, o + 14:o + 15],
                                None, ALU.mult).then_inc(p_done, 1)

            def outputs(u):
                kind, qt, h = UNITS2[u]
                heads = h + 1
                bank = result(dve, ("O2", kind, qt))
                src, dst = v3(bank[:, 0:heads * HD], heads), v3(o2_tok(kind, qt), heads)
                if kind == "B":
                    empties(V.tensor_copy(dst, src), ("O2", kind, qt))
                else:
                    r0 = inv_sum(u - h)
                    empties(V.tensor_tensor(dst, src, small[:, r0:r0 + heads].unsqueeze(2)
                                            .broadcast_to([P, heads, HD]), ALU.mult), ("O2", kind, qt))

            for u in range(AHEAD):
                logits(u)
            weigh(0)
            for u, (kind, qt, h) in enumerate(UNITS2):
                if u + 1 < len(UNITS2):
                    weigh(u + 1)
                if u + AHEAD < len(UNITS2):
                    logits(u + AHEAD)
                if u < TT * TOPK // 8:
                    top_keys(u)
                if u and UNITS2[u - 1][0:2] != (kind, qt):
                    outputs(u - 1)
            outputs(len(UNITS2) - 1)

            i = 0
            for nb in range(2):
                for br in range(3):
                    for tt in range(TT):
                        y = y_tok[:, tt, nb * NB:nb * NB + NB]
                        dve.wait_ge(sig_done, i + 1)
                        bank = result(dve, (f"branch{br}", nb, tt))
                        if i == 0:
                            wait_emptied(dve, ("oT2", "C", 1))
                        g = tmp[:, i % 2, :]
                        if br == 0:
                            empties(V.tensor_tensor(y, g, bank[:, :], ALU.mult), (f"branch{br}", nb, tt))
                            wait_emptied(dve, (f"branch{br}", nb, tt))
                        else:
                            t = lbuf[:, tt, 0:NB]
                            settle()
                            empties(V.tensor_tensor(t, g, bank[:, :], ALU.mult), (f"branch{br}", nb, tt))
                            wait_emptied(dve, (f"branch{br}", nb, tt))
                            ins = V.tensor_tensor(y, y, t, ALU.add)
                            if nb == 1 and br == 2 and tt == 1:
                                ins.then_inc(mix_done, 1)
                            else:
                                step(ins)
                        i += 1

            def residual(stage, done=None):
                for nb in range(2):
                    for tt in range(TT):
                        x = x_tok[:, tt, nb * NB:nb * NB + NB]
                        empties(V.tensor_tensor(x, x, result(dve, (stage, nb, tt))[:, :], ALU.add), (stage, nb, tt))
                for tt in range(TT):
                    wait_emptied(dve, (stage, 1, tt))

            residual("w_out")
            rms_input()
            gained("ffn2_h", COL_N2)
            ffn("ffn2")
            residual("ffn2_out")

        @block.gpsimd
        def _(pool):
            roots = [0]

            def mod_panel(e):
                prev = e - MODS
                if prev >= FIRST_DVE_EVENT:
                    pool.wait_ge(mod_acc, prev - FIRST_DVE_EVENT + 1)
                elif prev >= 0:
                    result(pool, ("mod", prev))
                l, blk = divmod(e, 12)
                pool.dma_start(modring[e % MODS], a["w_mod"][l, :, blk * NB:(blk + 1) * NB]
                               .rearrange("(p j) n -> p j n", j=KC)).then_inc(mod_landed[e % MODS], 16)

            def bias_row(dst, l, comp, sem_):
                pool.dma_start(dst, a["b_mod"][l, comp * D:(comp + 1) * D].partition_broadcast(P)).then_inc(sem_, 16)

            def ln_load(n):
                for i, w in enumerate(("ln_g", "ln_b")):
                    pool.dma_start(ln_rows[:, i, :], a[w][n // 2, n % 2, :].partition_broadcast(P))\
                        .then_inc(ln_landed, 16)

            def inverse_root(src, dst, n):
                roots[0] += 1
                pool.wait_ge(var_done, roots[0])
                nc.gpsimd.tensor_tensor(small[:, dst:dst + n], small[:, src:src + n], neghalf[:, 0:n], ALU.pow)\
                    .then_inc(rstd_done, 1)

            mod_panel(0)
            mod_panel(1)
            pool.dma_start(lam_in, a["attn_lambda"][0].partition_broadcast(P)).then_inc(lam_landed, 16)
            for e in range(2, 6):
                mod_panel(e)
            bias_row(g1row, 0, 2, g_landed[2])
            bias_row(g2row, 0, 5, g_landed[5])
            ln_load(0)
            for e in range(6, 16):
                mod_panel(e)
            pool.wait_ge(consts_done, 1)
            for _ in range(4):
                inverse_root(40, 32, 4)
            inverse_root(24, 32, 2)
            for comp in range(2):
                bias_row(mod_rows[:, comp, :], 1, comp, rows_landed)
            pool.dma_start(pool_m, a["const_pool"].rearrange("p (a b) -> p a b", a=TT * 4)).then_inc(poolm_landed, 16)
            pool.dma_start(pscale, a["pool_scale"][0].partition_broadcast(P)).then_inc(psc_landed, 16)
            pool.wait_ge(g1_used, 1)
            bias_row(g1row, 1, 2, g_landed[2])
            pool.wait_ge(ln_used, 1)
            ln_load(1)
            for e in range(16, N_EVENTS):
                mod_panel(e)
            inverse_root(24, 32, 2)
            pool.wait_ge(g2_used, 1)
            bias_row(g2row, 1, 5, g_landed[5])
            pool.wait_ge(ln_used, 2)
            ln_load(2)
            inverse_root(24, 32, 2)
            pool.wait_ge(ln_used, 3)
            ln_load(3)
            inverse_root(24, 32, 2)
            inverse_root(24, 32, 2)
            inverse_root(128, 224, 2 * SS_N)
            inverse_root(24, 32, 2)
            inverse_root(24, 32, 2)

        @block.sync
        def _(sp):
            n1 = 48 * DEPTH
            small_loads = [
                (colsrc[0:n1, :], a["b_mod"].rearrange("l (n p) -> (l n) p", p=P)),
                (colsrc[COL_N1:COL_N1 + KC, :], a["norm1_g_2"].rearrange("l (n p) -> (l n) p", p=P)),
                (colsrc[COL_N2:COL_N2 + KC, :], a["norm2_g_2"].rearrange("l (n p) -> (l n) p", p=P)),
                (colsrc[COL_SUB:COL_SUB + 1, :], a["attn_subln_g"]),
                (colsrc[COL_QK:COL_QK + 6, 0:HD], a["qk_norm_g_2"][0]),
                (colsrc[COL_QK:COL_QK + 6, HD:P], a["qk_norm_g_2"][0]),
                (possrc, a["nsa_cmp_pos_2"][0].rearrange("v (l j) d -> (v l) (j d)", j=2)),
                (oh_sb, a["const_onehot"]),
                (rm_sb, a["const_rowmask"]),
                (rel_sb, a["rel_bias_2"]),
            ]
            for dst, src in small_loads:
                sp.dma_start(dst, src).then_inc(cols_landed, 16)
            sp.dma_start(table[:, :], a["const_table"]).then_inc(table_landed, 16)
            sp.dma_start(x_tok, a["x"][0].rearrange("(t p) d -> p t d", p=P)).then_inc(x_landed, 16)
            sp.dma_start(y_tok, a["ctx"][0].rearrange("(t p) d -> p t d", p=P)).then_inc(ctx_landed, 16)
            sp.wait_ge(mod_landed[3 % MODS], 16 * (3 // MODS + 1))
            for i, (key, parts, chunks, width) in enumerate(panels):
                if i >= RING:
                    sp.wait_ge(w_used, i - RING + 1)
                slot = ring[i % RING][:, 0:chunks * width].rearrange("p (c n) -> p c n", c=chunks)
                for src, lo, n in parts:
                    sp.dma_start(slot[:, :, lo:lo + n], src).then_inc(w_landed[i % RING], 16)
                if key == ("ffn1_in", 2, 0):
                    sp.wait_ge(srow_stored, 16)
                    sp.wait_ge(mod_acc, N_EVENTS - FIRST_DVE_EVENT)
                    sp.dma_start(bias, bass.AP(scratch.tensor, P - 1, [[SROW - 1, P], [P * SROW, REL_HEADS], [1, SEQ]]))\
                        .then_inc(bias_landed, 16)
            for tt in range(TT):
                wait_emptied(sp, ("ffn2_out", 1, tt))
                sp.dma_start(out[0, tt * P:(tt + 1) * P, :], x_tok[:, tt, :]).then_inc(out_stored, 16)
            sp.wait_ge(out_stored, 16 * TT)


_INS = ["x", "c", "ctx", "c_ctx", "w_mod", "b_mod", "ln_g", "ln_b", "attn_w_qkv", "attn_lambda",
        "attn_subln_g", "attn_w_o", "pool_w", "pool_scale", "ffn_w_in", "ffn_w_out", "norm1_g_2",
        "norm2_g_2", "w_in_2", "qk_norm_g_2", "nsa_cmp_pos_2", "nsa_cmp_w_2", "w_branch_a_2",
        "w_branch_b_2", "w_branch_c_2", "w_out_2", "w_ffn_in_2", "w_ffn_out_2", "rel_bias_2"]


def kernel(**inputs):
    import concourse.bacc as _bacc
    from concourse.bass_utils import run_bass_kernel_spmd as _run

    nc = _bacc.Bacc("TRN2", target_bir_lowering=False, num_devices=1)
    arrays = {f"in_{n}": np.ascontiguousarray(inputs[n]) for n in _INS}
    arrays.update(shape_constants())
    args = {n.removeprefix("in_"): nc.dram_tensor(n, v.shape, F32, kind="ExternalInput").ap()
            for n, v in arrays.items()}
    out = nc.dram_tensor("out", (1, SEQ, D), F32, kind="ExternalOutput").ap()
    scratch = nc.dram_tensor("bias_rows", (REL_HEADS, P, SROW), F32, kind="Internal").ap()
    build(nc, args, out, scratch)
    return _run(nc, [arrays], core_ids=[0]).results[0]["out"]
```

```python
from contextlib import ExitStack

import numpy as np

import concourse.bass as bass
from concourse import mybir

F32 = mybir.dt.float32
F32R = mybir.dt.float32r
ALU = mybir.AluOpType
ACT = mybir.ActivationFunctionType
AX = mybir.AxisListType.X

P = 128
SEQ = 256
TT = SEQ // P
D = 1024
KC = D // P
NB = 512
PK = 4
HEADS = 8
HD = 64
DEPTH = 2
ALPHA = (2.0 * DEPTH) ** 0.25
LN_EPS = 1e-5
RMS_EPS = 1e-6
LAM_INIT = 0.8 - 0.6
D_FF = -(-8 * D // (3 * 256)) * 256
FC = D_FF // P
FNB = D_FF // 256
POOL_WINDOWS = (2, 4, 8, 16)
GRID_W = 64
NEG = -1.0e30
TAKEN = -3.0e38
TOPK = min(256, SEQ // 4)

AQ, AK, AV, IQ, IK, IW = 0, 512, 576, 640, 896, 960
BQ, BKC, BVC, BKS, BVS, BKW, BVW, BG = 964, 1476, 1604, 1732, 1860, 1988, 2116, 2244
CQ, CK, CV, MIX = 2268, 3036, 3804, 4572
ZW = MIX
Z_BLOCKS = [(0, 512), (512, 964), (964, 1476), (1476, 1860), (1860, 2268),
            (2268, 2780), (2780, 3292), (3292, 3804), (3804, 4316), (4316, 4572)]
CMP_LEN, CMP_STRIDE = 32, 16
N_CMP = (SEQ - CMP_LEN) // CMP_STRIDE + 1
C_GROUPS = ((128, 1), (512, 4), (2048, 16))
BUCKETS, MAX_DIST = 32, 2048
REL_HEADS = 28
SROW = 384

COL_BMOD, COL_N1, COL_N2, COL_SUB, COL_QK = 0, 96, 104, 112, 113
N_COLS = 119

SS_AQ, SS_AK, SS_BQ, SS_KS, SS_KW, SS_CQ, SS_CK, SS_N = 0, 8, 9, 17, 19, 21, 33, 45
SS_PARTS = ((0, SS_CQ), (SS_CQ, SS_CK), (SS_CK, SS_N))

RING = 4
PARTS = 2
AHEAD = 3
MODS = 2
WHOLE = ("pool", "cmp", "branch0", "branch1", "branch2")


def shape_constants():
    t = np.arange(SEQ)
    inv = np.power(np.float32(10000.0), -np.arange(16, dtype=np.float32) / np.float32(16))
    row = np.repeat(np.arange(SEQ // GRID_W, dtype=np.float32), GRID_W)
    col = np.tile(np.arange(GRID_W, dtype=np.float32), SEQ // GRID_W)
    ang = np.concatenate([row[:, None] * inv, col[:, None] * inv], axis=-1).astype(np.float32)
    cos, sin = np.cos(ang), np.sin(ang)
    rope = np.stack([np.concatenate([cos, cos], 1), np.concatenate([-sin, sin], 1)], 1)
    rope = rope.reshape(TT, P, 2 * HD).transpose(1, 0, 2).reshape(P, -1)
    dist = P + np.arange(P)[:, None] - np.arange(SEQ)[None, :]
    causal = np.where(dist >= 0, 0.0, NEG)
    cend = np.arange(N_CMP) * CMP_STRIDE + CMP_LEN - 1
    cmp_mask = np.where(cend[None, :] <= t[:, None], 0.0, NEG).reshape(TT, P, N_CMP)
    cmp_mask = cmp_mask.transpose(1, 0, 2).reshape(P, -1)
    table = np.concatenate([np.eye(P), rope, causal, cmp_mask], axis=1).astype(np.float32)

    d = SEQ - 1 - np.arange(SROW)
    n = np.maximum(d, 0)
    exact = BUCKETS // 2
    nf = np.maximum(n, 1).astype(np.float32)
    large = exact + (np.log(nf / np.float32(exact)) / np.float32(np.log(MAX_DIST / exact))
                     * np.float32(BUCKETS - exact)).astype(np.int32)
    bucket = np.where(n < exact, n, np.minimum(large, BUCKETS - 1))
    onehot = ((bucket[None, :] == np.arange(BUCKETS)[:, None]) & (d >= 0)).astype(np.float32)
    rowmask = np.zeros((REL_HEADS, SROW), np.float32)
    rowmask[:, d < 0] = NEG
    for g, (win, dil) in enumerate(C_GROUPS):
        rowmask[16 + 4 * g:20 + 4 * g, (d % dil != 0) | (d > win)] = NEG

    pool = np.zeros((len(POOL_WINDOWS), SEQ, SEQ), np.float32)
    for g, w in enumerate(POOL_WINDOWS):
        lo, hi = np.clip(t - w // 2, 0, SEQ), np.clip(t + w - w // 2, 0, SEQ)
        inside = (t[:, None] >= lo[None, :]) & (t[:, None] < hi[None, :])
        pool[g] = inside / (hi - lo)[None, :].astype(np.float32) - np.eye(SEQ)
    pool = pool.reshape(len(POOL_WINDOWS), TT, P, SEQ).transpose(2, 1, 0, 3)
    return {"const_table": table, "const_onehot": onehot, "const_rowmask": rowmask,
            "const_pool": np.ascontiguousarray(pool.reshape(P, -1)).astype(np.float32)}


def w_panels(a):
    out = []

    def add(key, w, kg, chunks, lo, hi):
        src = w[kg * PK * P:(kg * PK + chunks) * P, lo:hi].rearrange("(c p) n -> p c n", p=P)
        out.append((key, [(src, 0, hi - lo)], chunks, hi - lo))

    def ffn(name, w_in, w_out):
        for nb in range(FNB):
            for kg in range(2):
                rows = w_in[kg * PK * P:(kg + 1) * PK * P, :]
                parts = [(rows[:, h * D_FF + nb * 256:h * D_FF + nb * 256 + 256]
                          .rearrange("(c p) n -> p c n", p=P), h * 256, 256) for h in range(2)]
                out.append(((name + "_in", nb, kg), parts, PK, 512))
        for nb in range(2):
            for kg in range(-(-FC // PK)):
                add((name + "_out", nb, kg), w_out, kg, min(PK, FC - kg * PK), nb * NB, nb * NB + NB)

    for nb in range(6):
        for kg in range(2):
            add(("qkv", nb, kg), a["attn_w_qkv"][0], kg, PK, nb * NB, nb * NB + NB)
    for nb in range(2):
        for kg in range(2):
            add(("wo", nb, kg), a["attn_w_o"][0], kg, PK, nb * NB, nb * NB + NB)
    ffn("ffn0", a["ffn_w_in"][0], a["ffn_w_out"][0])
    out.append((("pool", 0, 0), [(a["pool_w"][0].rearrange("g (c p) n -> p (g c) n", p=P), 0, 256)], 8, 256))
    ffn("ffn1", a["ffn_w_in"][1], a["ffn_w_out"][1])
    w_in = a["w_in_2"][0]
    for nb, (lo, hi) in enumerate(Z_BLOCKS):
        for kg in range(2):
            add(("z", nb, kg), w_in, kg, PK, lo, hi)
    out.append((("cmp", 0, 0), [(a["nsa_cmp_w_2"][0].rearrange("v (l j) d e -> (j d) (v l) e", j=2), 0, HD)],
                32, HD))
    for nb in range(2):
        for br in range(3):
            for kg in range(2):
                lo = MIX + br * D + nb * NB
                add(("mix", nb * 3 + br, kg), w_in, kg, PK, lo, lo + NB)
    for nb in range(2):
        for br, w in enumerate(("w_branch_a_2", "w_branch_b_2", "w_branch_c_2")):
            add((f"branch{br}", nb, 0), a[w][0], 0, 2 if br == 2 else 4, nb * NB, nb * NB + NB)
    for nb in range(2):
        for kg in range(2):
            add(("w_out", nb, kg), a["w_out_2"][0], kg, PK, nb * NB, nb * NB + NB)
    ffn("ffn2", a["w_ffn_in_2"][0], a["w_ffn_out_2"][0])
    return out


def build(nc, a, out, scratch):
    panels = w_panels(a)
    panel_at = {key: i for i, (key, *_) in enumerate(panels)}

    with ExitStack() as ctx:
        def sb(name, cols, parts=P):
            return ctx.enter_context(nc.sbuf_tensor(name, [parts, cols], F32))

        def sem(name):
            return ctx.enter_context(nc.semaphore(name))

        def v3(ap, a_):
            return ap.rearrange("p (a b) -> p a b", a=a_)

        def parts(name, cols_, stack=ctx):
            return [stack.enter_context(nc.sbuf_tensor(f"{name}_{x}", [P, cols_], F32R)) for x in ("hi", "lo")]

        with ExitStack() as shared:
            ring_lo = [shared.enter_context(nc.sbuf_tensor(f"ring_lo{i}", [P, PK * NB], F32R)) for i in range(RING)]
        ring = [sb(f"ring{i}", PK * NB) for i in range(RING)]
        w_hi_buf = [ctx.enter_context(nc.sbuf_tensor(f"w_hi{i}", [P, PK * NB], F32R)) for i in range(PARTS)]
        with ExitStack() as shared:
            ff_parts = parts("ff", FC * SEQ, shared)
            shared.enter_context(nc.sbuf_tensor("between", [P, 12288 - 2 * FC * SEQ], F32))
            con_parts = parts("con", KC * SEQ, shared)
        big = sb("big", 16384)
        with ExitStack() as shared:
            prob_raw = shared.enter_context(nc.sbuf_tensor("prob", [P, 2 * KC * SEQ], F32))
        h_parts = parts("h", KC * SEQ)
        aux = sb("aux", 12288)
        x_tok = sb("x_tok", TT * D)[:].rearrange("p (t n) -> p t n", t=TT)
        y_tok = sb("y_tok", TT * D)[:].rearrange("p (t n) -> p t n", t=TT)
        table = sb("table", P + TT * 2 * HD + SEQ + TT * N_CMP)
        ident = table[:, 0:P]
        rope = v3(table[:, P:P + TT * 2 * HD], TT * 2)
        causal = table[:, P + 4 * HD:P + 4 * HD + SEQ]
        cmp_mask = v3(table[:, P + 4 * HD + SEQ:], TT)
        ones = sb("ones", P)
        neghalf = sb("neghalf", 96)
        cols = sb("cols", N_COLS)
        modcol = v3(sb("modcol", 64)[:], 8)
        cs_in = v3(sb("cs_in", 16)[:], 2)
        cs = sb("cs", 16)
        modacc_raw = sb("modacc", MODS * NB)
        modacc = v3(modacc_raw[:], MODS)
        tmp = v3(sb("tmp", 2 * NB)[:], 2)
        small = sb("small", 368)
        ss = v3(small[:, 128:128 + 2 * SS_N], TT)
        rs = v3(small[:, 224:224 + 2 * SS_N], TT)
        gates = small[:, 320:368].rearrange("p (t h g) -> p t h g", t=TT, h=8)
        srow = sb("srow", SROW, REL_HEADS)
        posT = sb("posT", 32)
        lam = sb("lam", 8)

        q_tok = v3(big[:, 0:2048], TT)
        k_tok = v3(big[:, 2048:6144], 4)
        v_tok = v3(big[:, 6144:10240], 4)
        qT = v3(big[:, 10240:12288], HEADS)
        kT = v3(big[:, 12288:16384], HEADS)
        hT = [v3(p_[:], KC) for p_ in h_parts]
        conT = [v3(p_[:], KC) for p_ in con_parts]
        ffT = [v3(p_[:], FC) for p_ in ff_parts]
        whole = v3(big[:, 0:2 * KC * SEQ], 2 * KC)
        mod_rows = v3(big[:, 11264:13312], 2)
        pool_m = v3(big[:, 13312:15360], TT * 4)
        pscale = big[:, 15360:16384]
        hx_tok = v3(big[:, 0:2048], TT)
        pooledT = v3(big[:, 2048:4096], KC)
        modring = [v3(aux[:, 4096 * i:4096 * i + 4096], KC) for i in range(MODS)]
        g1row, g2row = aux[:, 8192:9216], aux[:, 9216:10240]
        ln_rows = v3(aux[:, 10240:12288], 2)
        prob = prob_raw[:].rearrange("p (b m n) -> p b m n", b=AHEAD + 1, m=2)
        aT = v3(big[:, 0:1024], 2)
        z = v3(big[:, 0:TT * ZW], TT)
        ft = v3(big[:, TT * ZW:TT * ZW + 28 * SEQ], 28)
        oT2 = ft[:, 0:10, :]
        bias = v3(aux[:, 0:REL_HEADS * SEQ], REL_HEADS)
        kdup = aux[:, 7168:9728].rearrange("p (t b n) -> p t b n", t=TT, b=10)
        lbuf = v3(aux[:, 9216:12288], AHEAD + 1)
        score = [tmp[:, 0, 0:128], tmp[:, 0, 128:384]]
        work = [tmp[:, 1, 0:128], tmp[:, 1, 128:384]]
        selmask = [aux[:, 7168:7296], aux[:, 7296:7552]]
        pT = v3(aux[:, 7680:9216], 2)
        rel = v3(aux[:, 10240:10240 + 4 * SEQ], 4)
        o_c = v3(modacc_raw[:, 0:2 * SEQ], 2)
        xc = modacc_raw[:, 0:4 * 16 * N_CMP].rearrange("p (k l n) -> p k l n", k=4, l=16)
        cmp_k = srow[0:N_CMP, :]
        ckd = v3(cmp_k[:, 0:2 * P], 2)
        vcmp = v3(cmp_k[:, 2 * P:], 2)
        kcT = v3(sb("kcT", 2 * N_CMP)[:], 2)
        pcT = v3(table[0:N_CMP, P:P + 2 * P], 2)
        colsrc, possrc, oh_sb, rm_sb, rel_sb = (
            big[0:N_COLS, 0:P], big[0:32, 128:256], big[0:32, 256:640], big[0:REL_HEADS, 640:1024],
            big[0:32, 1024:1024 + REL_HEADS])
        lam_in = v3(big[:, 1100:1356], 4)

        psum = [ctx.enter_context(nc.psum_tensor(f"bank{i}", [P, NB], F32)) for i in range(8)]

        filled = [sem(f"bank_filled{i}") for i in range(8)]
        emptied = [sem(f"bank_emptied{i}") for i in range(8)]
        w_landed = [sem(f"w_landed{i}") for i in range(RING)]
        w_used = sem("w_used")
        w_hi, w_lo, w_pool, h_hi = sem("w_hi_by_act"), sem("w_lo_by_dve"), sem("w_split_by_pool"), sem("h_hi_done")
        pool_step = sem("pool_step")
        mod_landed = [sem(f"mod_landed{i}") for i in range(MODS)]
        mod_acc = sem("mod_acc")
        x_landed, ctx_landed, c_landed = sem("x_landed"), sem("ctx_landed"), sem("c_landed")
        table_landed, cols_landed, lam_landed = sem("table_landed"), sem("cols_landed"), sem("lam_landed")
        ln_landed, g_landed = sem("ln_landed"), {2: sem("g1_bias_landed"), 5: sem("g2_bias_landed")}
        lam_sum, lam_exp, gates_done, sig_done = sem("lam_sum"), sem("lam_exp"), sem("gates_done"), sem("sig_done")
        rows_landed, poolm_landed, psc_landed = sem("rows_landed"), sem("pool_m_landed"), sem("pscale_landed")
        srow_done, srow_stored, bias_landed = sem("srow_done"), sem("srow_stored"), sem("bias_landed")
        consts_done, csil_done = sem("consts_done"), sem("csil_done")
        dve_step = sem("dve_step")
        rope_done, x_done, g1_used, g2_used, ln_used = (
            sem("rope_done"), sem("x_done"), sem("g1_used"), sem("g2_used"), sem("ln_rows_used"))
        var_done, rstd_done = sem("var_done"), sem("rstd_done")
        nmax_done, exp_done, probs_done, o_done = (
            sem("nmax_done"), sem("exp_done"), sem("probs_done"), sem("o_done"))
        sq_done, hx_done, mix_done = sem("sq_done"), sem("hx_done"), sem("mix_done")
        xn_done, zsrc_done, xc_done, ckd_done = sem("xn_done"), sem("zsrc_done"), sem("xc_done"), sem("ckd_done")
        rel_done, rel_used, l_done, exp2_done, p_done = (
            sem("rel_done"), sem("rel_used"), sem("logits_done"), sem("exp2_done"), sem("p_done"))
        attn_done, out_stored = sem("attn_done"), sem("out_stored")

        block = ctx.enter_context(nc.Block())

        uses, where = [0] * 8, {}
        turn = {"gemm": 0, "misc": 0, "unit": 0, "mix": 0}
        POOLS = {"gemm": (0, 1, 2, 3, 4, 5), "misc": (6, 7), "unit": (0, 1, 2, 3, 4), "mix": (5,)}

        def result(eng, key):
            b, n = where[key]
            eng.wait_ge(filled[b], n)
            return psum[b]

        def empties(ins, key):
            ins.then_inc(emptied[where[key][0]], 1)

        def wait_emptied(eng, key):
            b, n = where[key]
            eng.wait_ge(emptied[b], n)

        def landings(i):
            return sum(len(panels[j][1]) for j in range(i % RING, i + 1, RING))

        by_pool = [key[0] == "mix" for key, *_ in panels]
        split_panels = [i for i, (key, *_) in enumerate(panels) if key[0] not in WHOLE]
        ordinal = {i: n for n, i in enumerate(split_panels)}
        shared_before = [sum(not by_pool[j] for j in split_panels if j <= i) for i in range(len(panels))]
        done = {}

        def raw_panel(i):
            _, _, chunks, width = panels[i]
            return ring[i % RING][:, 0:chunks * width].rearrange("p (c n) -> p c n", c=chunks)

        def panel_part(i, x):
            _, _, chunks, width = panels[i]
            buf = ring_lo[i % RING] if x else w_hi_buf[ordinal[i] % PARTS]
            return buf[:, 0:chunks * width].rearrange("p (c n) -> p c n", c=chunks)

        def wait_landed(eng, i):
            eng.wait_ge(w_landed[i % RING], 16 * landings(i))

        def wait_hi_free(eng, i):
            if ordinal[i] >= PARTS:
                eng.wait_ge(*done[split_panels[ordinal[i] - PARTS]])

        def wait_split(eng, i, hi_only=False):
            if not by_pool[i]:
                eng.wait_ge(w_hi, shared_before[i])
                if not hi_only:
                    eng.wait_ge(w_lo, shared_before[i])
            if not hi_only:
                eng.wait_ge(w_pool, ordinal[i] + 1)

        def splitter(one):
            nxt = [0]

            def split_to(i):
                while nxt[0] <= min(i, len(panels) - 1):
                    if nxt[0] in ordinal:
                        one(nxt[0])
                    nxt[0] += 1
            return split_to

        def last_panel(stage, nb):
            return max(i for i, (key, *_) in enumerate(panels) if key[:2] == (stage, nb))

        def mod_panel(eng, e):
            prev = e - MODS
            if prev >= FIRST_DVE_EVENT:
                eng.wait_ge(mod_acc, prev - FIRST_DVE_EVENT + 1)
            elif prev >= 0:
                result(eng, ("mod", prev))
            l, blk = divmod(e, 12)
            eng.dma_start(modring[e % MODS], a["w_mod"][l, :, blk * NB:(blk + 1) * NB]
                          .rearrange("(p j) n -> p j n", j=KC)).then_inc(mod_landed[e % MODS], 16)

        def mod_is_row(e):
            comp = (e % 12) // 2
            return comp in ((2, 5) if e < 12 else (0, 1, 2, 5))

        QKV_EVENTS = {0: [4], 1: [5], 2: [6, 7], 3: [8, 9], 4: [10, 11], 5: []}
        FFN_EVENTS = {"ffn0": {1: [12], 3: [13], 5: [14], 7: [15], 9: [16], 10: [17]},
                      "ffn1": {1: [22], 3: [23]}, "ffn2": {}}
        OUT_EVENTS = {"ffn0": {(0, 1): 18, (0, 4): 19, (1, 1): 20, (1, 4): 21}, "ffn1": {}, "ffn2": {}}
        event_panel = {e: last_panel("qkv", nb) for nb, es in QKV_EVENTS.items() for e in es}
        for name_, at in FFN_EVENTS.items():
            event_panel.update({e: last_panel(name_ + "_in", nb) for nb, es in at.items() for e in es})
            event_panel.update({e: panel_at[(name_ + "_out",) + k_] for k_, e in OUT_EVENTS[name_].items()})
        FIRST_DVE_EVENT, N_EVENTS = 4, 24
        UNITS0 = [(qt, h) for qt in range(TT) for h in range(HEADS)]
        UNITS2 = [("B", qt, h) for qt in range(TT) for h in range(8)] + \
                 [("C", qt, h) for qt in range(TT) for h in range(4)] + \
                 [("A", qt, h) for qt in range(TT) for h in range(8)]
        MIX_PIECES = 2 * 3 * TT * 2
        MIX_AT = {u: range(u * MIX_PIECES // len(UNITS2), (u + 1) * MIX_PIECES // len(UNITS2))
                  for u in range(len(UNITS2))}
        MIX_Z = [[(0, 0, 512)], [(964, 0, 512)], [(2268, 0, 512)], [(2780, 0, 512)], [(3292, 0, 512)],
                 [(1476, 0, 384), (640, 384, 128)]]
        FT_PAIRS = [(0, 2), (2, 2), (4, 1), (5, 2), (7, 1), (8, 2), (10, 2), (12, 2), (14, 2),
                    (16, 2), (18, 2), (20, 2), (22, 2), (24, 2), (26, 2)]
        FT_GAIN = {0: 0, 2: 0, 4: 1, 8: 2, 10: 2, 12: 3, 14: 3, 16: 4, 18: 4, 20: 4, 22: 5, 24: 5, 26: 5}
        FT_ON_ACT = {0, 4, 7, 10, 14, 18, 22, 26}

        def ft_source(b, tt):
            if b < 4:
                return z[:, tt, AQ + b * P:AQ + (b + 1) * P]
            if b in (5, 6):
                return z[:, tt, IQ + (b - 5) * P:IQ + (b - 4) * P]
            if 8 <= b < 12:
                return z[:, tt, BQ + (b - 8) * P:BQ + (b - 7) * P]
            if 16 <= b < 22:
                return z[:, tt, CQ + (b - 16) * P:CQ + (b - 15) * P]
            if b >= 22:
                return z[:, tt, CK + (b - 22) * P:CK + (b - 21) * P]
            return kdup[:, tt, {4: 0, 7: 1, 12: 2, 13: 3, 14: 4, 15: 5}[b], :]

        def unit_segments(kind, h):
            if kind == "A":
                return [(h // 2, 4, h, AV)]
            if kind == "B":
                g = h // 4
                return [(8 + h // 2, 12 + g, 8 + h, BVS + g * HD), (8 + h // 2, 14 + g, 8 + h, BVW + g * HD)]
            return [(16 + (4 * g + h) // 2, 22 + (4 * g + h) // 2, 16 + 4 * g + h, CV + (4 * g + h) * HD)
                    for g in range(3)]

        def o2_tok(kind, qt):
            return {"A": y_tok[:, qt, 0:512], "B": y_tok[:, qt, 512:1024], "C": o_c[:, qt, :]}[kind]

        @block.tensor
        def _(pe):
            released = [0]
            next_panel = [0]

            def take(key, pool="gemm"):
                b = POOLS[pool][turn[pool] % len(POOLS[pool])]
                turn[pool] += 1
                if uses[b]:
                    pe.wait_ge(emptied[b], uses[b])
                uses[b] += 1
                where[key] = (b, uses[b])
                return psum[b]

            def fills(ins, key):
                ins.then_inc(filled[where[key][0]], 1)

            def panel(key):
                i = panel_at[key]
                assert i == next_panel[0], key
                next_panel[0] += 1
                if i not in ordinal:
                    wait_landed(pe, i)
                    return [raw_panel(i)]
                wait_split(pe, i)
                return [panel_part(i, 0), panel_part(i, 1)]

            def mm(o, l, r, start, stop, **kw):
                return nc.tensor.matmul(o, l, r, start=start, stop=stop, **kw)

            def product(o, ls, rs_, start, stop, **kw):
                pairs = [(0, 0)] if len(ls) == 1 else [(0, 0), (0, 1), (1, 0)]
                for n, (x, y) in enumerate(pairs):
                    ins = mm(o, ls[x], rs_[y], start and n == 0, stop and n == len(pairs) - 1, **kw)
                return ins

            def release(key, ins, filled_key=None):
                if filled_key is None:
                    ins.then_inc(w_used, 1)
                    released[0] += 1
                    done[panel_at[key]] = (w_used, released[0])
                else:
                    b, n = where[filled_key]
                    done[panel_at[key]] = (filled[b], n)

            def gemm(stage, lhs, tts, nb, width, groups, events={}):
                banks = {tt: take((stage, nb, tt)) for tt in tts}
                last = groups[-1][1] - 1
                for kg, (lo, hi) in enumerate(groups):
                    w = panel((stage, nb, kg))
                    for tt in tts:
                        for c in range(lo, hi):
                            ins = product(banks[tt][:, 0:width], lhs(tt, c), [x[:, c - lo, :] for x in w],
                                          c == 0, c == last)
                        if hi - 1 == last:
                            fills(ins, (stage, nb, tt))
                    release((stage, nb, kg), ins, (stage, nb, tts[-1]) if hi - 1 == last else None)
                    if (nb, kg) in events:
                        mod_reduce(events[(nb, kg)])

            HALVES = [(0, 4), (4, 8)]

            def transposes(key, sources, pool="gemm"):
                bank = take(key, pool)
                for i, src in enumerate(sources):
                    ins = nc.tensor.transpose(bank[0:src.shape[1], i * P:i * P + src.shape[0]], src,
                                              ident[0:src.shape[0], 0:src.shape[0]])
                fills(ins, key)

            def mod_reduce(e):
                pe.wait_ge(mod_acc, e - FIRST_DVE_EVENT + 1)
                acc = modacc[:, e % MODS, :]
                bank = take(("mod", e), "misc")
                if mod_is_row(e):
                    ins = mm(bank[:, :], ones[:, :], acc, True, True)
                else:
                    for j in range(4):
                        ins = mm(bank[:, j:j + 1], acc[:, j * P:(j + 1) * P], ones[:, 0:1], True, True)
                fills(ins, ("mod", e))

            def x_transposes(stage, tok, ready, version):
                for ch in range(KC):
                    if ch == 0:
                        pe.wait_ge(ready, version)
                    transposes((stage, ch), [tok[:, tt, ch * P:(ch + 1) * P] for tt in range(TT)])

            def token_tile(x, c, tt):
                return [x_[:, c, tt * P:(tt + 1) * P] for x_ in x]

            def ffn(name):
                wait_emptied(pe, (name + "_h", KC - 1))
                for nb in range(FNB):
                    banks = [take((name, "g", nb)), take((name, "u", nb))]
                    for kg in range(2):
                        w = panel((name + "_in", nb, kg))
                        for half in range(2):
                            for s in range(2):
                                for c in range(PK):
                                    lo = half * 256 + s * P
                                    ins = product(banks[half][:, s * 256:s * 256 + 256],
                                                  [x[:, c, lo:lo + P] for x in w],
                                                  [x[:, kg * PK + c, :] for x in hT], kg == 0 and c == 0 and s == 0,
                                                  kg == 1 and c == PK - 1, skip_group_check=True)
                            if kg == 1:
                                fills(ins, (name, "gu"[half], nb))
                        release((name + "_in", nb, kg), ins, (name, "u", nb) if kg == 1 else None)
                    for e in FFN_EVENTS[name].get(nb, []):
                        mod_reduce(e)
                wait_emptied(pe, (name, "u", FNB - 1))
                groups = [(k, min(k + PK, FC)) for k in range(0, FC, PK)]
                for nb in range(2):
                    gemm(name + "_out", lambda tt, c: token_tile(ffT, c, tt), range(TT), nb, NB, groups, OUT_EVENTS[name])

            pe.wait_ge(table_landed, 16)
            pe.wait_ge(cols_landed, 16 * 10)
            transposes("cols", [colsrc])
            transposes("pos", [possrc])
            fills(mm(take("srow")[0:REL_HEADS, 0:SROW], rel_sb, oh_sb, True, True), "srow")

            pe.wait_ge(csil_done, 1)
            for e in range(FIRST_DVE_EVENT):
                pe.wait_ge(mod_landed[e % MODS], 16 * (e // MODS + 1))
                bank = take(("mod", e), "misc")
                for s in range(4):
                    for j in range(KC):
                        ins = mm(bank[:, 2 * s:2 * s + 2], modring[e % MODS][:, j, s * P:(s + 1) * P],
                                 cs[:, 2 * j:2 * j + 2], j == 0, j == KC - 1)
                fills(ins, ("mod", e))

            pe.wait_ge(x_landed, 16)
            pe.wait_ge(ctx_landed, 16)
            for ch in range(KC):
                transposes(("lat", ch), [x_tok[:, tt, ch * P:(ch + 1) * P] for tt in range(TT)])
                transposes(("con", ch), [y_tok[:, tt, ch * P:(ch + 1) * P] for tt in range(TT)])

            wait_emptied(pe, ("lat", KC - 1))
            wait_emptied(pe, ("con", KC - 1))
            for nb in range(6):
                gemm("qkv", lambda tt, c: token_tile(conT if tt >= TT else hT, c, tt % TT), range(2 if nb < 2 else 4),
                     nb, NB, HALVES)
                for e in QKV_EVENTS[nb]:
                    mod_reduce(e)

            for h in range(HEADS):
                pe.wait_ge(rope_done, 6 if h < 4 else 8)
                for tt in (2, 3):
                    wait_emptied(pe, ("qkv", 2 + h // 4, tt))
                transposes(("qT", h), [q_tok[:, tt, h * P:(h + 1) * P] for tt in range(TT)])
                transposes(("kT", h), [k_tok[:, tt, h * P:(h + 1) * P] for tt in range(4)])
            for tt in range(4):
                wait_emptied(pe, ("qkv", 5, tt))

            def scores(u):
                qt, h = UNITS0[u]
                wait_emptied(pe, ("qT", h))
                wait_emptied(pe, ("kT", h))
                for m in range(2):
                    rows = slice(m * HD, (m + 1) * HD)
                    fills(mm(take(("S", u, m))[:, :], qT[rows, h, qt * P:(qt + 1) * P], kT[rows, h, :],
                             True, True), ("S", u, m))

            def turn_probs(u):
                pe.wait_ge(probs_done, u + 1)
                transposes(("PT", u), [prob[:, u % 4, 0, kb * P:(kb + 1) * P] for kb in range(4)])

            def values(u):
                qt, h = UNITS0[u]
                if u % 4 == 0:
                    take(("O", u // 4), "misc")
                o = psum[where[("O", u // 4)][0]]
                wait_emptied(pe, ("PT", u))
                for kb in range(4):
                    ins = mm(o[:, (u % 4) * P:(u % 4 + 1) * P], aT[:, u % 2, kb * P:(kb + 1) * P],
                             v_tok[:, kb, h * P:(h + 1) * P], kb == 0, kb == 3)
                if u % 4 == 3:
                    fills(ins, ("O", u // 4))

            for u in range(AHEAD):
                scores(u)
            for u in range(len(UNITS0)):
                turn_probs(u)
                if u + AHEAD < len(UNITS0):
                    scores(u + AHEAD)
                values(u)

            pe.wait_ge(o_done, 4)
            for h in range(HEADS):
                transposes(("oT", h), [y_tok[:, tt, h * P:(h + 1) * P] for tt in range(TT)])
            wait_emptied(pe, ("oT", HEADS - 1))
            for nb in range(2):
                gemm("wo", lambda tt, c: token_tile(hT, c, tt), range(TT), nb, NB, HALVES)
            x_transposes("ffn0_h", x_tok, x_done, 2)
            ffn("ffn0")

            pe.wait_ge(hx_done, 2)
            pe.wait_ge(poolm_landed, 16)
            for ch in range(KC):
                bank = take(("pl", ch))
                for kt in range(TT):
                    ins = mm(bank[:, 0:SEQ], hx_tok[:, kt, ch * P:(ch + 1) * P],
                             pool_m[:, kt * 4 + ch // 2, :], kt == 0, kt == TT - 1)
                fills(ins, ("pl", ch))
            wait_emptied(pe, ("pl", KC - 1))
            w, = panel(("pool", 0, 0))
            for nb in range(2):
                for tt in range(TT):
                    bank = take(("poolw", nb, tt))
                    for g in (2 * nb, 2 * nb + 1):
                        for c in range(2):
                            ins = mm(bank[:, (g % 2) * 256:(g % 2) * 256 + 256],
                                     pooledT[:, 2 * g + c, tt * P:(tt + 1) * P], w[:, 2 * g + c, :],
                                     c == 0, c == 1)
                    fills(ins, ("poolw", nb, tt))
            release(("pool", 0, 0), ins, ("poolw", 1, TT - 1))
            x_transposes("ffn1_h", x_tok, x_done, 6)
            ffn("ffn1")

            x_transposes("z_h", y_tok, xn_done, 2)
            wait_emptied(pe, ("z_h", KC - 1))
            for nb, (lo, hi) in enumerate(Z_BLOCKS):
                gemm("z", lambda tt, c: token_tile(hT, c, tt), range(TT), nb, hi - lo, HALVES)

            pe.wait_ge(zsrc_done, 1)
            for tt in range(TT):
                wait_emptied(pe, ("z", len(Z_BLOCKS) - 1, tt))
            for i in range(4):
                transposes(("dupT", i), [kdup[:, tt, 6 + i, :] for tt in range(TT)])
            for b0, n in FT_PAIRS:
                transposes(("ft", b0), [ft_source(b0 + j, tt) for j in range(n) for tt in range(TT)])

            w, = panel(("cmp", 0, 0))
            pe.wait_ge(xc_done, 1)
            bank = take("cmp")
            for i in range(4):
                kv = i // 2
                for l in range(16):
                    ins = mm(bank[0:N_CMP, i * HD:(i + 1) * HD], xc[:, i, l, :], w[:, kv * 16 + l, :], l == 0, l == 15)
            fills(ins, "cmp")
            release(("cmp", 0, 0), ins, "cmp")
            pe.wait_ge(ckd_done, 1)
            transposes("kcT", [ckd[:, 0, :], ckd[:, 1, :]])
            for b0, _ in FT_PAIRS[-2:]:
                wait_emptied(pe, ("ft", b0))

            for qt in range(TT):
                nk = (qt + 1) * P
                for j in range(2):
                    rows = slice(j * HD, (j + 1) * HD)
                    bank = take(("I", qt, j))
                    for pr in range(2):
                        ins = mm(bank[:, pr * 256:pr * 256 + nk], ft[rows, 5 + pr, qt * P:(qt + 1) * P],
                                 ft[rows, 7, 0:nk], True, True)
                    fills(ins, ("I", qt, j))

            def scores2(u):
                kind, qt, h = UNITS2[u]
                nk = (qt + 1) * P
                rows = slice((h % 2) * HD, (h % 2 + 1) * HD)
                segs = unit_segments(kind, h)
                for s, (qb, kb, _, _) in enumerate(segs):
                    if s % 2 == 0:
                        bank = take(("S2", u, s // 2), "unit")
                    ins = mm(bank[:, (s % 2) * 256:(s % 2) * 256 + nk], ft[rows, qb, qt * P:(qt + 1) * P],
                             ft[rows, kb, 0:nk], True, True)
                    if s % 2 == 1 or s == len(segs) - 1:
                        fills(ins, ("S2", u, s // 2))
                if kind == "B":
                    fills(mm(take(("S2", u, "c"), "unit")[:, 0:N_CMP], ft[rows, segs[0][0], qt * P:(qt + 1) * P],
                             kcT[rows, h // 4, :], True, True), ("S2", u, "c"))

            def turn_probs2(u):
                kind, qt, h = UNITS2[u]
                nblk = (qt + 1) * len(unit_segments(kind, h))
                pe.wait_ge(p_done, u + 1)
                p = lbuf[:, u % 4, :]
                for i in range(0, nblk, 4):
                    transposes(("PT2", u, i // 4), [p[:, b * P:(b + 1) * P] for b in range(i, min(i + 4, nblk))],
                               "unit")
                if kind == "B":
                    transposes(("PT2", u, "c"), [p[:, nblk * P:nblk * P + N_CMP]], "unit")

            def values2(u):
                kind, qt, h = UNITS2[u]
                segs = unit_segments(kind, h)
                nkb = qt + 1
                nblk = nkb * len(segs)
                group = (kind, qt)
                if h == 0:
                    take(("O2",) + group, "misc")
                o = psum[where[("O2",) + group][0]][:, h * HD:(h + 1) * HD]
                for i in range(0, nblk, 4):
                    wait_emptied(pe, ("PT2", u, i // 4))
                last = nblk - 1 if kind != "B" else nblk
                for b in range(nblk):
                    v = z[:, b % nkb, segs[b // nkb][3]:segs[b // nkb][3] + HD]
                    ins = mm(o, pT[:, u % 2, b * P:(b + 1) * P], v, b == 0, b == last)
                if kind == "B":
                    wait_emptied(pe, ("PT2", u, "c"))
                    ins = mm(o, pcT[:, u % 2, :], vcmp[:, h // 4, :], False, True)
                if h == (3 if kind == "C" else 7):
                    fills(ins, ("O2",) + group)

            mix_w = {}

            def mix_piece(i):
                b, tt, kg = i // 4, i % 4 // 2, i % 2
                if tt == 0:
                    mix_w[kg] = panel(("mix", b, kg))
                if kg == 0:
                    take(("mix", b, tt), "mix")
                bank = psum[where[("mix", b, tt)][0]]
                for c in range(PK):
                    ins = product(bank[:, :], token_tile(hT, kg * PK + c, tt), [x[:, c, :] for x in mix_w[kg]],
                                  kg == 0 and c == 0, kg == 1 and c == PK - 1)
                if kg == 1:
                    fills(ins, ("mix", b, tt))
                if tt == TT - 1:
                    release(("mix", b, kg), ins, ("mix", b, tt) if kg == 1 else None)

            for u in range(AHEAD):
                scores2(u)
            for u in range(len(UNITS2)):
                turn_probs2(u)
                if u + AHEAD < len(UNITS2):
                    scores2(u + AHEAD)
                for i in MIX_AT[u]:
                    mix_piece(i)
                values2(u)

            for kind, n in (("A", 4), ("B", 4), ("C", 2)):
                for qt in range(TT):
                    wait_emptied(pe, ("O2", kind, qt))
                for i in range(n):
                    transposes(("oT2", kind, i), [o2_tok(kind, qt)[:, i * P:(i + 1) * P] for qt in range(TT)])
            wait_emptied(pe, ("oT2", "C", 1))
            for nb in range(2):
                for br in range(3):
                    n = 2 if br == 2 else 4
                    gemm(f"branch{br}", lambda tt, c: token_tile([oT2], 4 * br + c, tt), range(TT), nb, NB,
                         [(0, n)])
            x_transposes("mixed", y_tok, mix_done, 1)
            wait_emptied(pe, ("mixed", KC - 1))
            for nb in range(2):
                gemm("w_out", lambda tt, c: token_tile(hT, c, tt), range(TT), nb, NB, HALVES)
            x_transposes("ffn2_h", y_tok, xn_done, 4)
            ffn("ffn2")
            assert next_panel[0] == len(panels)

        @block.scalar
        def _(act):
            def split_hi(i):
                if not by_pool[i]:
                    wait_hi_free(act, i)
                    wait_landed(act, i)
                    nc.scalar.activation(panel_part(i, 0), raw_panel(i), ACT.Copy).then_inc(w_hi, 1)

            split_to = splitter(split_hi)

            def highs(stage, dst, func, kw=lambda ch: {}, chunks=range(KC)):
                for ch in chunks:
                    nc.scalar.activation(dst[:, ch, :], result(act, (stage, ch))[:, 0:SEQ], func, **kw(ch))\
                        .then_inc(h_hi, 1)

            def shifted(shift, scale):
                return lambda ch: dict(bias=modcol[:, shift, ch:ch + 1], scale=modcol[:, scale, ch:ch + 1])

            def row_load(dst, src, sem_):
                act.dma_start(dst, src.partition_broadcast(P)).then_inc(sem_, 16)

            def bias_row(dst, l, comp, sem_):
                row_load(dst, a["b_mod"][l, comp * D:(comp + 1) * D], sem_)

            def ln_load(n):
                act.wait_ge(ln_used, n)
                for i, w in enumerate(("ln_g", "ln_b")):
                    row_load(ln_rows[:, i, :], a[w][n // 2, n % 2, :], ln_landed)

            act.dma_start(cs_in[:, 0, :], a["c"].rearrange("a (p j) -> p (a j)", p=P)).then_inc(c_landed, 16)
            act.dma_start(cs_in[:, 1, :], a["c_ctx"].rearrange("(p j) -> p j", p=P)).then_inc(c_landed, 16)
            act.wait_ge(c_landed, 32)
            nc.scalar.activation(cs[:, :].rearrange("p (j c) -> p c j", c=2), cs_in, ACT.Silu).then_inc(csil_done, 1)
            act.wait_ge(lam_sum, 1)
            nc.scalar.activation(lam[:, 2:4], lam[:, 0:2], ACT.Exp).then_inc(lam_exp, 1)

            for ch in range(KC):
                if ch == 0:
                    for e in range(4):
                        wait_emptied(act, ("mod", e))
                highs("lat", hT[0], ACT.Identity, shifted(0, 1), [ch])
                highs("con", conT[0], ACT.Identity, shifted(2, 3), [ch])
            split_to(1)

            for nb in range(6):
                split_to(last_panel("qkv", nb) + 2)
                for tt in range(2 if nb < 2 else 4):
                    dst = (q_tok, k_tok, v_tok)[nb // 2][:, tt, (nb % 2) * NB:(nb % 2) * NB + NB]
                    empties(nc.scalar.activation(dst, result(act, ("qkv", nb, tt))[:, :], ACT.Copy),
                            ("qkv", nb, tt))
            for h in range(HEADS):
                empties(nc.scalar.activation(kT[:, h, :], result(act, ("kT", h))[:, :], ACT.Copy), ("kT", h))

            act.wait_ge(srow_done, 1)
            act.dma_start(scratch, srow[:, :].unsqueeze(1).broadcast_to([REL_HEADS, P, SROW])).then_inc(srow_stored, 16)
            def exps(u):
                act.wait_ge(nmax_done, u + 1)
                if u > AHEAD:
                    b, n = where[("PT", u - AHEAD - 1)]
                    act.wait_ge(filled[b], n)
                for m in range(2):
                    ins = nc.scalar.activation(prob[:, u % 4, m, :], result(act, ("S", u, m))[:, :], ACT.Exp,
                                               bias=small[:, 8 * (u % 4) + m:8 * (u % 4) + m + 1], scale=HD ** -0.5,
                                               accum_out=small[:, 8 * (u % 4) + 2 + m:8 * (u % 4) + 3 + m])
                    empties(ins, ("S", u, m))

            for u in range(AHEAD):
                exps(u)
            for u in range(len(UNITS0)):
                bank = result(act, ("PT", u))
                empties(nc.scalar.activation(aT[:, u % 2, :], bank[:, :], ACT.Copy), ("PT", u))
                if u + AHEAD < len(UNITS0):
                    exps(u + AHEAD)
                if u % 4 == 3:
                    b = result(act, ("O", u // 4))
                    if u // 4:
                        act.wait_ge(o_done, u // 4)
                    nc.scalar.activation(tmp[:, 0, :], b[:, :], ACT.Square).then_inc(sq_done, 1)
            highs("oT", hT[0], ACT.Copy, lambda ch: dict(scale=cols[:, COL_SUB:COL_SUB + 1]))
            for comp in range(2):
                bias_row(mod_rows[:, comp, :], 1, comp, rows_landed)
            act.dma_start(pool_m, a["const_pool"].rearrange("p (a b) -> p a b", a=TT * 4)).then_inc(poolm_landed, 16)
            row_load(pscale, a["pool_scale"][0], psc_landed)
            split_to(last_panel("wo", 1) + 2)

            def gain(col):
                return lambda ch: dict(scale=cols[:, col + ch:col + ch + 1])

            def ffn(name):
                for nb in range(FNB):
                    split_to(last_panel(name + "_in", nb) + 2)
                    if name == "ffn0" and nb == 2:
                        act.wait_ge(g1_used, 1)
                        bias_row(g1row, 1, 2, g_landed[2])
                        ln_load(1)
                    if name == "ffn1" and nb == 2:
                        ln_load(3)
                    bank = result(act, (name, "g", nb))
                    if nb >= 2:
                        wait_emptied(act, (name, "u", nb - 2))
                    empties(nc.scalar.activation(tmp[:, nb % 2, :], bank[:, :], ACT.Silu), (name, "g", nb))
                split_to(last_panel(name + "_out", 1) + 2)

            highs("ffn0_h", hT[0], ACT.Identity, shifted(4, 5))
            ffn("ffn0")
            for ch in range(KC):
                empties(nc.scalar.activation(pooledT[:, ch, :], result(act, ("pl", ch))[:, 0:SEQ], ACT.Copy),
                        ("pl", ch))
            act.wait_ge(g2_used, 1)
            bias_row(g2row, 1, 5, g_landed[5])
            ln_load(2)
            split_to(last_panel("pool", 0) + 2)
            highs("ffn1_h", hT[0], ACT.Identity, shifted(6, 7))
            ffn("ffn1")

            highs("z_h", hT[0], ACT.Copy, gain(COL_N1))
            for nb, (lo, hi) in enumerate(Z_BLOCKS):
                split_to(last_panel("z", nb) + 2)
                for tt in range(TT):
                    empties(nc.scalar.activation(z[:, tt, lo:hi], result(act, ("z", nb, tt))[:, 0:hi - lo], ACT.Copy),
                            ("z", nb, tt))
                if nb == 4:
                    for tt in range(TT):
                        wait_emptied(act, ("z", 4, tt))
                        g = v3(z[:, tt, BG:BG + 24], 8)
                        nc.scalar.activation(gates[:, tt, :, 0:2], g[:, :, 1:3], ACT.Sigmoid).then_inc(gates_done, 1)
                        nc.scalar.activation(gates[:, tt, :, 2:3], g[:, :, 0:1], ACT.Sigmoid).then_inc(gates_done, 1)
            for b0, n in FT_PAIRS:
                if b0 in FT_ON_ACT:
                    src = v3(result(act, ("ft", b0))[:, 0:n * SEQ], n)
                    if b0 in FT_GAIN:
                        g = COL_QK + FT_GAIN[b0]
                        ins = nc.scalar.activation(ft[:, b0:b0 + n, :], src, ACT.Copy, scale=cols[:, g:g + 1])
                    else:
                        ins = nc.scalar.activation(ft[:, b0:b0 + n, :], src, ACT.Copy)
                    empties(ins, ("ft", b0))

            for qt in range(TT):
                nk = (qt + 1) * P
                for j in range(2):
                    bank = result(act, ("I", qt, j))
                    if j == 0 and qt > 0:
                        act.wait_ge(rel_used, qt)
                    ins = nc.scalar.activation(rel[:, j:4:2, 0:nk], v3(bank[:, :], 2)[:, :, 0:nk], ACT.Relu)
                    empties(ins, ("I", qt, j))

            def exps2(u):
                kind, qt, h = UNITS2[u]
                nk = (qt + 1) * P
                act.wait_ge(l_done, u + 1)
                o = 64 + 16 * (u % 4)
                parts = [(0, nk), (nk, 2 * nk), (2 * nk, 2 * nk + N_CMP)] if kind == "B" else \
                        [(0, nk * (3 if kind == "C" else 1))]
                for i, (lo, hi) in enumerate(parts):
                    ins = nc.scalar.activation(lbuf[:, u % 4, lo:hi], lbuf[:, u % 4, lo:hi], ACT.Exp,
                                               bias=small[:, o + i:o + i + 1],
                                               accum_out=small[:, o + 4 + i:o + 5 + i])
                ins.then_inc(exp2_done, 1)

            for u in range(AHEAD):
                exps2(u)
            for u, (kind, qt, h) in enumerate(UNITS2):
                nblk = (qt + 1) * len(unit_segments(kind, h))
                for i in range(0, nblk, 4):
                    n = min(4, nblk - i)
                    empties(nc.scalar.activation(pT[:, u % 2, i * P:(i + n) * P],
                                                 result(act, ("PT2", u, i // 4))[:, 0:n * P], ACT.Copy),
                            ("PT2", u, i // 4))
                if kind == "B":
                    empties(nc.scalar.activation(pcT[:, u % 2, :], result(act, ("PT2", u, "c"))[0:N_CMP, 0:P], ACT.Copy),
                            ("PT2", u, "c"))
                if u + AHEAD < len(UNITS2):
                    exps2(u + AHEAD)
                for i in MIX_AT[u]:
                    if i % 2 == 1:
                        b, tt = i // 4, i % 4 // 2
                        bank = result(act, ("mix", b, tt))
                        for k, (zc, lo, n) in enumerate(MIX_Z[b]):
                            ins = nc.scalar.activation(z[:, tt, zc:zc + n], bank[:, lo:lo + n], ACT.Copy)
                        empties(ins, ("mix", b, tt))
            for kind, n in (("A", 4), ("B", 4), ("C", 2)):
                for i in range(n):
                    empties(nc.scalar.activation(oT2[:, {"A": 0, "B": 4, "C": 8}[kind] + i, :],
                                                 result(act, ("oT2", kind, i))[:, 0:SEQ], ACT.Copy), ("oT2", kind, i))
            i = 0
            for nb in range(2):
                for br in range(3):
                    for tt in range(TT):
                        wait_emptied(act, ("mix", nb * 3 + br, tt))
                        if i >= 2:
                            n2, b2 = divmod(i - 2, 6)
                            wait_emptied(act, (f"branch{b2 // 2}", n2, b2 % 2))
                        for zc, lo, n in MIX_Z[nb * 3 + br]:
                            ins = nc.scalar.activation(tmp[:, i % 2, lo:lo + n], z[:, tt, zc:zc + n], ACT.Sigmoid)
                        ins.then_inc(sig_done, 1)
                        i += 1
            split_to(last_panel("branch2", 1) + 2)
            highs("mixed", hT[0], ACT.Copy)
            split_to(last_panel("w_out", 1) + 2)
            highs("ffn2_h", hT[0], ACT.Copy, gain(COL_N2))
            ffn("ffn2")

        @block.vector
        def _(dve):
            steps = [0]
            V = nc.vector

            def step(ins):
                ins.then_inc(dve_step, 1)
                steps[0] += 1

            def settle():
                dve.wait_ge(dve_step, steps[0])

            def half_lo(i):
                if not by_pool[i]:
                    half = slice(0, panels[i][2] // 2)
                    wait_split(dve, i, hi_only=True)
                    V.tensor_tensor(panel_part(i, 1)[:, half, :], raw_panel(i)[:, half, :],
                                    panel_part(i, 0)[:, half, :].bitcast(F32), ALU.subtract).then_inc(w_lo, 1)

            split_to = splitter(half_lo)
            highs = [0]

            def lows(stage, dst, shift=None, scale=None, chunks=range(KC), at=0):
                for ch in chunks:
                    bank = result(dve, (stage, ch))
                    highs[0] += 1
                    dve.wait_ge(h_hi, highs[0])
                    if shift is not None:
                        full = whole[:, at + ch, :]
                        step(V.tensor_scalar(full, bank[:, 0:SEQ], scale(ch), shift(ch), ALU.mult, ALU.add))
                        settle()
                    hi = dst[0][:, ch, :].bitcast(F32)
                    if shift is not None:
                        ins = V.tensor_tensor(dst[1][:, ch, :], full, hi, ALU.subtract)
                    elif scale is not None:
                        ins = V.scalar_tensor_tensor(dst[1][:, ch, :], bank[:, 0:SEQ], scale(ch), hi,
                                                     ALU.mult, ALU.subtract)
                    else:
                        ins = V.tensor_tensor(dst[1][:, ch, :], bank[:, 0:SEQ], hi, ALU.subtract)
                    empties(ins, (stage, ch))

            def mod_col(slot):
                return lambda ch: modcol[:, slot, ch:ch + 1]

            def gain(col):
                return lambda ch: cols[:, col + ch:col + ch + 1]

            step(V.memset(ones[:, :], 1.0))
            V.memset(neghalf[:, :], -0.5).then_inc(consts_done, 1)
            bank = result(dve, "cols")
            empties(V.tensor_copy(cols[:, :], bank[:, 0:N_COLS]), "cols")
            wait_emptied(dve, "cols")
            step(V.tensor_scalar(cols[:, COL_SUB:COL_SUB + 1], cols[:, COL_SUB:COL_SUB + 1], 1.0 - LAM_INIT, None,
                                 ALU.mult))
            empties(V.tensor_copy(posT[:, :], result(dve, "pos")[:, 0:32]), "pos")
            bank = result(dve, "srow")
            empties(V.tensor_tensor(srow[:, :], bank[0:REL_HEADS, 0:SROW], rm_sb, ALU.add), "srow")
            wait_emptied(dve, "srow")
            V.memset(lam[:, 7:8], 0.0).then_inc(srow_done, 1)

            dve.wait_ge(lam_landed, 16)
            lp = small[:, 128:256]
            step(V.tensor_tensor(v3(lp, 2), lam_in[:, 0:4:2, :], lam_in[:, 1:4:2, :], ALU.mult))
            settle()
            V.tensor_reduce(lam[:, 0:2], v3(lp, 2), AX, ALU.add).then_inc(lam_sum, 1)
            dve.wait_ge(lam_exp, 1)
            step(V.tensor_tensor(lam[:, 4:5], lam[:, 3:4], lam[:, 2:3], ALU.subtract))
            settle()
            step(V.tensor_scalar(lam[:, 5:6], lam[:, 4:5], -LAM_INIT, None, ALU.add))

            for e in range(4):
                comp, half = divmod(e, 2)
                src = result(dve, ("mod", e))[:, 0:8].rearrange("p (s c) -> p c s", c=2)
                bcol = cols[:, COL_BMOD + comp * KC + half * 4:COL_BMOD + comp * KC + half * 4 + 4]
                step(V.scalar_tensor_tensor(modcol[:, comp, half * 4:half * 4 + 4], src[:, 0, :], float(comp),
                                            bcol, ALU.add, ALU.add))
                empties(V.scalar_tensor_tensor(modcol[:, 2 + comp, half * 4:half * 4 + 4], src[:, 1, :],
                                               float(comp), bcol, ALU.add, ALU.add), ("mod", e))
            wait_emptied(dve, ("mod", 2))
            wait_emptied(dve, ("mod", 3))
            for ch in range(KC):
                lows("lat", hT, mod_col(0), mod_col(1), [ch])
                lows("con", conT, mod_col(2), mod_col(3), [ch], KC)
            split_to(1)

            def mod_product(e):
                if e >= N_EVENTS:
                    return
                dve.wait_ge(mod_landed[e % MODS], 16 * (e // MODS + 1))
                if e - MODS >= FIRST_DVE_EVENT:
                    result(dve, ("mod", e - MODS))
                acc = modacc[:, e % MODS, :]
                w = modring[e % MODS]
                for j in range(KC):
                    c = cs[:, 2 * j:2 * j + 1]
                    if j == 0:
                        ins = V.tensor_scalar(acc, w[:, j, :], c, None, ALU.mult)
                    else:
                        settle()
                        ins = V.scalar_tensor_tensor(acc, w[:, j, :], c, acc, ALU.mult, ALU.add)
                    if j < KC - 1:
                        step(ins)
                ins.then_inc(mod_acc, 1)

            def mod_finish(e):
                comp, half = divmod(e % 12, 2)
                cols_ = slice(half * NB, half * NB + NB)
                bank = result(dve, ("mod", e))
                if mod_is_row(e):
                    if comp in (0, 1):
                        dst = mod_rows[:, comp, cols_]
                        dve.wait_ge(rows_landed, 32)
                    else:
                        dst = (g1row if comp == 2 else g2row)[:, cols_]
                        dve.wait_ge(g_landed[comp], 16 * (e // 12 + 1))
                    ins = V.scalar_tensor_tensor(dst, bank[:, :], 1.0 if comp == 1 else 0.0, dst, ALU.add, ALU.add)
                else:
                    slot = (4 if e < 12 else 6) + comp - 3
                    b0 = COL_BMOD + (e // 12) * 48 + comp * KC + half * 4
                    ins = V.scalar_tensor_tensor(modcol[:, slot, half * 4:half * 4 + 4], bank[:, 0:4],
                                                 1.0 if comp == 4 else 0.0, cols[:, b0:b0 + 4], ALU.add, ALU.add)
                empties(ins, ("mod", e))

            dve.wait_ge(csil_done, 1)
            mod_product(4)
            mod_product(5)
            for nb in range(6):
                split_to(last_panel("qkv", nb) + 2)
                if nb < 4:
                    for tt in range(TT):
                        buf = (q_tok if nb < 2 else k_tok)[:, tt, (nb % 2) * NB:(nb % 2) * NB + NB]
                        wait_emptied(dve, ("qkv", nb, tt))
                        pairs = buf.rearrange("p (h s d) -> p h s d", s=2, d=HD // 2)
                        t0 = tmp[:, 0, :].rearrange("p (h n) -> p h n", n=HD)
                        t1 = tmp[:, 1, :].rearrange("p (h s d) -> p h s d", s=2, d=HD // 2)
                        cos2 = rope[:, 2 * tt, :].unsqueeze(1).broadcast_to([P, 8, HD])
                        sin2 = rope[:, 2 * tt + 1, :]
                        settle()
                        step(V.tensor_tensor(t0, buf.rearrange("p (h n) -> p h n", n=HD), cos2, ALU.mult))
                        for s in range(2):
                            sn = sin2[:, s * 32:(s + 1) * 32].unsqueeze(1).broadcast_to([P, 8, 32])
                            step(V.tensor_tensor(t1[:, :, s, :], pairs[:, :, 1 - s, :], sn, ALU.mult))
                        settle()
                        V.tensor_tensor(buf, tmp[:, 0, :], tmp[:, 1, :], ALU.add).then_inc(rope_done, 1)
                        dve.wait_ge(rope_done, 2 * nb + tt + 1)
                for e in QKV_EVENTS[nb]:
                    mod_finish(e)
                    mod_product(e + 2)
            for h in range(HEADS):
                empties(V.tensor_copy(qT[:, h, :], result(dve, ("qT", h))[:, 0:SEQ]), ("qT", h))

            def maxima(u):
                s = 8 * (u % 4)
                for m in range(2):
                    step(V.tensor_reduce(small[:, s + 4 + m:s + 5 + m], result(dve, ("S", u, m))[:, :], AX, ALU.max))
                settle()
                V.tensor_scalar(small[:, s:s + 2], small[:, s + 4:s + 6], -HD ** -0.5, None, ALU.mult)\
                    .then_inc(nmax_done, 1)

            def combine(u):
                s = 8 * (u % 4)
                wait_emptied(dve, ("S", u, 0))
                wait_emptied(dve, ("S", u, 1))
                step(V.reciprocal(small[:, s + 6:s + 8], small[:, s + 2:s + 4]))
                settle()
                step(V.tensor_scalar(small[:, 44:45], small[:, s + 7:s + 8], lam[:, 5:6], None, ALU.mult))
                settle()
                p0, p1 = prob[:, u % 4, 0, :], prob[:, u % 4, 1, :]
                step(V.tensor_scalar(p1, p1, small[:, 44:45], None, ALU.mult))
                settle()
                V.scalar_tensor_tensor(p0, p0, small[:, s + 6:s + 7], p1, ALU.mult, ALU.add).then_inc(probs_done, 1)

            rstds = [0]

            def inverse_root(var, n):
                rstds[0] += 1
                dve.wait_ge(rstd_done, rstds[0])
                return small[:, 32:32 + n]

            def head_var(g):
                dve.wait_ge(sq_done, g + 1)
                step(V.tensor_reduce(small[:, 36:40], v3(tmp[:, 0, :], 4), AX, ALU.add))
                settle()
                V.tensor_scalar(small[:, 40:44], small[:, 36:40], 1.0 / P, LN_EPS, ALU.mult, ALU.add)\
                    .then_inc(var_done, 1)

            def head_norm(g):
                r = inverse_root(None, 4)
                qt, h0 = UNITS0[4 * g]
                ins = V.tensor_tensor(v3(y_tok[:, qt, h0 * P:(h0 + 4) * P], 4), v3(result(dve, ("O", g))[:, :], 4),
                                      r.unsqueeze(2).broadcast_to([P, 4, P]), ALU.mult)
                empties(ins, ("O", g))
                wait_emptied(dve, ("O", g))
                V.memset(small[:, 47:48], 0.0).then_inc(o_done, 1)

            for u in range(AHEAD):
                maxima(u)
            combine(0)
            for u in range(len(UNITS0)):
                if u + 1 < len(UNITS0):
                    combine(u + 1)
                if u + AHEAD < len(UNITS0):
                    maxima(u + AHEAD)
                if u and u % 4 == 0:
                    head_var(u // 4 - 1)
                if u > 1 and u % 4 == 1:
                    head_norm(u // 4 - 1)
            head_var(3)
            head_norm(3)
            lows("oT", hT, None, lambda ch: cols[:, COL_SUB:COL_SUB + 1])
            split_to(last_panel("wo", 1) + 2)

            xs = [0]

            def residual_norm(stage, gate, ln, used):
                for nb in range(2):
                    for tt in range(TT):
                        sl = slice(nb * NB, nb * NB + NB)
                        y = y_tok[:, tt, sl]
                        empties(V.tensor_tensor(y, result(dve, (stage, nb, tt))[:, :], gate[:, sl], ALU.mult),
                                (stage, nb, tt))
                        wait_emptied(dve, (stage, nb, tt))
                        step(V.scalar_tensor_tensor(y, x_tok[:, tt, sl], ALPHA, y, ALU.mult, ALU.add))
                        settle()
                        st = small[:, 100 + 12 * tt + 6 * nb:106 + 12 * tt + 6 * nb]
                        step(V.bn_stats(st, y))
                V.memset(small[:, 47:48], 0.0).then_inc(used, 1)
                settle()
                for tt in range(TT):
                    step(V.bn_aggr(small[:, 124 + 2 * tt:126 + 2 * tt], small[:, 100 + 12 * tt:112 + 12 * tt]))
                settle()
                V.tensor_scalar(small[:, 24:26], small[:, 125:129:2], LN_EPS, None, ALU.add).then_inc(var_done, 1)
                r = inverse_root(None, 2)
                for tt in range(TT):
                    step(V.tensor_scalar(y_tok[:, tt, :], y_tok[:, tt, :], small[:, 124 + 2 * tt:125 + 2 * tt],
                                         r[:, tt:tt + 1], ALU.subtract, ALU.mult))
                    settle()
                    if tt == 0:
                        dve.wait_ge(ln_landed, 32 * (ln + 1))
                    step(V.tensor_tensor(y_tok[:, tt, :], y_tok[:, tt, :], ln_rows[:, 0, :], ALU.mult))
                    settle()
                    V.tensor_tensor(x_tok[:, tt, :], y_tok[:, tt, :], ln_rows[:, 1, :], ALU.add).then_inc(x_done, 1)
                    xs[0] += 1
                dve.wait_ge(x_done, xs[0])
                V.memset(small[:, 47:48], 0.0).then_inc(ln_used, 1)

            def ffn(name):
                for nb in range(FNB):
                    split_to(last_panel(name + "_in", nb) + 2)
                    wait_emptied(dve, (name, "g", nb))
                    bank = result(dve, (name, "u", nb))
                    t = tmp[:, nb % 2, :]
                    step(V.tensor_tensor(t, t, bank[:, :], ALU.mult))
                    settle()
                    hi, lo = (x[:, 2 * nb:2 * nb + 2, :] for x in ffT)
                    step(V.tensor_copy(hi, v3(t, 2)))
                    settle()
                    empties(V.tensor_tensor(lo, v3(t, 2), hi.bitcast(F32), ALU.subtract), (name, "u", nb))
                    for e in FFN_EVENTS[name].get(nb, []):
                        mod_finish(e)
                        mod_product(e + 2)
                for (nb, kg), e in OUT_EVENTS[name].items():
                    split_to(panel_at[(name + "_out", nb, kg)] + 2)
                    mod_finish(e)
                    mod_product(e + 2)
                split_to(last_panel(name + "_out", 1) + 2)

            residual_norm("wo", g1row, 0, g1_used)
            lows("ffn0_h", hT, mod_col(4), mod_col(5))
            ffn("ffn0")
            residual_norm("ffn0_out", g2row, 1, g2_used)

            dve.wait_ge(psc_landed, 16)
            step(V.tensor_tensor(g1row, g1row, pscale, ALU.mult))
            for tt in range(TT):
                step(V.tensor_tensor(hx_tok[:, tt, :], x_tok[:, tt, :], mod_rows[:, 1, :], ALU.mult))
                settle()
                V.tensor_tensor(hx_tok[:, tt, :], hx_tok[:, tt, :], mod_rows[:, 0, :], ALU.add).then_inc(hx_done, 1)
            split_to(last_panel("pool", 0) + 2)
            residual_norm("poolw", g1row, 2, g1_used)
            lows("ffn1_h", hT, mod_col(6), mod_col(7))
            ffn("ffn1")
            residual_norm("ffn1_out", g2row, 3, g2_used)

            def rms_input():
                for tt in range(TT):
                    step(V.tensor_tensor_reduce(y_tok[:, tt, :], x_tok[:, tt, :], x_tok[:, tt, :], 1.0, 0.0,
                                                ALU.mult, ALU.add, small[:, 20 + tt:21 + tt]))
                settle()
                V.tensor_scalar(small[:, 24:26], small[:, 20:22], 1.0 / D, RMS_EPS, ALU.mult, ALU.add)\
                    .then_inc(var_done, 1)
                r = inverse_root(None, 2)
                for tt in range(TT):
                    V.tensor_scalar(y_tok[:, tt, :], x_tok[:, tt, :], r[:, tt:tt + 1], None, ALU.mult)\
                        .then_inc(xn_done, 1)

            rms_input()
            lows("z_h", hT, None, gain(COL_N1))

            scr = tmp[:, :, :].rearrange("p a b -> p (a b)")

            def squares(col, heads, idx):
                for tt in range(TT):
                    zz = z[:, tt, col:col + heads * HD]
                    settle()
                    step(V.tensor_tensor(scr[:, 0:heads * HD], zz, zz, ALU.mult))
                    settle()
                    step(V.tensor_reduce(ss[:, tt, idx:idx + heads], v3(scr[:, 0:heads * HD], heads), AX, ALU.add))

            def after_block(nb):
                split_to(last_panel("z", nb) + 2)
                wait_emptied(dve, ("z", nb, 0))
                wait_emptied(dve, ("z", nb, 1))

            def mean_squares(lo, hi):
                settle()
                V.tensor_scalar(ss[:, :, lo:hi], ss[:, :, lo:hi], 1.0 / HD, RMS_EPS, ALU.mult, ALU.add)\
                    .then_inc(var_done, 1)

            after_block(0)
            squares(AQ, 8, SS_AQ)
            after_block(1)
            squares(AK, 1, SS_AK)
            for tt in range(TT):
                step(V.tensor_copy(v3(kdup[:, tt, 1, :], 2), z[:, tt, IK:IK + HD].unsqueeze(1).broadcast_to([P, 2, HD])))
            after_block(2)
            squares(BQ, 8, SS_BQ)
            after_block(3)
            squares(BKS, 2, SS_KS)
            for tt in range(TT):
                src = z[:, tt, BKC:BKC + 4 * HD].rearrange("p (b n) -> p b n", b=4)
                step(V.tensor_copy(kdup[:, tt, 6:10, :].rearrange("p b (s n) -> p b s n", s=2),
                                   src.unsqueeze(2).broadcast_to([P, 4, 2, HD])))
            after_block(4)
            squares(BKW, 2, SS_KW)
            mean_squares(0, SS_CQ)
            after_block(5)
            after_block(6)
            squares(CQ, 12, SS_CQ)
            mean_squares(SS_CQ, SS_CK)
            after_block(7)
            squares(CK, 12, SS_CK)
            mean_squares(SS_CK, SS_N)
            after_block(8)
            rstds[0] += len(SS_PARTS)
            dve.wait_ge(rstd_done, rstds[0])
            for tt in range(TT):
                for idx, col, slot in ((SS_AK, AK, 0), (SS_KS, BKS, 2), (SS_KS + 1, BKS + HD, 3),
                                       (SS_KW, BKW, 4), (SS_KW + 1, BKW + HD, 5)):
                    step(V.tensor_scalar(v3(kdup[:, tt, slot, :], 2),
                                         z[:, tt, col:col + HD].unsqueeze(1).broadcast_to([P, 2, HD]),
                                         rs[:, tt, idx:idx + 1], None, ALU.mult))
                ck = v3(z[:, tt, CK:CK + 768], 12)
                step(V.tensor_tensor(ck, ck, rs[:, tt, SS_CK:SS_CK + 12].unsqueeze(2).broadcast_to([P, 12, HD]),
                                     ALU.mult))
            settle()
            V.tensor_scalar(small[:, 224:224 + 2 * SS_N], small[:, 224:224 + 2 * SS_N], HD ** -0.5, None, ALU.mult)\
                .then_inc(zsrc_done, 1)

            split_to(last_panel("z", 9) + 2)
            for i in range(4):
                bank = result(dve, ("dupT", i))
                for half in range(2):
                    rows = slice(half * HD, (half + 1) * HD)
                    for lo in range(2):
                        win = bank[rows, lo * CMP_STRIDE:lo * CMP_STRIDE + N_CMP * CMP_STRIDE]
                        win = win.rearrange("p (n l j) -> p j l n", l=8, j=2)[:, half, :, :]
                        pos = posT[rows, (i // 2) * 16 + lo * 8:(i // 2) * 16 + lo * 8 + 8]
                        ins = V.tensor_tensor(xc[rows, i, lo * 8:lo * 8 + 8, :], win,
                                              pos.unsqueeze(2).broadcast_to([HD, 8, N_CMP]), ALU.add)
                        if half == 1 and lo == 1:
                            empties(ins, ("dupT", i))
                        else:
                            step(ins)
            wait_emptied(dve, ("dupT", 3))
            V.memset(small[:, 47:48], 0.0).then_inc(xc_done, 1)
            for b0, n in FT_PAIRS:
                if b0 not in FT_ON_ACT:
                    src = v3(result(dve, ("ft", b0))[:, 0:n * SEQ], n)
                    if b0 in FT_GAIN:
                        g = COL_QK + FT_GAIN[b0]
                        ins = V.tensor_scalar(ft[:, b0:b0 + n, :], src, cols[:, g:g + 1], None, ALU.mult)
                    else:
                        ins = V.tensor_copy(ft[:, b0:b0 + n, :], src)
                    empties(ins, ("ft", b0))

            bank = result(dve, "cmp")
            step(V.tensor_copy(ckd[:, :, 0:HD], v3(bank[0:N_CMP, 0:2 * HD], 2)))
            empties(V.tensor_copy(vcmp, v3(bank[0:N_CMP, 2 * HD:4 * HD], 2)), "cmp")
            settle()
            sq = v3(scr[0:N_CMP, 0:2 * HD], 2)
            step(V.tensor_tensor(sq, ckd[:, :, 0:HD], ckd[:, :, 0:HD], ALU.mult))
            settle()
            step(V.memset(small[:, 20:22], 1.0))
            settle()
            step(V.tensor_reduce(small[0:N_CMP, 20:22], sq, AX, ALU.add))
            settle()
            V.tensor_scalar(small[:, 24:26], small[:, 20:22], 1.0 / HD, RMS_EPS, ALU.mult, ALU.add)\
                .then_inc(var_done, 1)
            r = inverse_root(None, 2)
            step(V.tensor_tensor(ckd[:, :, 0:HD], ckd[:, :, 0:HD],
                                 r[0:N_CMP, :].unsqueeze(2).broadcast_to([N_CMP, 2, HD]), ALU.mult))
            settle()
            V.tensor_copy(ckd[:, :, HD:P], ckd[:, :, 0:HD]).then_inc(ckd_done, 1)
            bank = result(dve, "kcT")
            src = bank[:, 0:2 * P].rearrange("p (g n) -> p g n", g=2)[:, :, 0:N_CMP]
            empties(V.tensor_scalar(kcT, src, cols[:, COL_QK + 3:COL_QK + 4], None, ALU.mult), "kcT")

            dve.wait_ge(bias_landed, 16)
            for qt in range(TT):
                nk = (qt + 1) * P
                for h in range(4):
                    wait_emptied(dve, ("I", qt, h % 2))
                    settle()
                    ins = V.scalar_tensor_tensor(score[qt], rel[:, h, 0:nk], z[:, qt, IW + h:IW + h + 1],
                                                 causal[:, SEQ - nk:SEQ] if h == 0 else score[qt],
                                                 ALU.mult, ALU.add)
                    if h < 3:
                        step(ins)
                ins.then_inc(rel_used, 1)
                dve.wait_ge(rel_used, qt + 1)

            def top_keys(i):
                qt, it = divmod(i, TOPK // 8)
                src = score[qt] if it == 0 else work[qt]
                settle()
                step(V.max(small[:, 40:48], src))
                settle()
                step(V.match_replace(work[qt], small[:, 40:48], src, TAKEN))
                if it == TOPK // 8 - 1:
                    settle()
                    step(V.tensor_scalar(selmask[qt], work[qt], 0.5 * TAKEN, NEG, ALU.is_gt, ALU.mult))

            dve.wait_ge(gates_done, 2 * TT)

            def logits(u):
                kind, qt, h = UNITS2[u]
                nk = (qt + 1) * P
                L = lbuf[:, u % 4, :]
                o = 64 + 16 * (u % 4)
                segs = unit_segments(kind, h)
                v = u - AHEAD - 1
                if v >= 0:
                    kk, q2, h2 = UNITS2[v]
                    nb2 = (q2 + 1) * len(unit_segments(kk, h2))
                    result(dve, ("PT2", v, "c" if kk == "B" else (nb2 - 1) // 4))
                for s, (qb, kb, bh, _) in enumerate(segs):
                    idx = {"A": SS_AQ + h, "B": SS_BQ + h, "C": SS_CQ + 4 * s + h}[kind]
                    bank = result(dve, ("S2", u, s // 2))
                    ins = V.scalar_tensor_tensor(L[:, s * nk:(s + 1) * nk], bank[:, (s % 2) * 256:(s % 2) * 256 + nk],
                                                 rs[:, qt, idx:idx + 1], bias[:, bh, SEQ - nk:SEQ], ALU.mult, ALU.add)
                    if s % 2 == 1 or s == len(segs) - 1:
                        empties(ins, ("S2", u, s // 2))
                        wait_emptied(dve, ("S2", u, s // 2))
                    else:
                        step(ins)
                if kind == "A":
                    step(V.tensor_tensor(L[:, 0:nk], L[:, 0:nk], selmask[qt], ALU.add))
                    settle()
                if kind == "B":
                    end = 2 * nk + N_CMP
                    empties(V.scalar_tensor_tensor(L[:, 2 * nk:end], result(dve, ("S2", u, "c"))[:, 0:N_CMP],
                                                   rs[:, qt, SS_BQ + h:SS_BQ + h + 1], cmp_mask[:, qt, :],
                                                   ALU.mult, ALU.add), ("S2", u, "c"))
                    step(V.tensor_reduce(small[:, o + 8:o + 10], v3(L[:, 0:2 * nk], 2), AX, ALU.max))
                    wait_emptied(dve, ("S2", u, "c"))
                    step(V.tensor_reduce(small[:, o + 10:o + 11], L[:, 2 * nk:end], AX, ALU.max))
                    settle()
                    V.tensor_scalar(small[:, o:o + 3], small[:, o + 8:o + 11], 0.1 * NEG, -1.0, ALU.max, ALU.mult)\
                        .then_inc(l_done, 1)
                else:
                    step(V.tensor_reduce(small[:, o + 8:o + 9], L[:, 0:len(segs) * nk], AX, ALU.max))
                    settle()
                    V.tensor_scalar(small[:, o:o + 1], small[:, o + 8:o + 9], -1.0, None, ALU.mult).then_inc(l_done, 1)

            def inv_sum(u):
                kind, qt, h = UNITS2[u]
                return 48 + 8 * qt + h

            def weigh(u):
                kind, qt, h = UNITS2[u]
                nk = (qt + 1) * P
                L = lbuf[:, u % 4, :]
                o = 64 + 16 * (u % 4)
                dve.wait_ge(exp2_done, u + 1)
                if kind != "B":
                    V.reciprocal(small[:, inv_sum(u):inv_sum(u) + 1], small[:, o + 4:o + 5]).then_inc(p_done, 1)
                    return
                step(V.tensor_scalar(small[:, o + 12:o + 15], small[:, o + 4:o + 7], 1e-30, None, ALU.max))
                settle()
                step(V.reciprocal(small[:, o + 8:o + 11], small[:, o + 12:o + 15]))
                settle()
                step(V.tensor_tensor(small[:, o + 12:o + 15], small[:, o + 8:o + 11], gates[:, qt, h, :], ALU.mult))
                settle()
                step(V.tensor_scalar(L[:, 0:nk], L[:, 0:nk], small[:, o + 12:o + 13], None, ALU.mult))
                step(V.tensor_scalar(L[:, nk:2 * nk], L[:, nk:2 * nk], small[:, o + 13:o + 14], None, ALU.mult))
                V.tensor_scalar(L[:, 2 * nk:2 * nk + N_CMP], L[:, 2 * nk:2 * nk + N_CMP], small[:, o + 14:o + 15],
                                None, ALU.mult).then_inc(p_done, 1)

            def outputs(u):
                kind, qt, h = UNITS2[u]
                heads = h + 1
                bank = result(dve, ("O2", kind, qt))
                src, dst = v3(bank[:, 0:heads * HD], heads), v3(o2_tok(kind, qt), heads)
                if kind == "B":
                    empties(V.tensor_copy(dst, src), ("O2", kind, qt))
                else:
                    r0 = inv_sum(u - h)
                    empties(V.tensor_tensor(dst, src, small[:, r0:r0 + heads].unsqueeze(2)
                                            .broadcast_to([P, heads, HD]), ALU.mult), ("O2", kind, qt))

            for u in range(AHEAD):
                logits(u)
            weigh(0)
            for u, (kind, qt, h) in enumerate(UNITS2):
                if u + 1 < len(UNITS2):
                    weigh(u + 1)
                if u + AHEAD < len(UNITS2):
                    logits(u + AHEAD)
                if u < TT * TOPK // 8:
                    top_keys(u)
                if u and UNITS2[u - 1][0:2] != (kind, qt):
                    outputs(u - 1)
            outputs(len(UNITS2) - 1)

            i = 0
            for nb in range(2):
                for br in range(3):
                    for tt in range(TT):
                        y = y_tok[:, tt, nb * NB:nb * NB + NB]
                        dve.wait_ge(sig_done, i + 1)
                        bank = result(dve, (f"branch{br}", nb, tt))
                        if i == 0:
                            wait_emptied(dve, ("oT2", "C", 1))
                        g = tmp[:, i % 2, :]
                        if br == 0:
                            empties(V.tensor_tensor(y, g, bank[:, :], ALU.mult), (f"branch{br}", nb, tt))
                            wait_emptied(dve, (f"branch{br}", nb, tt))
                        else:
                            t = lbuf[:, tt, 0:NB]
                            settle()
                            empties(V.tensor_tensor(t, g, bank[:, :], ALU.mult), (f"branch{br}", nb, tt))
                            wait_emptied(dve, (f"branch{br}", nb, tt))
                            ins = V.tensor_tensor(y, y, t, ALU.add)
                            if nb == 1 and br == 2 and tt == 1:
                                ins.then_inc(mix_done, 1)
                            else:
                                step(ins)
                        i += 1

            def residual(stage, done=None):
                for nb in range(2):
                    for tt in range(TT):
                        x = x_tok[:, tt, nb * NB:nb * NB + NB]
                        empties(V.tensor_tensor(x, x, result(dve, (stage, nb, tt))[:, :], ALU.add), (stage, nb, tt))
                for tt in range(TT):
                    wait_emptied(dve, (stage, 1, tt))

            split_to(last_panel("branch2", 1) + 2)
            lows("mixed", hT)
            split_to(last_panel("w_out", 1) + 2)
            residual("w_out")
            rms_input()
            lows("ffn2_h", hT, None, gain(COL_N2))
            ffn("ffn2")
            residual("ffn2_out")

        @block.gpsimd
        def _(pool):
            roots = [0]

            def pool_share(i):
                raw, hi, lo = raw_panel(i), panel_part(i, 0), panel_part(i, 1)
                if by_pool[i]:
                    wait_hi_free(pool, i)
                    wait_landed(pool, i)
                    copies[0] += 1
                    nc.gpsimd.tensor_copy(hi, raw).then_inc(pool_step, 1)
                    pool.wait_ge(pool_step, copies[0])
                    half = slice(0, panels[i][2])
                else:
                    wait_split(pool, i, hi_only=True)
                    half = slice(panels[i][2] // 2, panels[i][2])
                nc.gpsimd.tensor_tensor(lo[:, half, :], raw[:, half, :], hi[:, half, :].bitcast(F32), ALU.subtract)\
                    .then_inc(w_pool, 1)

            split_to = splitter(pool_share)
            copies = [0]

            def inverse_root(src, dst, exponent):
                roots[0] += 1
                pool.wait_ge(var_done, roots[0])
                nc.gpsimd.tensor_tensor(dst, src, exponent, ALU.pow).then_inc(rstd_done, 1)

            def token_root():
                inverse_root(small[:, 24:26], small[:, 32:34], neghalf[:, 0:2])

            split_to(last_panel("qkv", 5) + 2)
            pool.wait_ge(consts_done, 1)
            for _ in range(4):
                inverse_root(small[:, 40:44], small[:, 32:36], neghalf[:, 0:4])
            for stage, nb in (("wo", 1), ("ffn0_out", 1), ("pool", 0), ("ffn1_out", 1)):
                split_to(last_panel(stage, nb) + 2)
                token_root()
            token_root()
            for (lo, hi), nb in zip(SS_PARTS, (6, 8, 8)):
                split_to(last_panel("z", nb))
                inverse_root(ss[:, :, lo:hi], rs[:, :, lo:hi], v3(neghalf[:, 0:2 * (hi - lo)], TT))
            split_to(last_panel("z", 9) + 2)
            token_root()
            split_to(last_panel("w_out", 1) + 2)
            token_root()
            split_to(len(panels))

        @block.sync
        def _(sp):
            def row_load(dst, src, sem_):
                sp.dma_start(dst, src.partition_broadcast(P)).then_inc(sem_, 16)

            mod_panel(sp, 0)
            mod_panel(sp, 1)
            n1 = 48 * DEPTH
            small_loads = [
                (colsrc[0:n1, :], a["b_mod"].rearrange("l (n p) -> (l n) p", p=P)),
                (colsrc[COL_N1:COL_N1 + KC, :], a["norm1_g_2"].rearrange("l (n p) -> (l n) p", p=P)),
                (colsrc[COL_N2:COL_N2 + KC, :], a["norm2_g_2"].rearrange("l (n p) -> (l n) p", p=P)),
                (colsrc[COL_SUB:COL_SUB + 1, :], a["attn_subln_g"]),
                (colsrc[COL_QK:COL_QK + 6, 0:HD], a["qk_norm_g_2"][0]),
                (colsrc[COL_QK:COL_QK + 6, HD:P], a["qk_norm_g_2"][0]),
                (possrc, a["nsa_cmp_pos_2"][0].rearrange("v (l j) d -> (v l) (j d)", j=2)),
                (oh_sb, a["const_onehot"]),
                (rm_sb, a["const_rowmask"]),
                (rel_sb, a["rel_bias_2"]),
            ]
            for dst, src in small_loads:
                sp.dma_start(dst, src).then_inc(cols_landed, 16)
            sp.dma_start(table[:, :], a["const_table"]).then_inc(table_landed, 16)
            sp.dma_start(x_tok, a["x"][0].rearrange("(t p) d -> p t d", p=P)).then_inc(x_landed, 16)
            sp.dma_start(y_tok, a["ctx"][0].rearrange("(t p) d -> p t d", p=P)).then_inc(ctx_landed, 16)
            row_load(lam_in, a["attn_lambda"][0], lam_landed)
            mod_panel(sp, 2)
            mod_panel(sp, 3)
            mods_before = {RING: [4, 5], 5: [6, 7]}
            for e in range(8, N_EVENTS):
                mods_before.setdefault(event_panel[e - 4] + 5, []).append(e)
            for i, (key, srcs, chunks, width) in enumerate(panels):
                for e in mods_before.get(i, []):
                    mod_panel(sp, e)
                if i >= RING:
                    sp.wait_ge(*done[i - RING])
                slot = raw_panel(i)
                for src, lo, n in srcs:
                    sp.dma_start(slot[:, :, lo:lo + n], src).then_inc(w_landed[i % RING], 16)
                if i == RING:
                    for comp, row in ((2, g1row), (5, g2row)):
                        row_load(row, a["b_mod"][0, comp * D:(comp + 1) * D], g_landed[comp])
                    for r, w in enumerate(("ln_g", "ln_b")):
                        row_load(ln_rows[:, r, :], a[w][0, 0, :], ln_landed)
                if key == ("ffn1_in", 2, 0):
                    sp.wait_ge(srow_stored, 16)
                    sp.wait_ge(mod_acc, N_EVENTS - FIRST_DVE_EVENT)
                    sp.dma_start(bias, bass.AP(scratch.tensor, P - 1, [[SROW - 1, P], [P * SROW, REL_HEADS], [1, SEQ]]))\
                        .then_inc(bias_landed, 16)
            for tt in range(TT):
                wait_emptied(sp, ("ffn2_out", 1, tt))
                sp.dma_start(out[0, tt * P:(tt + 1) * P, :], x_tok[:, tt, :]).then_inc(out_stored, 16)
            sp.wait_ge(out_stored, 16 * TT)


_INS = ["x", "c", "ctx", "c_ctx", "w_mod", "b_mod", "ln_g", "ln_b", "attn_w_qkv", "attn_lambda",
        "attn_subln_g", "attn_w_o", "pool_w", "pool_scale", "ffn_w_in", "ffn_w_out", "norm1_g_2",
        "norm2_g_2", "w_in_2", "qk_norm_g_2", "nsa_cmp_pos_2", "nsa_cmp_w_2", "w_branch_a_2",
        "w_branch_b_2", "w_branch_c_2", "w_out_2", "w_ffn_in_2", "w_ffn_out_2", "rel_bias_2"]


def kernel(**inputs):
    import concourse.bacc as _bacc
    from concourse.bass_utils import run_bass_kernel_spmd as _run

    nc = _bacc.Bacc("TRN2", target_bir_lowering=False, num_devices=1)
    arrays = {f"in_{n}": np.ascontiguousarray(inputs[n]) for n in _INS}
    arrays.update(shape_constants())
    args = {n.removeprefix("in_"): nc.dram_tensor(n, v.shape, F32, kind="ExternalInput").ap()
            for n, v in arrays.items()}
    out = nc.dram_tensor("out", (1, SEQ, D), F32, kind="ExternalOutput").ap()
    scratch = nc.dram_tensor("bias_rows", (REL_HEADS, P, SROW), F32, kind="Internal").ap()
    build(nc, args, out, scratch)
    return _run(nc, [arrays], core_ids=[0]).results[0]["out"]
```

```python
from contextlib import ExitStack

import numpy as np

import concourse.bass as bass
from concourse import mybir

F32 = mybir.dt.float32
F32R = mybir.dt.float32r
ALU = mybir.AluOpType
ACT = mybir.ActivationFunctionType
AX = mybir.AxisListType.X

P = 128
SEQ = 256
TT = SEQ // P
D = 1024
KC = D // P
NB = 512
PK = 4
HEADS = 8
HD = 64
DEPTH = 2
ALPHA = (2.0 * DEPTH) ** 0.25
LN_EPS = 1e-5
RMS_EPS = 1e-6
LAM_INIT = 0.8 - 0.6
D_FF = -(-8 * D // (3 * 256)) * 256
FC = D_FF // P
FNB = D_FF // 256
POOL_WINDOWS = (2, 4, 8, 16)
GRID_W = 64
NEG = -1.0e30
TAKEN = -3.0e38
TOPK = min(256, SEQ // 4)

AQ, AK, AV, IQ, IK, IW = 0, 512, 576, 640, 896, 960
BQ, BKC, BVC, BKS, BVS, BKW, BVW, BG = 964, 1476, 1604, 1732, 1860, 1988, 2116, 2244
CQ, CK, CV, MIX = 2268, 3036, 3804, 4572
ZW = MIX
Z_BLOCKS = [(0, 512), (512, 964), (964, 1476), (1476, 1860), (1860, 2268),
            (2268, 2780), (2780, 3292), (3292, 3804), (3804, 4316), (4316, 4572)]
CMP_LEN, CMP_STRIDE = 32, 16
N_CMP = (SEQ - CMP_LEN) // CMP_STRIDE + 1
C_GROUPS = ((128, 1), (512, 4), (2048, 16))
BUCKETS, MAX_DIST = 32, 2048
REL_HEADS = 28
SROW = 384

COL_BMOD, COL_N1, COL_N2, COL_SUB, COL_QK = 0, 96, 104, 112, 113
N_COLS = 119

SS_AQ, SS_AK, SS_BQ, SS_KS, SS_KW, SS_CQ, SS_CK, SS_N = 0, 8, 9, 17, 19, 21, 33, 45
SS_PARTS = ((0, SS_CQ), (SS_CQ, SS_CK), (SS_CK, SS_N))

RING = 4
PARTS = 2
AHEAD = 3
MODS = 2
WHOLE = ("pool", "cmp", "branch0", "branch1", "branch2")


def shape_constants():
    t = np.arange(SEQ)
    inv = np.power(np.float32(10000.0), -np.arange(16, dtype=np.float32) / np.float32(16))
    row = np.repeat(np.arange(SEQ // GRID_W, dtype=np.float32), GRID_W)
    col = np.tile(np.arange(GRID_W, dtype=np.float32), SEQ // GRID_W)
    ang = np.concatenate([row[:, None] * inv, col[:, None] * inv], axis=-1).astype(np.float32)
    cos, sin = np.cos(ang), np.sin(ang)
    rope = np.stack([np.concatenate([cos, cos], 1), np.concatenate([-sin, sin], 1)], 1)
    rope = rope.reshape(TT, P, 2 * HD).transpose(1, 0, 2).reshape(P, -1)
    dist = P + np.arange(P)[:, None] - np.arange(SEQ)[None, :]
    causal = np.where(dist >= 0, 0.0, NEG)
    cend = np.arange(N_CMP) * CMP_STRIDE + CMP_LEN - 1
    cmp_mask = np.where(cend[None, :] <= t[:, None], 0.0, NEG).reshape(TT, P, N_CMP)
    cmp_mask = cmp_mask.transpose(1, 0, 2).reshape(P, -1)
    table = np.concatenate([np.eye(P), rope, causal, cmp_mask], axis=1).astype(np.float32)

    d = SEQ - 1 - np.arange(SROW)
    n = np.maximum(d, 0)
    exact = BUCKETS // 2
    nf = np.maximum(n, 1).astype(np.float32)
    large = exact + (np.log(nf / np.float32(exact)) / np.float32(np.log(MAX_DIST / exact))
                     * np.float32(BUCKETS - exact)).astype(np.int32)
    bucket = np.where(n < exact, n, np.minimum(large, BUCKETS - 1))
    onehot = ((bucket[None, :] == np.arange(BUCKETS)[:, None]) & (d >= 0)).astype(np.float32)
    rowmask = np.zeros((REL_HEADS, SROW), np.float32)
    rowmask[:, d < 0] = NEG
    for g, (win, dil) in enumerate(C_GROUPS):
        rowmask[16 + 4 * g:20 + 4 * g, (d % dil != 0) | (d > win)] = NEG

    pool = np.zeros((len(POOL_WINDOWS), SEQ, SEQ), np.float32)
    for g, w in enumerate(POOL_WINDOWS):
        lo, hi = np.clip(t - w // 2, 0, SEQ), np.clip(t + w - w // 2, 0, SEQ)
        inside = (t[:, None] >= lo[None, :]) & (t[:, None] < hi[None, :])
        pool[g] = inside / (hi - lo)[None, :].astype(np.float32) - np.eye(SEQ)
    pool = pool.reshape(len(POOL_WINDOWS), TT, P, SEQ).transpose(2, 1, 0, 3)
    return {"const_table": table, "const_onehot": onehot, "const_rowmask": rowmask,
            "const_pool": np.ascontiguousarray(pool.reshape(P, -1)).astype(np.float32)}


def w_panels(a):
    out = []

    def add(key, w, kg, chunks, lo, hi):
        src = w[kg * PK * P:(kg * PK + chunks) * P, lo:hi].rearrange("(c p) n -> p c n", p=P)
        out.append((key, [(src, 0, hi - lo)], chunks, hi - lo))

    def ffn(name, w_in, w_out):
        for nb in range(FNB):
            for kg in range(2):
                rows = w_in[kg * PK * P:(kg + 1) * PK * P, :]
                parts = [(rows[:, h * D_FF + nb * 256:h * D_FF + nb * 256 + 256]
                          .rearrange("(c p) n -> p c n", p=P), h * 256, 256) for h in range(2)]
                out.append(((name + "_in", nb, kg), parts, PK, 512))
        for nb in range(2):
            for kg in range(-(-FC // PK)):
                add((name + "_out", nb, kg), w_out, kg, min(PK, FC - kg * PK), nb * NB, nb * NB + NB)

    for nb in range(6):
        for kg in range(2):
            add(("qkv", nb, kg), a["attn_w_qkv"][0], kg, PK, nb * NB, nb * NB + NB)
    for nb in range(2):
        for kg in range(2):
            add(("wo", nb, kg), a["attn_w_o"][0], kg, PK, nb * NB, nb * NB + NB)
    ffn("ffn0", a["ffn_w_in"][0], a["ffn_w_out"][0])
    out.append((("pool", 0, 0), [(a["pool_w"][0].rearrange("g (c p) n -> p (g c) n", p=P), 0, 256)], 8, 256))
    ffn("ffn1", a["ffn_w_in"][1], a["ffn_w_out"][1])
    w_in = a["w_in_2"][0]
    for nb, (lo, hi) in enumerate(Z_BLOCKS):
        for kg in range(2):
            add(("z", nb, kg), w_in, kg, PK, lo, hi)
    out.append((("cmp", 0, 0), [(a["nsa_cmp_w_2"][0].rearrange("v (l j) d e -> (j d) (v l) e", j=2), 0, HD)],
                32, HD))
    for nb in range(2):
        for br in range(3):
            for kg in range(2):
                lo = MIX + br * D + nb * NB
                add(("mix", nb * 3 + br, kg), w_in, kg, PK, lo, lo + NB)
    for nb in range(2):
        for br, w in enumerate(("w_branch_a_2", "w_branch_b_2", "w_branch_c_2")):
            add((f"branch{br}", nb, 0), a[w][0], 0, 2 if br == 2 else 4, nb * NB, nb * NB + NB)
    for nb in range(2):
        for kg in range(2):
            add(("w_out", nb, kg), a["w_out_2"][0], kg, PK, nb * NB, nb * NB + NB)
    ffn("ffn2", a["w_ffn_in_2"][0], a["w_ffn_out_2"][0])
    return out


def build(nc, a, out, scratch):
    panels = w_panels(a)
    panel_at = {key: i for i, (key, *_) in enumerate(panels)}

    with ExitStack() as ctx:
        def sb(name, cols, parts=P):
            return ctx.enter_context(nc.sbuf_tensor(name, [parts, cols], F32))

        def sem(name):
            return ctx.enter_context(nc.semaphore(name))

        def v3(ap, a_):
            return ap.rearrange("p (a b) -> p a b", a=a_)

        def parts(name, cols_, stack=ctx):
            return [stack.enter_context(nc.sbuf_tensor(f"{name}_{x}", [P, cols_], F32R)) for x in ("hi", "lo")]

        with ExitStack() as shared:
            ring_lo = [shared.enter_context(nc.sbuf_tensor(f"ring_lo{i}", [P, PK * NB], F32R)) for i in range(RING)]
        ring = [sb(f"ring{i}", PK * NB) for i in range(RING)]
        w_hi_buf = [ctx.enter_context(nc.sbuf_tensor(f"w_hi{i}", [P, PK * NB], F32R)) for i in range(PARTS)]
        with ExitStack() as shared:
            ff_parts = parts("ff", FC * SEQ, shared)
            shared.enter_context(nc.sbuf_tensor("between", [P, 12288 - 2 * FC * SEQ], F32))
            con_parts = parts("con", KC * SEQ, shared)
        big = sb("big", 16384)
        with ExitStack() as shared:
            prob_raw = shared.enter_context(nc.sbuf_tensor("prob", [P, 2 * KC * SEQ], F32))
        h_parts = parts("h", KC * SEQ)
        aux = sb("aux", 12288)
        x_tok = sb("x_tok", TT * D)[:].rearrange("p (t n) -> p t n", t=TT)
        y_tok = sb("y_tok", TT * D)[:].rearrange("p (t n) -> p t n", t=TT)
        table = sb("table", P + TT * 2 * HD + SEQ + TT * N_CMP)
        ident = table[:, 0:P]
        rope = v3(table[:, P:P + TT * 2 * HD], TT * 2)
        causal = table[:, P + 4 * HD:P + 4 * HD + SEQ]
        cmp_mask = v3(table[:, P + 4 * HD + SEQ:], TT)
        ones = sb("ones", P)
        neghalf = sb("neghalf", 96)
        cols = sb("cols", N_COLS)
        modcol = v3(sb("modcol", 64)[:], 8)
        cs_in = v3(sb("cs_in", 16)[:], 2)
        cs = sb("cs", 16)
        modacc_raw = sb("modacc", MODS * NB)
        modacc = v3(modacc_raw[:], MODS)
        tmp = v3(sb("tmp", 2 * NB)[:], 2)
        small = sb("small", 368)
        ln_cols = v3(sb("ln_cols", 6 * KC)[:], 6)
        rms_z = small[:, 16:18]
        ss = v3(small[:, 128:128 + 2 * SS_N], TT)
        rs = v3(small[:, 224:224 + 2 * SS_N], TT)
        gates = small[:, 320:368].rearrange("p (t h g) -> p t h g", t=TT, h=8)
        srow = sb("srow", SROW, REL_HEADS)
        posT = sb("posT", 32)
        lam = sb("lam", 8)

        q_tok = v3(big[:, 0:2048], TT)
        k_tok = v3(big[:, 2048:6144], 4)
        v_tok = v3(big[:, 6144:10240], 4)
        qT = v3(big[:, 10240:12288], HEADS)
        kT = v3(big[:, 12288:16384], HEADS)
        hT = [v3(p_[:], KC) for p_ in h_parts]
        conT = [v3(p_[:], KC) for p_ in con_parts]
        ffT = [v3(p_[:], FC) for p_ in ff_parts]
        whole = v3(big[:, 0:2 * KC * SEQ], 2 * KC)
        mod_rows = v3(big[:, 11264:13312], 2)
        pool_m = v3(big[:, 13312:15360], TT * 4)
        pscale = big[:, 15360:16384]
        hx_tok = v3(big[:, 0:2048], TT)
        pooledT = v3(big[:, 2048:4096], KC)
        modring = [v3(aux[:, 4096 * i:4096 * i + 4096], KC) for i in range(MODS)]
        g1row, g2row = aux[:, 8192:9216], aux[:, 9216:10240]
        ln_rows = v3(aux[:, 10240:12288], 2)
        prob = prob_raw[:].rearrange("p (b m n) -> p b m n", b=AHEAD + 1, m=2)
        aT = v3(big[:, 0:1024], 2)
        z = v3(big[:, 0:TT * ZW], TT)
        ft = v3(big[:, TT * ZW:TT * ZW + 28 * SEQ], 28)
        oT2 = ft[:, 0:10, :]
        bias = v3(aux[:, 0:REL_HEADS * SEQ], REL_HEADS)
        kdup = aux[:, 7168:9728].rearrange("p (t b n) -> p t b n", t=TT, b=10)
        lbuf = v3(aux[:, 9216:12288], AHEAD + 1)
        score = [tmp[:, 0, 0:128], tmp[:, 0, 128:384]]
        work = [tmp[:, 1, 0:128], tmp[:, 1, 128:384]]
        selmask = [aux[:, 7168:7296], aux[:, 7296:7552]]
        pT = v3(aux[:, 7680:9216], 2)
        rel = v3(aux[:, 10240:10240 + 4 * SEQ], 4)
        o_c = v3(modacc_raw[:, 0:2 * SEQ], 2)
        xc = modacc_raw[:, 0:4 * 16 * N_CMP].rearrange("p (k l n) -> p k l n", k=4, l=16)
        cmp_k = srow[0:N_CMP, :]
        ckd = v3(cmp_k[:, 0:2 * P], 2)
        vcmp = v3(cmp_k[:, 2 * P:], 2)
        kcT = v3(sb("kcT", 2 * N_CMP)[:], 2)
        pcT = v3(table[0:N_CMP, P:P + 2 * P], 2)
        colsrc, possrc, oh_sb, rm_sb, rel_sb = (
            big[0:N_COLS, 0:P], big[0:32, 128:256], big[0:32, 256:640], big[0:REL_HEADS, 640:1024],
            big[0:32, 1024:1024 + REL_HEADS])
        lam_in = v3(big[:, 1100:1356], 4)
        lnsrc = big[0:6 * KC, 1356:1356 + P]

        psum = [ctx.enter_context(nc.psum_tensor(f"bank{i}", [P, NB], F32)) for i in range(8)]

        filled = [sem(f"bank_filled{i}") for i in range(8)]
        emptied = [sem(f"bank_emptied{i}") for i in range(8)]
        w_landed = [sem(f"w_landed{i}") for i in range(RING)]
        w_used = sem("w_used")
        w_hi, w_lo, w_pool, h_hi = sem("w_hi_by_act"), sem("w_lo_by_dve"), sem("w_split_by_pool"), sem("h_hi_done")
        mod_landed = [sem(f"mod_landed{i}") for i in range(MODS)]
        mod_acc = sem("mod_acc")
        x_landed, ctx_landed, c_landed = sem("x_landed"), sem("ctx_landed"), sem("c_landed")
        table_landed, cols_landed, lam_landed = sem("table_landed"), sem("cols_landed"), sem("lam_landed")
        ln_landed, g_landed = sem("ln_landed"), {2: sem("g1_bias_landed"), 5: sem("g2_bias_landed")}
        lam_sum, lam_exp, gates_done, sig_done = sem("lam_sum"), sem("lam_exp"), sem("gates_done"), sem("sig_done")
        rows_landed, poolm_landed, psc_landed = sem("rows_landed"), sem("pool_m_landed"), sem("pscale_landed")
        srow_done, srow_stored, bias_landed = sem("srow_done"), sem("srow_stored"), sem("bias_landed")
        consts_done, csil_done = sem("consts_done"), sem("csil_done")
        dve_step = sem("dve_step")
        rope_done, x_done, g1_used, g2_used, ln_used = (
            sem("rope_done"), sem("x_done"), sem("g1_used"), sem("g2_used"), sem("ln_rows_used"))
        var_done, rstd_done = sem("var_done"), sem("rstd_done")
        nmax_done, probs_done, o_done = sem("nmax_done"), sem("probs_done"), sem("o_done")
        sq_done, hx_done, mix_done = sem("sq_done"), sem("hx_done"), sem("mix_done")
        ssq_done = sem("x_squares_done")
        xn_done, dup_done, zsrc_done = sem("xn_done"), sem("dup_done"), sem("zsrc_done")
        xc_done, ckd_done = sem("xc_done"), sem("ckd_done")
        rel_used, l_done, exp2_done, p_done = (
            sem("rel_used"), sem("logits_done"), sem("exp2_done"), sem("p_done"))
        out_stored = sem("out_stored")

        block = ctx.enter_context(nc.Block())

        uses, where = [0] * 8, {}
        turn = {"gemm": 0, "misc": 0, "unit": 0, "mix": 0}
        POOLS = {"gemm": (0, 1, 2, 3, 4, 5), "misc": (6, 7), "unit": (0, 1, 2, 3, 4), "mix": (5,)}

        def result(eng, key):
            b, n = where[key]
            eng.wait_ge(filled[b], n)
            return psum[b]

        def empties(ins, key):
            ins.then_inc(emptied[where[key][0]], 1)

        def wait_emptied(eng, key):
            b, n = where[key]
            eng.wait_ge(emptied[b], n)

        def landings(i):
            return sum(len(panels[j][1]) for j in range(i % RING, i + 1, RING))

        lo_by_pool = [key[0] == "mix" for key, *_ in panels]
        split_panels = [i for i, (key, *_) in enumerate(panels) if key[0] not in WHOLE]
        ordinal = {i: n for n, i in enumerate(split_panels)}
        shared_before = [sum(not lo_by_pool[j] for j in split_panels if j <= i) for i in range(len(panels))]
        done = {}

        def raw_panel(i):
            _, _, chunks, width = panels[i]
            return ring[i % RING][:, 0:chunks * width].rearrange("p (c n) -> p c n", c=chunks)

        def panel_part(i, x):
            _, _, chunks, width = panels[i]
            buf = ring_lo[i % RING] if x else w_hi_buf[ordinal[i] % PARTS]
            return buf[:, 0:chunks * width].rearrange("p (c n) -> p c n", c=chunks)

        def wait_landed(eng, i):
            eng.wait_ge(w_landed[i % RING], 16 * landings(i))

        def wait_hi_free(eng, i):
            if ordinal[i] >= PARTS:
                eng.wait_ge(*done[split_panels[ordinal[i] - PARTS]])

        def wait_split(eng, i, hi_only=False):
            eng.wait_ge(w_hi, ordinal[i] + 1)
            if not hi_only:
                if not lo_by_pool[i]:
                    eng.wait_ge(w_lo, shared_before[i])
                eng.wait_ge(w_pool, ordinal[i] + 1)

        def splitter(one):
            nxt = [0]

            def split_to(i):
                while nxt[0] <= min(i, len(panels) - 1):
                    if nxt[0] in ordinal:
                        one(nxt[0])
                    nxt[0] += 1
            return split_to

        def last_panel(stage, nb):
            return max(i for i, (key, *_) in enumerate(panels) if key[:2] == (stage, nb))

        def mod_panel(eng, e):
            prev = e - MODS
            if prev >= FIRST_DVE_EVENT:
                eng.wait_ge(mod_acc, prev - FIRST_DVE_EVENT + 1)
            elif prev >= 0:
                result(eng, ("modrow", prev))
            l, blk = divmod(e, 12)
            eng.dma_start(modring[e % MODS], a["w_mod"][l, :, blk * NB:(blk + 1) * NB]
                          .rearrange("(p j) n -> p j n", j=KC)).then_inc(mod_landed[e % MODS], 16)

        def mod_is_row(e):
            comp = (e % 12) // 2
            return comp in ((2, 5) if e < 12 else (0, 1, 2, 5))

        QKV_EVENTS = {0: [], 1: [4, 5], 2: [6, 7], 3: [8, 9], 4: [10, 11], 5: []}
        FFN_EVENTS = {"ffn0": {1: [12], 3: [13], 5: [14], 7: [15], 9: [16], 10: [17]},
                      "ffn1": {1: [22], 3: [23]}, "ffn2": {}}
        OUT_EVENTS = {"ffn0": {(0, 1): 18, (0, 3): 19, (0, 5): 20, (1, 2): 21}, "ffn1": {}, "ffn2": {}}
        event_panel = {e: last_panel("qkv", nb) for nb, es in QKV_EVENTS.items() for e in es}
        for name_, at in FFN_EVENTS.items():
            event_panel.update({e: last_panel(name_ + "_in", nb) for nb, es in at.items() for e in es})
            event_panel.update({e: panel_at[(name_ + "_out",) + k_] for k_, e in OUT_EVENTS[name_].items()})
        FIRST_DVE_EVENT, N_EVENTS = 4, 24
        N_SMALL_LOADS = 16
        ROOTS_BEFORE_Z = 9
        UNITS0 = [(qt, h) for qt in range(TT) for h in range(HEADS)]
        UNITS2 = [("B", qt, h) for qt in range(TT) for h in range(8)] + \
                 [("C", qt, h) for qt in range(TT) for h in range(4)] + \
                 [("A", qt, h) for qt in range(TT) for h in range(8)]
        MIX_PIECES = 2 * 3 * TT * 2
        MIX_AT = {u: range(u * MIX_PIECES // len(UNITS2), (u + 1) * MIX_PIECES // len(UNITS2))
                  for u in range(len(UNITS2))}
        MIX_Z = [[(0, 0, 512)], [(964, 0, 512)], [(2268, 0, 512)], [(2780, 0, 512)], [(3292, 0, 512)],
                 [(1476, 0, 384), (640, 384, 128)]]
        FT_PLAIN = [(0, 2), (2, 2), (5, 2), (7, 1), (8, 2), (10, 2), (16, 2), (18, 2), (20, 2)]
        FT_NORMED = [(4, 1), (12, 2), (14, 2), (22, 2), (24, 2), (26, 2)]
        FT_PAIRS = FT_PLAIN + FT_NORMED
        FT_GAIN = {0: 0, 2: 0, 4: 1, 8: 2, 10: 2, 12: 3, 14: 3, 16: 4, 18: 4, 20: 4, 22: 5, 24: 5, 26: 5}
        FT_ON_ACT = {b for b, _ in FT_PLAIN} | {24}

        def ft_source(b, tt):
            if b < 4:
                return z[:, tt, AQ + b * P:AQ + (b + 1) * P]
            if b in (5, 6):
                return z[:, tt, IQ + (b - 5) * P:IQ + (b - 4) * P]
            if 8 <= b < 12:
                return z[:, tt, BQ + (b - 8) * P:BQ + (b - 7) * P]
            if 16 <= b < 22:
                return z[:, tt, CQ + (b - 16) * P:CQ + (b - 15) * P]
            if b >= 22:
                return z[:, tt, CK + (b - 22) * P:CK + (b - 21) * P]
            return kdup[:, tt, {4: 0, 7: 1, 12: 2, 13: 3, 14: 4, 15: 5}[b], :]

        def unit_segments(kind, h):
            if kind == "A":
                return [(h // 2, 4, h, AV)]
            if kind == "B":
                g = h // 4
                return [(8 + h // 2, 12 + g, 8 + h, BVS + g * HD), (8 + h // 2, 14 + g, 8 + h, BVW + g * HD)]
            return [(16 + (4 * g + h) // 2, 22 + (4 * g + h) // 2, 16 + 4 * g + h, CV + (4 * g + h) * HD)
                    for g in range(3)]

        def o2_tok(kind, qt):
            return {"A": y_tok[:, qt, 0:512], "B": y_tok[:, qt, 512:1024], "C": o_c[:, qt, :]}[kind]

        @block.tensor
        def _(pe):
            released = [0]
            next_panel = [0]

            def take(key, pool="gemm"):
                b = POOLS[pool][turn[pool] % len(POOLS[pool])]
                turn[pool] += 1
                if uses[b]:
                    pe.wait_ge(emptied[b], uses[b])
                uses[b] += 1
                where[key] = (b, uses[b])
                return psum[b]

            def fills(ins, key):
                ins.then_inc(filled[where[key][0]], 1)

            def panel(key):
                i = panel_at[key]
                assert i == next_panel[0], key
                next_panel[0] += 1
                if i not in ordinal:
                    wait_landed(pe, i)
                    return [raw_panel(i)]
                wait_split(pe, i)
                return [panel_part(i, 0), panel_part(i, 1)]

            def mm(o, l, r, start, stop, **kw):
                return nc.tensor.matmul(o, l, r, start=start, stop=stop, **kw)

            def product(o, ls, rs_, start, stop, **kw):
                pairs = [(0, 0)] if len(ls) == 1 else [(0, 0), (0, 1), (1, 0)]
                for n, (x, y) in enumerate(pairs):
                    ins = mm(o, ls[x], rs_[y], start and n == 0, stop and n == len(pairs) - 1, **kw)
                return ins

            def release(key, ins, filled_key=None):
                if filled_key is None:
                    ins.then_inc(w_used, 1)
                    released[0] += 1
                    done[panel_at[key]] = (w_used, released[0])
                else:
                    b, n = where[filled_key]
                    done[panel_at[key]] = (filled[b], n)

            def gemm(stage, lhs, tts, nb, width, groups, events={}, inputs=lambda c: ()):
                banks = {tt: take((stage, nb, tt)) for tt in tts}
                last = groups[-1][1] - 1
                for kg, (lo, hi) in enumerate(groups):
                    if nb == 0:
                        for key in inputs(hi - 1):
                            wait_emptied(pe, key)
                    w = panel((stage, nb, kg))
                    for tt in tts:
                        for c in range(lo, hi):
                            ins = product(banks[tt][:, 0:width], lhs(tt, c), [x[:, c - lo, :] for x in w],
                                          c == 0, c == last)
                        if hi - 1 == last:
                            fills(ins, (stage, nb, tt))
                    release((stage, nb, kg), ins, (stage, nb, tts[-1]) if hi - 1 == last else None)
                    if (nb, kg) in events:
                        mod_reduce(events[(nb, kg)])

            HALVES = [(0, 4), (4, 8)]

            def transposes(key, sources, pool="gemm"):
                bank = take(key, pool)
                for i, src in enumerate(sources):
                    ins = nc.tensor.transpose(bank[0:src.shape[1], i * P:i * P + src.shape[0]], src,
                                              ident[0:src.shape[0], 0:src.shape[0]])
                fills(ins, key)

            def mod_reduce(e):
                pe.wait_ge(mod_acc, e - FIRST_DVE_EVENT + 1)
                acc = modacc[:, e % MODS, :]
                bank = take(("mod", e), "misc")
                if mod_is_row(e):
                    ins = mm(bank[:, :], ones[:, :], acc, True, True)
                else:
                    for j in range(4):
                        ins = mm(bank[:, j:j + 1], acc[:, j * P:(j + 1) * P], ones[:, 0:1], True, True)
                fills(ins, ("mod", e))

            def x_transposes(stage, tok, ready, version):
                for ch in range(KC):
                    if ch == 0:
                        pe.wait_ge(ready, version)
                    transposes((stage, ch), [tok[:, tt, ch * P:(ch + 1) * P] for tt in range(TT)])

            def token_tile(x, c, tt):
                return [x_[:, c, tt * P:(tt + 1) * P] for x_ in x]

            def ffn(name):
                for nb in range(FNB):
                    banks = [take((name, "g", nb)), take((name, "u", nb))]
                    for kg in range(2):
                        if nb == 0:
                            wait_emptied(pe, (name + "_h", kg * PK + PK - 1))
                        w = panel((name + "_in", nb, kg))
                        for half in range(2):
                            for s in range(2):
                                for c in range(PK):
                                    lo = half * 256 + s * P
                                    ins = product(banks[half][:, s * 256:s * 256 + 256],
                                                  [x[:, c, lo:lo + P] for x in w],
                                                  [x[:, kg * PK + c, :] for x in hT], kg == 0 and c == 0 and s == 0,
                                                  kg == 1 and c == PK - 1, skip_group_check=True)
                            if kg == 1:
                                fills(ins, (name, "gu"[half], nb))
                        release((name + "_in", nb, kg), ins, (name, "u", nb) if kg == 1 else None)
                    for e in FFN_EVENTS[name].get(nb, []):
                        mod_reduce(e)
                groups = [(k, min(k + PK, FC)) for k in range(0, FC, PK)]
                for nb in range(2):
                    gemm(name + "_out", lambda tt, c: token_tile(ffT, c, tt), range(TT), nb, NB, groups,
                         OUT_EVENTS[name], inputs=lambda c: ((name, "u", c // 2),))

            pe.wait_ge(table_landed, 16)
            pe.wait_ge(cols_landed, 16 * N_SMALL_LOADS)
            transposes("cols", [colsrc])
            transposes("ln_cols", [lnsrc])
            transposes("pos", [possrc])
            fills(mm(take("srow")[0:REL_HEADS, 0:SROW], rel_sb, oh_sb, True, True), "srow")

            def mod_columns(e):
                wait_emptied(pe, ("modrow", e))
                bank = take(("mod", e), "misc")
                for s in range(4):
                    ins = nc.tensor.transpose(bank[:, 2 * s:2 * s + 2], modacc[0:2, e % MODS, s * P:(s + 1) * P],
                                              ident[0:2, 0:2])
                fills(ins, ("mod", e))

            pe.wait_ge(csil_done, 1)
            for e in range(FIRST_DVE_EVENT):
                pe.wait_ge(mod_landed[e % MODS], 16 * (e // MODS + 1))
                bank = take(("modrow", e))
                for j in range(KC):
                    ins = mm(bank[0:2, :], cs[:, 2 * j:2 * j + 2], modring[e % MODS][:, j, :], j == 0, j == KC - 1)
                fills(ins, ("modrow", e))
                if e:
                    mod_columns(e - 1)
            mod_columns(FIRST_DVE_EVENT - 1)

            x_transposes("lat", x_tok, x_landed, 16)

            for nb in range(6):
                if nb == 2:
                    wait_emptied(pe, ("con", KC - 1))
                gemm("qkv", lambda tt, c: token_tile(conT if tt >= TT else hT, c, tt % TT), range(2 if nb < 2 else 4),
                     nb, NB, HALVES, inputs=lambda c: (("lat", c),))
                if nb == 0:
                    x_transposes("con", y_tok, ctx_landed, 16)
                for e in QKV_EVENTS[nb]:
                    mod_reduce(e)

            for h in range(HEADS):
                pe.wait_ge(rope_done, 6 if h < 4 else 8)
                for tt in (2, 3):
                    wait_emptied(pe, ("qkv", 2 + h // 4, tt))
                transposes(("qT", h), [q_tok[:, tt, h * P:(h + 1) * P] for tt in range(TT)])
                transposes(("kT", h), [k_tok[:, tt, h * P:(h + 1) * P] for tt in range(4)])
            for tt in range(4):
                wait_emptied(pe, ("qkv", 5, tt))

            def scores(u):
                qt, h = UNITS0[u]
                wait_emptied(pe, ("qT", h))
                wait_emptied(pe, ("kT", h))
                for m in range(2):
                    rows = slice(m * HD, (m + 1) * HD)
                    fills(mm(take(("S", u, m))[:, :], qT[rows, h, qt * P:(qt + 1) * P], kT[rows, h, :],
                             True, True), ("S", u, m))

            def turn_probs(u):
                pe.wait_ge(probs_done, u + 1)
                transposes(("PT", u), [prob[:, u % 4, 0, kb * P:(kb + 1) * P] for kb in range(4)])

            def values(u):
                qt, h = UNITS0[u]
                if u % 4 == 0:
                    take(("O", u // 4), "misc")
                o = psum[where[("O", u // 4)][0]]
                wait_emptied(pe, ("PT", u))
                for kb in range(4):
                    ins = mm(o[:, (u % 4) * P:(u % 4 + 1) * P], aT[:, u % 2, kb * P:(kb + 1) * P],
                             v_tok[:, kb, h * P:(h + 1) * P], kb == 0, kb == 3)
                if u % 4 == 3:
                    fills(ins, ("O", u // 4))

            for u in range(AHEAD):
                scores(u)
            for u in range(len(UNITS0)):
                turn_probs(u)
                if u + AHEAD < len(UNITS0):
                    scores(u + AHEAD)
                values(u)

            pe.wait_ge(o_done, 4)
            for h in range(HEADS):
                transposes(("oT", h), [y_tok[:, tt, h * P:(h + 1) * P] for tt in range(TT)])
            for nb in range(2):
                gemm("wo", lambda tt, c: token_tile(hT, c, tt), range(TT), nb, NB, HALVES,
                     inputs=lambda c: (("oT", c),))
            x_transposes("ffn0_h", y_tok, xn_done, 2)
            ffn("ffn0")

            pe.wait_ge(poolm_landed, 16)
            for kt in range(TT):
                pe.wait_ge(hx_done, kt + 1)
                for ch in range(KC):
                    if kt == 0:
                        take(("pl", ch), "gemm" if ch < len(POOLS["gemm"]) else "misc")
                    bank = psum[where[("pl", ch)][0]]
                    ins = mm(bank[:, 0:SEQ], hx_tok[:, kt, ch * P:(ch + 1) * P],
                             pool_m[:, kt * 4 + ch // 2, :], kt == 0, kt == TT - 1)
                    if kt == TT - 1:
                        fills(ins, ("pl", ch))
            wait_emptied(pe, ("pl", KC - 1))
            w, = panel(("pool", 0, 0))
            for nb in range(2):
                for tt in range(TT):
                    bank = take(("poolw", nb, tt))
                    for g in (2 * nb, 2 * nb + 1):
                        for c in range(2):
                            ins = mm(bank[:, (g % 2) * 256:(g % 2) * 256 + 256],
                                     pooledT[:, 2 * g + c, tt * P:(tt + 1) * P], w[:, 2 * g + c, :],
                                     c == 0, c == 1)
                    fills(ins, ("poolw", nb, tt))
            release(("pool", 0, 0), ins, ("poolw", 1, TT - 1))
            x_transposes("ffn1_h", y_tok, xn_done, 4)
            ffn("ffn1")

            x_transposes("z_h", y_tok, xn_done, 6)
            for nb, (lo, hi) in enumerate(Z_BLOCKS):
                gemm("z", lambda tt, c: token_tile(hT, c, tt), range(TT), nb, hi - lo, HALVES,
                     inputs=lambda c: (("z_h", c),))

            pe.wait_ge(dup_done, 1)
            for nb in range(6, len(Z_BLOCKS)):
                for tt in range(TT):
                    wait_emptied(pe, ("z", nb, tt))
            for b0, n in FT_PAIRS:
                if b0 == FT_NORMED[0][0]:
                    pe.wait_ge(zsrc_done, 1)
                    for i in range(4):
                        transposes(("dupT", i), [kdup[:, tt, 6 + i, :] for tt in range(TT)])
                transposes(("ft", b0), [ft_source(b0 + j, tt) for j in range(n) for tt in range(TT)])

            mix_w = {}

            def mix_piece(i):
                b, tt, kg = i // 4, i % 4 // 2, i % 2
                if tt == 0:
                    mix_w[kg] = panel(("mix", b, kg))
                if kg == 0:
                    take(("mix", b, tt), "mix")
                bank = psum[where[("mix", b, tt)][0]]
                for c in range(PK):
                    ins = product(bank[:, :], token_tile(hT, kg * PK + c, tt), [x[:, c, :] for x in mix_w[kg]],
                                  kg == 0 and c == 0, kg == 1 and c == PK - 1)
                if kg == 1:
                    fills(ins, ("mix", b, tt))
                if tt == TT - 1:
                    release(("mix", b, kg), ins, ("mix", b, tt) if kg == 1 else None)

            w, = panel(("cmp", 0, 0))
            pe.wait_ge(xc_done, 1)
            bank = take("cmp")
            for i in range(4):
                kv = i // 2
                for l in range(16):
                    ins = mm(bank[0:N_CMP, i * HD:(i + 1) * HD], xc[:, i, l, :], w[:, kv * 16 + l, :], l == 0, l == 15)
            fills(ins, "cmp")
            release(("cmp", 0, 0), ins, "cmp")
            pe.wait_ge(ckd_done, 1)
            transposes("kcT", [ckd[:, 0, :], ckd[:, 1, :]])
            for b0, _ in FT_PAIRS[-2:]:
                wait_emptied(pe, ("ft", b0))

            for qt in range(TT):
                nk = (qt + 1) * P
                for j in range(2):
                    rows = slice(j * HD, (j + 1) * HD)
                    bank = take(("I", qt, j))
                    for pr in range(2):
                        ins = mm(bank[:, pr * 256:pr * 256 + nk], ft[rows, 5 + pr, qt * P:(qt + 1) * P],
                                 ft[rows, 7, 0:nk], True, True)
                    fills(ins, ("I", qt, j))
            def scores2(u):
                kind, qt, h = UNITS2[u]
                nk = (qt + 1) * P
                rows = slice((h % 2) * HD, (h % 2 + 1) * HD)
                segs = unit_segments(kind, h)
                for s, (qb, kb, _, _) in enumerate(segs):
                    if s % 2 == 0:
                        bank = take(("S2", u, s // 2), "unit")
                    ins = mm(bank[:, (s % 2) * 256:(s % 2) * 256 + nk], ft[rows, qb, qt * P:(qt + 1) * P],
                             ft[rows, kb, 0:nk], True, True)
                    if s % 2 == 1 or s == len(segs) - 1:
                        fills(ins, ("S2", u, s // 2))
                if kind == "B":
                    fills(mm(take(("S2", u, "c"), "unit")[:, 0:N_CMP], ft[rows, segs[0][0], qt * P:(qt + 1) * P],
                             kcT[rows, h // 4, :], True, True), ("S2", u, "c"))

            def turn_probs2(u):
                kind, qt, h = UNITS2[u]
                nblk = (qt + 1) * len(unit_segments(kind, h))
                pe.wait_ge(p_done, u + 1)
                p = lbuf[:, u % 4, :]
                for i in range(0, nblk, 4):
                    transposes(("PT2", u, i // 4), [p[:, b * P:(b + 1) * P] for b in range(i, min(i + 4, nblk))],
                               "unit")
                if kind == "B":
                    transposes(("PT2", u, "c"), [p[:, nblk * P:nblk * P + N_CMP]], "unit")

            def values2(u):
                kind, qt, h = UNITS2[u]
                segs = unit_segments(kind, h)
                nkb = qt + 1
                nblk = nkb * len(segs)
                group = (kind, qt)
                if h == 0:
                    take(("O2",) + group, "misc")
                o = psum[where[("O2",) + group][0]][:, h * HD:(h + 1) * HD]
                for i in range(0, nblk, 4):
                    wait_emptied(pe, ("PT2", u, i // 4))
                last = nblk - 1 if kind != "B" else nblk
                for b in range(nblk):
                    v = z[:, b % nkb, segs[b // nkb][3]:segs[b // nkb][3] + HD]
                    ins = mm(o, pT[:, u % 2, b * P:(b + 1) * P], v, b == 0, b == last)
                if kind == "B":
                    wait_emptied(pe, ("PT2", u, "c"))
                    ins = mm(o, pcT[:, u % 2, :], vcmp[:, h // 4, :], False, True)
                if h == (3 if kind == "C" else 7):
                    fills(ins, ("O2",) + group)

            for u in range(AHEAD):
                scores2(u)
            for u in range(len(UNITS2)):
                turn_probs2(u)
                if u + AHEAD < len(UNITS2):
                    scores2(u + AHEAD)
                for i in MIX_AT[u]:
                    mix_piece(i)
                values2(u)

            for kind, n in (("A", 4), ("B", 4), ("C", 2)):
                for qt in range(TT):
                    wait_emptied(pe, ("O2", kind, qt))
                for i in range(n):
                    transposes(("oT2", kind, i), [o2_tok(kind, qt)[:, i * P:(i + 1) * P] for qt in range(TT)])
            wait_emptied(pe, ("oT2", "C", 1))
            for nb in range(2):
                for br in range(3):
                    n = 2 if br == 2 else 4
                    gemm(f"branch{br}", lambda tt, c: token_tile([oT2], 4 * br + c, tt), range(TT), nb, NB,
                         [(0, n)])
            x_transposes("mixed", y_tok, mix_done, 1)
            for nb in range(2):
                gemm("w_out", lambda tt, c: token_tile(hT, c, tt), range(TT), nb, NB, HALVES,
                     inputs=lambda c: (("mixed", c),))
            x_transposes("ffn2_h", y_tok, xn_done, 8)
            ffn("ffn2")
            assert next_panel[0] == len(panels)

        @block.scalar
        def _(act):
            def split_hi(i):
                wait_hi_free(act, i)
                wait_landed(act, i)
                nc.scalar.activation(panel_part(i, 0), raw_panel(i), ACT.Copy).then_inc(w_hi, 1)

            split_to = splitter(split_hi)

            def highs(stage, dst, func, kw=lambda ch: {}, chunks=range(KC), at=0):
                for ch in chunks:
                    if func == ACT.Identity and ch % 2 == 0:
                        nc.scalar.activation(whole[:, at + ch, :], result(act, (stage, ch))[:, 0:SEQ], func, **kw(ch))
                    nc.scalar.activation(dst[:, ch, :], result(act, (stage, ch))[:, 0:SEQ], func, **kw(ch))\
                        .then_inc(h_hi, 1)

            def shifted(shift, scale):
                return lambda ch: dict(bias=modcol[:, shift, ch:ch + 1], scale=modcol[:, scale, ch:ch + 1])

            def row_load(dst, src, sem_):
                act.dma_start(dst, src.partition_broadcast(P)).then_inc(sem_, 16)

            def bias_row(dst, l, comp, sem_):
                row_load(dst, a["b_mod"][l, comp * D:(comp + 1) * D], sem_)

            def ln_load(n):
                act.wait_ge(ln_used, n)
                for i, w in enumerate(("ln_g", "ln_b")):
                    row_load(ln_rows[:, i, :], a[w][n // 2, n % 2, :], ln_landed)

            act.dma_start(cs_in[:, 0, :], a["c"].rearrange("a (p j) -> p (a j)", p=P)).then_inc(c_landed, 16)
            act.dma_start(cs_in[:, 1, :], a["c_ctx"].rearrange("(p j) -> p j", p=P)).then_inc(c_landed, 16)
            act.wait_ge(c_landed, 32)
            nc.scalar.activation(cs[:, :].rearrange("p (j c) -> p c j", c=2), cs_in, ACT.Silu).then_inc(csil_done, 1)
            act.wait_ge(lam_sum, 1)
            nc.scalar.activation(lam[:, 2:4], lam[:, 0:2], ACT.Exp).then_inc(lam_exp, 1)

            for e in range(4):
                wait_emptied(act, ("mod", e))
            highs("lat", hT[0], ACT.Identity, shifted(0, 1), range(PK))
            split_to(0)
            highs("lat", hT[0], ACT.Identity, shifted(0, 1), range(PK, KC))
            split_to(1)

            for nb in range(6):
                split_to(last_panel("qkv", nb) + 2)
                for tt in range(2 if nb < 2 else 4):
                    dst = (q_tok, k_tok, v_tok)[nb // 2][:, tt, (nb % 2) * NB:(nb % 2) * NB + NB]
                    empties(nc.scalar.activation(dst, result(act, ("qkv", nb, tt))[:, :], ACT.Copy),
                            ("qkv", nb, tt))
                if nb == 0:
                    highs("con", conT[0], ACT.Identity, shifted(2, 3), at=KC)
            for h in range(HEADS):
                empties(nc.scalar.activation(kT[:, h, :], result(act, ("kT", h))[:, :], ACT.Copy), ("kT", h))

            act.wait_ge(srow_done, 1)
            act.dma_start(scratch, srow[:, :].unsqueeze(1).broadcast_to([REL_HEADS, P, SROW])).then_inc(srow_stored, 16)
            def exps(u):
                act.wait_ge(nmax_done, u + 1)
                if u > AHEAD:
                    b, n = where[("PT", u - AHEAD - 1)]
                    act.wait_ge(filled[b], n)
                for m in range(2):
                    ins = nc.scalar.activation(prob[:, u % 4, m, :], result(act, ("S", u, m))[:, :], ACT.Exp,
                                               bias=small[:, 8 * (u % 4) + m:8 * (u % 4) + m + 1], scale=HD ** -0.5,
                                               accum_out=small[:, 8 * (u % 4) + 2 + m:8 * (u % 4) + 3 + m])
                    empties(ins, ("S", u, m))

            for u in range(AHEAD):
                exps(u)
            for u in range(len(UNITS0)):
                bank = result(act, ("PT", u))
                empties(nc.scalar.activation(aT[:, u % 2, :], bank[:, :], ACT.Copy), ("PT", u))
                if u + AHEAD < len(UNITS0):
                    exps(u + AHEAD)
                if u % 4 == 3:
                    b = result(act, ("O", u // 4))
                    if u // 4:
                        act.wait_ge(o_done, u // 4)
                    nc.scalar.activation(tmp[:, 0, :], b[:, :], ACT.Square).then_inc(sq_done, 1)
            highs("oT", hT[0], ACT.Copy, lambda ch: dict(scale=cols[:, COL_SUB:COL_SUB + 1]))
            for comp in range(2):
                bias_row(mod_rows[:, comp, :], 1, comp, rows_landed)
            act.dma_start(pool_m, a["const_pool"].rearrange("p (a b) -> p a b", a=TT * 4)).then_inc(poolm_landed, 16)
            row_load(pscale, a["pool_scale"][0], psc_landed)
            split_to(last_panel("wo", 1) + 2)

            def gain(col):
                return lambda ch: dict(scale=cols[:, col + ch:col + ch + 1])

            def ffn(name):
                for nb in range(FNB):
                    split_to(last_panel(name + "_in", nb) + 2)
                    if name == "ffn0" and nb == 2:
                        act.wait_ge(g1_used, 1)
                        bias_row(g1row, 1, 2, g_landed[2])
                        ln_load(1)
                    if name == "ffn1" and nb == 2:
                        ln_load(3)
                    bank = result(act, (name, "g", nb))
                    if nb >= 2:
                        wait_emptied(act, (name, "u", nb - 2))
                    empties(nc.scalar.activation(tmp[:, nb % 2, :], bank[:, :], ACT.Silu), (name, "g", nb))
                split_to(last_panel(name + "_out", 1) + 2)

            highs("ffn0_h", hT[0], ACT.Identity, shifted(4, 5))
            ffn("ffn0")
            for ch in range(KC):
                empties(nc.scalar.activation(pooledT[:, ch, :], result(act, ("pl", ch))[:, 0:SEQ], ACT.Copy),
                        ("pl", ch))
            act.wait_ge(g2_used, 1)
            bias_row(g2row, 1, 5, g_landed[5])
            ln_load(2)
            split_to(last_panel("pool", 0) + 2)
            highs("ffn1_h", hT[0], ACT.Identity, shifted(6, 7))
            ffn("ffn1")

            def sum_squares(n):
                for tt in range(TT):
                    act.wait_ge(x_done, n + tt + 1)
                    nc.scalar.activation(y_tok[:, tt, :], x_tok[:, tt, :], ACT.Square,
                                         accum_out=small[:, 20 + tt:21 + tt]).then_inc(ssq_done, 1)

            highs("z_h", hT[0], ACT.Identity, lambda ch: dict(bias=ln_cols[:, 5, ch:ch + 1],
                                                              scale=ln_cols[:, 4, ch:ch + 1]))
            sum_squares(0)
            for nb, (lo, hi) in enumerate(Z_BLOCKS):
                split_to(last_panel("z", nb) + (2 if nb < len(Z_BLOCKS) - 1 else 0))
                if nb == 0:
                    act.wait_ge(rstd_done, ROOTS_BEFORE_Z)
                for tt in range(TT):
                    empties(nc.scalar.activation(z[:, tt, lo:hi], result(act, ("z", nb, tt))[:, 0:hi - lo], ACT.Copy,
                                                 scale=rms_z[:, tt:tt + 1]),
                            ("z", nb, tt))
                if nb == 4:
                    for tt in range(TT):
                        wait_emptied(act, ("z", 4, tt))
                        g = v3(z[:, tt, BG:BG + 24], 8)
                        nc.scalar.activation(gates[:, tt, :, 0:2], g[:, :, 1:3], ACT.Sigmoid).then_inc(gates_done, 1)
                        nc.scalar.activation(gates[:, tt, :, 2:3], g[:, :, 0:1], ACT.Sigmoid).then_inc(gates_done, 1)
            for b0, n in FT_PAIRS:
                if b0 in FT_ON_ACT:
                    src = v3(result(act, ("ft", b0))[:, 0:n * SEQ], n)
                    if b0 in FT_GAIN:
                        g = COL_QK + FT_GAIN[b0]
                        ins = nc.scalar.activation(ft[:, b0:b0 + n, :], src, ACT.Copy, scale=cols[:, g:g + 1])
                    else:
                        ins = nc.scalar.activation(ft[:, b0:b0 + n, :], src, ACT.Copy)
                    empties(ins, ("ft", b0))
                if b0 == FT_PLAIN[-1][0]:
                    split_to(panel_at[("mix", 0, 1)])

            def mix_out(i):
                b, tt = i // 4, i % 4 // 2
                bank = result(act, ("mix", b, tt))
                for zc, lo, n in MIX_Z[b]:
                    ins = nc.scalar.activation(z[:, tt, zc:zc + n], bank[:, lo:lo + n], ACT.Copy,
                                               scale=rms_z[:, tt:tt + 1])
                empties(ins, ("mix", b, tt))

            for qt in range(TT):
                nk = (qt + 1) * P
                for j in range(2):
                    bank = result(act, ("I", qt, j))
                    if j == 0 and qt > 0:
                        act.wait_ge(rel_used, qt)
                    ins = nc.scalar.activation(rel[:, j:4:2, 0:nk], v3(bank[:, :], 2)[:, :, 0:nk], ACT.Relu)
                    empties(ins, ("I", qt, j))

            def exps2(u):
                kind, qt, h = UNITS2[u]
                nk = (qt + 1) * P
                act.wait_ge(l_done, u + 1)
                o = 64 + 16 * (u % 4)
                parts = [(0, nk), (nk, 2 * nk), (2 * nk, 2 * nk + N_CMP)] if kind == "B" else \
                        [(0, nk * (3 if kind == "C" else 1))]
                for i, (lo, hi) in enumerate(parts):
                    ins = nc.scalar.activation(lbuf[:, u % 4, lo:hi], lbuf[:, u % 4, lo:hi], ACT.Exp,
                                               bias=small[:, o + i:o + i + 1],
                                               accum_out=small[:, o + 4 + i:o + 5 + i])
                ins.then_inc(exp2_done, 1)

            for u in range(AHEAD):
                exps2(u)
            for u, (kind, qt, h) in enumerate(UNITS2):
                nblk = (qt + 1) * len(unit_segments(kind, h))
                for i in range(0, nblk, 4):
                    n = min(4, nblk - i)
                    empties(nc.scalar.activation(pT[:, u % 2, i * P:(i + n) * P],
                                                 result(act, ("PT2", u, i // 4))[:, 0:n * P], ACT.Copy),
                            ("PT2", u, i // 4))
                if kind == "B":
                    empties(nc.scalar.activation(pcT[:, u % 2, :], result(act, ("PT2", u, "c"))[0:N_CMP, 0:P], ACT.Copy),
                            ("PT2", u, "c"))
                for i in MIX_AT[u - 1] if u else ():
                    if i % 4 >= 2:
                        split_to(panel_at[("mix", i // 4, i % 2)] + PARTS)
                if u + AHEAD < len(UNITS2):
                    exps2(u + AHEAD)
                for i in MIX_AT[u]:
                    if i % 2 == 1:
                        mix_out(i)
            for kind, n in (("A", 4), ("B", 4), ("C", 2)):
                for i in range(n):
                    empties(nc.scalar.activation(oT2[:, {"A": 0, "B": 4, "C": 8}[kind] + i, :],
                                                 result(act, ("oT2", kind, i))[:, 0:SEQ], ACT.Copy), ("oT2", kind, i))
            i = 0
            for nb in range(2):
                for br in range(3):
                    for tt in range(TT):
                        wait_emptied(act, ("mix", nb * 3 + br, tt))
                        if i >= 2:
                            n2, b2 = divmod(i - 2, 6)
                            wait_emptied(act, (f"branch{b2 // 2}", n2, b2 % 2))
                        for zc, lo, n in MIX_Z[nb * 3 + br]:
                            ins = nc.scalar.activation(tmp[:, i % 2, lo:lo + n], z[:, tt, zc:zc + n], ACT.Sigmoid)
                        ins.then_inc(sig_done, 1)
                        i += 1
            split_to(last_panel("branch2", 1) + 2)
            highs("mixed", hT[0], ACT.Copy)
            split_to(last_panel("w_out", 1) + 2)
            sum_squares(TT)
            highs("ffn2_h", hT[0], ACT.Copy, gain(COL_N2))
            ffn("ffn2")

        @block.vector
        def _(dve):
            steps = [0]
            V = nc.vector

            def step(ins):
                ins.then_inc(dve_step, 1)
                steps[0] += 1

            def settle():
                dve.wait_ge(dve_step, steps[0])

            def half_lo(i):
                if not lo_by_pool[i]:
                    half = slice(0, panels[i][2] // 2)
                    wait_split(dve, i, hi_only=True)
                    V.tensor_tensor(panel_part(i, 1)[:, half, :], raw_panel(i)[:, half, :],
                                    panel_part(i, 0)[:, half, :].bitcast(F32), ALU.subtract).then_inc(w_lo, 1)

            split_to = splitter(half_lo)
            highs = [0]

            def lows(stage, dst, shift=None, scale=None, chunks=range(KC), at=0):
                for ch in chunks:
                    bank = result(dve, (stage, ch))
                    highs[0] += 1
                    dve.wait_ge(h_hi, highs[0])
                    full = whole[:, at + ch, :]
                    if shift is not None and ch % 2:
                        step(V.tensor_scalar(full, bank[:, 0:SEQ], scale(ch), shift(ch), ALU.mult, ALU.add))
                        settle()
                    hi = dst[0][:, ch, :].bitcast(F32)
                    if shift is not None:
                        ins = V.tensor_tensor(dst[1][:, ch, :], full, hi, ALU.subtract)
                    elif scale is not None:
                        ins = V.scalar_tensor_tensor(dst[1][:, ch, :], bank[:, 0:SEQ], scale(ch), hi,
                                                     ALU.mult, ALU.subtract)
                    else:
                        ins = V.tensor_tensor(dst[1][:, ch, :], bank[:, 0:SEQ], hi, ALU.subtract)
                    empties(ins, (stage, ch))

            def mod_col(slot):
                return lambda ch: modcol[:, slot, ch:ch + 1]

            def gain(col):
                return lambda ch: cols[:, col + ch:col + ch + 1]

            step(V.memset(ones[:, :], 1.0))
            V.memset(neghalf[:, :], -0.5).then_inc(consts_done, 1)
            bank = result(dve, "cols")
            empties(V.tensor_copy(cols[:, :], bank[:, 0:N_COLS]), "cols")
            wait_emptied(dve, "cols")
            step(V.tensor_scalar(cols[:, COL_SUB:COL_SUB + 1], cols[:, COL_SUB:COL_SUB + 1], 1.0 - LAM_INIT, None,
                                 ALU.mult))
            empties(V.tensor_copy(ln_cols, v3(result(dve, "ln_cols")[:, 0:6 * KC], 6)), "ln_cols")
            empties(V.tensor_copy(posT[:, :], result(dve, "pos")[:, 0:32]), "pos")
            bank = result(dve, "srow")
            empties(V.tensor_tensor(srow[:, :], bank[0:REL_HEADS, 0:SROW], rm_sb, ALU.add), "srow")
            wait_emptied(dve, "srow")
            V.memset(lam[:, 7:8], 0.0).then_inc(srow_done, 1)

            dve.wait_ge(lam_landed, 16)
            lp = small[:, 128:256]
            step(V.tensor_tensor(v3(lp, 2), lam_in[:, 0:4:2, :], lam_in[:, 1:4:2, :], ALU.mult))
            settle()
            V.tensor_reduce(lam[:, 0:2], v3(lp, 2), AX, ALU.add).then_inc(lam_sum, 1)
            dve.wait_ge(lam_exp, 1)
            step(V.tensor_tensor(lam[:, 4:5], lam[:, 3:4], lam[:, 2:3], ALU.subtract))
            settle()
            step(V.tensor_scalar(lam[:, 5:6], lam[:, 4:5], -LAM_INIT, None, ALU.add))

            def mod_row(e):
                empties(V.tensor_copy(modacc[0:2, e % MODS, :], result(dve, ("modrow", e))[0:2, :]), ("modrow", e))

            mod_row(0)
            for e in range(FIRST_DVE_EVENT):
                if e + 1 < FIRST_DVE_EVENT:
                    mod_row(e + 1)
                comp, half = divmod(e, 2)
                src = result(dve, ("mod", e))[:, 0:8].rearrange("p (s c) -> p c s", c=2)
                bcol = cols[:, COL_BMOD + comp * KC + half * 4:COL_BMOD + comp * KC + half * 4 + 4]
                step(V.scalar_tensor_tensor(modcol[:, comp, half * 4:half * 4 + 4], src[:, 0, :], float(comp),
                                            bcol, ALU.add, ALU.add))
                empties(V.scalar_tensor_tensor(modcol[:, 2 + comp, half * 4:half * 4 + 4], src[:, 1, :],
                                               float(comp), bcol, ALU.add, ALU.add), ("mod", e))
            wait_emptied(dve, ("mod", 2))
            wait_emptied(dve, ("mod", 3))
            lows("lat", hT, mod_col(0), mod_col(1), range(PK))
            split_to(0)
            lows("lat", hT, mod_col(0), mod_col(1), range(PK, KC))
            split_to(1)

            def mod_product(e, js=range(KC)):
                if e >= N_EVENTS:
                    return
                if js[0] == 0:
                    dve.wait_ge(mod_landed[e % MODS], 16 * (e // MODS + 1))
                    if e - MODS >= FIRST_DVE_EVENT:
                        result(dve, ("mod", e - MODS))
                acc = modacc[:, e % MODS, :]
                w = modring[e % MODS]
                for j in js:
                    c = cs[:, 2 * j:2 * j + 1]
                    if j == 0:
                        ins = V.tensor_scalar(acc, w[:, j, :], c, None, ALU.mult)
                    else:
                        settle()
                        ins = V.scalar_tensor_tensor(acc, w[:, j, :], c, acc, ALU.mult, ALU.add)
                    if j < KC - 1:
                        step(ins)
                    else:
                        ins.then_inc(mod_acc, 1)

            def mod_finish(e):
                comp, half = divmod(e % 12, 2)
                cols_ = slice(half * NB, half * NB + NB)
                bank = result(dve, ("mod", e))
                if mod_is_row(e):
                    if comp in (0, 1):
                        dst = mod_rows[:, comp, cols_]
                        dve.wait_ge(rows_landed, 32)
                    else:
                        dst = (g1row if comp == 2 else g2row)[:, cols_]
                        dve.wait_ge(g_landed[comp], 16 * (e // 12 + 1))
                    ins = V.scalar_tensor_tensor(dst, bank[:, :], 1.0 if comp == 1 else 0.0, dst, ALU.add, ALU.add)
                else:
                    slot = (4 if e < 12 else 6) + comp - 3
                    b0 = COL_BMOD + (e // 12) * 48 + comp * KC + half * 4
                    ins = V.scalar_tensor_tensor(modcol[:, slot, half * 4:half * 4 + 4], bank[:, 0:4],
                                                 1.0 if comp == 4 else 0.0, cols[:, b0:b0 + 4], ALU.add, ALU.add)
                empties(ins, ("mod", e))

            dve.wait_ge(csil_done, 1)
            mod_product(4)
            for nb in range(6):
                split_to(last_panel("qkv", nb) + 2)
                if nb < 4:
                    for tt in range(TT):
                        buf = (q_tok if nb < 2 else k_tok)[:, tt, (nb % 2) * NB:(nb % 2) * NB + NB]
                        wait_emptied(dve, ("qkv", nb, tt))
                        pairs = buf.rearrange("p (h s d) -> p h s d", s=2, d=HD // 2)
                        t0 = tmp[:, 0, :].rearrange("p (h n) -> p h n", n=HD)
                        t1 = tmp[:, 1, :].rearrange("p (h s d) -> p h s d", s=2, d=HD // 2)
                        cos2 = rope[:, 2 * tt, :].unsqueeze(1).broadcast_to([P, 8, HD])
                        sin2 = rope[:, 2 * tt + 1, :]
                        settle()
                        step(V.tensor_tensor(t0, buf.rearrange("p (h n) -> p h n", n=HD), cos2, ALU.mult))
                        for s in range(2):
                            sn = sin2[:, s * 32:(s + 1) * 32].unsqueeze(1).broadcast_to([P, 8, 32])
                            step(V.tensor_tensor(t1[:, :, s, :], pairs[:, :, 1 - s, :], sn, ALU.mult))
                        settle()
                        V.tensor_tensor(buf, tmp[:, 0, :], tmp[:, 1, :], ALU.add).then_inc(rope_done, 1)
                        dve.wait_ge(rope_done, 2 * nb + tt + 1)
                if nb == 0:
                    lows("con", conT, mod_col(2), mod_col(3), at=KC)
                    mod_product(5)
                for e in QKV_EVENTS[nb]:
                    mod_finish(e)
                    mod_product(e + 2)
            for h in range(HEADS):
                empties(V.tensor_copy(qT[:, h, :], result(dve, ("qT", h))[:, 0:SEQ]), ("qT", h))

            def maxima(u):
                s = 8 * (u % 4)
                for m in range(2):
                    step(V.tensor_reduce(small[:, s + 4 + m:s + 5 + m], result(dve, ("S", u, m))[:, :], AX, ALU.max))
                settle()
                V.tensor_scalar(small[:, s:s + 2], small[:, s + 4:s + 6], -HD ** -0.5, None, ALU.mult)\
                    .then_inc(nmax_done, 1)

            def combine(u):
                s = 8 * (u % 4)
                wait_emptied(dve, ("S", u, 0))
                wait_emptied(dve, ("S", u, 1))
                step(V.reciprocal(small[:, s + 6:s + 8], small[:, s + 2:s + 4]))
                settle()
                step(V.tensor_scalar(small[:, 44:45], small[:, s + 7:s + 8], lam[:, 5:6], None, ALU.mult))
                settle()
                p0, p1 = prob[:, u % 4, 0, :], prob[:, u % 4, 1, :]
                step(V.tensor_scalar(p1, p1, small[:, 44:45], None, ALU.mult))
                settle()
                V.scalar_tensor_tensor(p0, p0, small[:, s + 6:s + 7], p1, ALU.mult, ALU.add).then_inc(probs_done, 1)

            rstds, xns = [0], [0]

            def inverse_root():
                rstds[0] += 1
                dve.wait_ge(rstd_done, rstds[0])

            def head_var(g):
                dve.wait_ge(sq_done, g + 1)
                step(V.tensor_reduce(small[:, 36:40], v3(tmp[:, 0, :], 4), AX, ALU.add))
                settle()
                V.tensor_scalar(small[:, 40:44], small[:, 36:40], 1.0 / P, LN_EPS, ALU.mult, ALU.add)\
                    .then_inc(var_done, 1)

            def head_norm(g):
                inverse_root()
                r = small[:, 32:36]
                qt, h0 = UNITS0[4 * g]
                ins = V.tensor_tensor(v3(y_tok[:, qt, h0 * P:(h0 + 4) * P], 4), v3(result(dve, ("O", g))[:, :], 4),
                                      r.unsqueeze(2).broadcast_to([P, 4, P]), ALU.mult)
                empties(ins, ("O", g))
                wait_emptied(dve, ("O", g))
                V.memset(small[:, 47:48], 0.0).then_inc(o_done, 1)

            for u in range(AHEAD):
                maxima(u)
            combine(0)
            for u in range(len(UNITS0)):
                if u + 1 < len(UNITS0):
                    combine(u + 1)
                if u + AHEAD < len(UNITS0):
                    maxima(u + AHEAD)
                if u and u % 4 == 0:
                    head_var(u // 4 - 1)
                if u > 1 and u % 4 == 1:
                    head_norm(u // 4 - 1)
            head_var(3)
            head_norm(3)
            lows("oT", hT, None, lambda ch: cols[:, COL_SUB:COL_SUB + 1])

            def residual_stats(stage, gate, used, events={}, late=lambda: None):
                for nb in range(2):
                    last = last_panel("pool", 0) if stage == "poolw" else last_panel(stage, nb)
                    for (n, kg), e in events.items():
                        if n == nb:
                            split_to(panel_at[(stage, nb, kg)] + 2)
                            mod_finish(e)
                            mod_product(e + 2)
                    if nb == 1:
                        late()
                    split_to(last + (2 if nb == 0 and stage != "poolw" else 1))
                    for tt in range(TT):
                        sl = slice(nb * NB, nb * NB + NB)
                        y = y_tok[:, tt, sl]
                        empties(V.tensor_tensor(y, result(dve, (stage, nb, tt))[:, :], gate[:, sl], ALU.mult),
                                (stage, nb, tt))
                        wait_emptied(dve, (stage, nb, tt))
                        step(V.scalar_tensor_tensor(y, x_tok[:, tt, sl], ALPHA, y, ALU.mult, ALU.add))
                        settle()
                        st = small[:, 100 + 12 * tt + 6 * nb:106 + 12 * tt + 6 * nb]
                        step(V.bn_stats(st, y))
                settle()
                for tt in range(TT):
                    step(V.bn_aggr(small[:, 124 + 2 * tt:126 + 2 * tt], small[:, 100 + 12 * tt:112 + 12 * tt]))
                settle()
                V.tensor_scalar(small[:, 24:26], small[:, 125:129:2], LN_EPS, None, ALU.add).then_inc(var_done, 1)
                V.memset(small[:, 47:48], 0.0).then_inc(used, 1)
                split_to(last + 2)
                inverse_root()

            def mean(tt):
                return small[:, 124 + 2 * tt:125 + 2 * tt]

            def rstd(tt):
                return small[:, 32 + tt:33 + tt]

            def normalise():
                for tt in range(TT):
                    V.tensor_scalar(y_tok[:, tt, :], y_tok[:, tt, :], mean(tt), rstd(tt),
                                    ALU.subtract, ALU.mult).then_inc(xn_done, 1)
                    xns[0] += 1

            def affine(dst, tt, gain_row, bias_row):
                step(V.scalar_tensor_tensor(dst, y_tok[:, tt, :], mean(tt), gain_row, ALU.subtract, ALU.mult))
                settle()
                return V.scalar_tensor_tensor(dst, dst, rstd(tt), bias_row, ALU.mult, ALU.add)

            def x_from_normalised(ln, signal=None):
                dve.wait_ge(xn_done, xns[0])
                dve.wait_ge(ln_landed, 32 * (ln + 1))
                for tt in range(TT):
                    step(V.tensor_tensor(x_tok[:, tt, :], y_tok[:, tt, :], ln_rows[:, 0, :], ALU.mult))
                for tt in range(TT):
                    settle()
                    ins = V.tensor_tensor(x_tok[:, tt, :], x_tok[:, tt, :], ln_rows[:, 1, :], ALU.add)
                    if signal is None:
                        step(ins)
                    else:
                        ins.then_inc(signal, 1)
                settle()
                V.memset(small[:, 47:48], 0.0).then_inc(ln_used, 1)

            def fold_norm(slot, l):
                shift, scale = modcol[:, slot, :], modcol[:, slot + 1, :]
                t = small[:, 240:248]
                for e in (12 * l + 6, 12 * l + 7, 12 * l + 8, 12 * l + 9):
                    wait_emptied(dve, ("mod", e))
                settle()
                step(V.tensor_tensor(t, ln_cols[:, 2 * l + 1, :], scale, ALU.mult))
                settle()
                step(V.tensor_tensor(shift, shift, t, ALU.add))
                step(V.tensor_tensor(scale, scale, ln_cols[:, 2 * l, :], ALU.mult))

            def fold_rows(half, t):
                sl = slice(half * NB, half * NB + NB)
                shift, scale = mod_rows[:, 0, sl], mod_rows[:, 1, sl]
                dve.wait_ge(ln_landed, 32 * 2)
                for e in (12 + half, 14 + half):
                    wait_emptied(dve, ("mod", e))
                step(V.tensor_tensor(t, ln_rows[:, 1, sl], scale, ALU.mult))
                settle()
                step(V.tensor_tensor(shift, shift, t, ALU.add))
                return V.tensor_tensor(scale, scale, ln_rows[:, 0, sl], ALU.mult)

            def ffn(name):
                for nb in range(FNB):
                    split_to(panel_at[(name + "_in", nb, 0)] + 2)
                    for e in FFN_EVENTS[name].get(nb - 1, []):
                        mod_product(e + 2, range(PK, KC))
                    split_to(last_panel(name + "_in", nb) + 2)
                    wait_emptied(dve, (name, "g", nb))
                    bank = result(dve, (name, "u", nb))
                    t = tmp[:, nb % 2, :]
                    step(V.tensor_tensor(t, t, bank[:, :], ALU.mult))
                    settle()
                    hi, lo = (x[:, 2 * nb:2 * nb + 2, :] for x in ffT)
                    step(V.tensor_copy(hi, v3(t, 2)))
                    settle()
                    ins = V.tensor_tensor(lo, v3(t, 2), hi.bitcast(F32), ALU.subtract)
                    if name == "ffn0" and nb in (8, 9):
                        step(ins)
                        settle()
                        ins = fold_rows(nb - 8, t)
                    empties(ins, (name, "u", nb))
                    for e in FFN_EVENTS[name].get(nb, []):
                        mod_finish(e)
                        mod_product(e + 2, range(KC if nb == FNB - 1 else PK))

            fold_norm(4, 0)
            residual_stats("wo", g1row, g1_used)
            normalise()
            lows("ffn0_h", hT, mod_col(4), mod_col(5))
            x_from_normalised(0)
            ffn("ffn0")
            dve.wait_ge(psc_landed, 16)
            wait_emptied(dve, ("mod", 16))
            wait_emptied(dve, ("mod", 17))
            step(V.tensor_tensor(g1row, g1row, pscale, ALU.mult))
            residual_stats("ffn0_out", g2row, g2_used, OUT_EVENTS["ffn0"], lambda: fold_norm(6, 1))

            for tt in range(TT):
                affine(hx_tok[:, tt, :], tt, mod_rows[:, 1, :], mod_rows[:, 0, :]).then_inc(hx_done, 1)
            for tt in range(TT):
                step(affine(x_tok[:, tt, :], tt, ln_rows[:, 0, :], ln_rows[:, 1, :]))
            settle()
            V.memset(small[:, 47:48], 0.0).then_inc(ln_used, 1)
            residual_stats("poolw", g1row, g1_used)
            normalise()
            lows("ffn1_h", hT, mod_col(6), mod_col(7))
            x_from_normalised(2)
            ffn("ffn1")
            g1 = cols[:, COL_N1:COL_N1 + KC]
            step(V.tensor_tensor(ln_cols[:, 4, :], ln_cols[:, 4, :], g1, ALU.mult))
            step(V.tensor_tensor(ln_cols[:, 5, :], ln_cols[:, 5, :], g1, ALU.mult))
            residual_stats("ffn1_out", g2row, g2_used)
            normalise()
            lows("z_h", hT, lambda ch: ln_cols[:, 5, ch:ch + 1], lambda ch: ln_cols[:, 4, ch:ch + 1])
            x_from_normalised(3, x_done)

            def mean_square(n):
                dve.wait_ge(ssq_done, n)
                V.tensor_scalar(small[:, 24:26], small[:, 20:22], 1.0 / D, RMS_EPS, ALU.mult, ALU.add)\
                    .then_inc(var_done, 1)
                inverse_root()

            split_to(last_panel("z", 0) + 1)
            mean_square(TT)

            def rms_input(n):
                mean_square(n)
                for tt in range(TT):
                    V.tensor_scalar(y_tok[:, tt, :], x_tok[:, tt, :], rstd(tt), None, ALU.mult)\
                        .then_inc(xn_done, 1)

            scr = tmp[:, :, :].rearrange("p a b -> p (a b)")

            def squares(col, heads, idx, meanwhile=0):
                for tt in range(TT):
                    zz = z[:, tt, col:col + heads * HD]
                    settle()
                    step(V.tensor_tensor(scr[:, 0:heads * HD], zz, zz, ALU.mult))
                    settle()
                    step(V.tensor_reduce(ss[:, tt, idx:idx + heads], v3(scr[:, 0:heads * HD], heads), AX, ALU.add))
                    split_to(meanwhile)

            def after_block(nb):
                split_to(last_panel("z", nb) + 2)
                wait_emptied(dve, ("z", nb, 0))
                wait_emptied(dve, ("z", nb, 1))

            def mean_squares(lo, hi):
                settle()
                V.tensor_scalar(ss[:, :, lo:hi], ss[:, :, lo:hi], 1.0 / HD, RMS_EPS, ALU.mult, ALU.add)\
                    .then_inc(var_done, 1)

            after_block(0)
            squares(AQ, 8, SS_AQ)
            after_block(1)
            squares(AK, 1, SS_AK)
            for tt in range(TT):
                step(V.tensor_copy(v3(kdup[:, tt, 1, :], 2), z[:, tt, IK:IK + HD].unsqueeze(1).broadcast_to([P, 2, HD])))
            after_block(2)
            squares(BQ, 8, SS_BQ)
            after_block(3)
            squares(BKS, 2, SS_KS)
            for tt in range(TT):
                src = z[:, tt, BKC:BKC + 4 * HD].rearrange("p (b n) -> p b n", b=4)
                step(V.tensor_copy(kdup[:, tt, 6:10, :].rearrange("p b (s n) -> p b s n", s=2),
                                   src.unsqueeze(2).broadcast_to([P, 4, 2, HD])))
            settle()
            V.memset(small[:, 47:48], 0.0).then_inc(dup_done, 1)
            after_block(4)
            squares(BKW, 2, SS_KW)
            mean_squares(0, SS_CQ)
            after_block(5)
            after_block(6)
            squares(CQ, 12, SS_CQ, last_panel("z", 7) + 1)
            mean_squares(SS_CQ, SS_CK)
            after_block(7)
            squares(CK, 12, SS_CK, last_panel("z", 8) + 1)
            mean_squares(SS_CK, SS_N)
            after_block(8)
            rstds[0] += len(SS_PARTS)
            dve.wait_ge(rstd_done, rstds[0])
            for tt in range(TT):
                for idx, col, slot in ((SS_AK, AK, 0), (SS_KS, BKS, 2), (SS_KS + 1, BKS + HD, 3),
                                       (SS_KW, BKW, 4), (SS_KW + 1, BKW + HD, 5)):
                    step(V.tensor_scalar(v3(kdup[:, tt, slot, :], 2),
                                         z[:, tt, col:col + HD].unsqueeze(1).broadcast_to([P, 2, HD]),
                                         rs[:, tt, idx:idx + 1], None, ALU.mult))
                ck = v3(z[:, tt, CK:CK + 768], 12)
                step(V.tensor_tensor(ck, ck, rs[:, tt, SS_CK:SS_CK + 12].unsqueeze(2).broadcast_to([P, 12, HD]),
                                     ALU.mult))
            settle()
            V.tensor_scalar(small[:, 224:224 + 2 * SS_N], small[:, 224:224 + 2 * SS_N], HD ** -0.5, None, ALU.mult)\
                .then_inc(zsrc_done, 1)

            split_to(last_panel("z", 9) + 2)
            for i in range(4):
                bank = result(dve, ("dupT", i))
                for half in range(2):
                    rows = slice(half * HD, (half + 1) * HD)
                    for lo in range(2):
                        win = bank[rows, lo * CMP_STRIDE:lo * CMP_STRIDE + N_CMP * CMP_STRIDE]
                        win = win.rearrange("p (n l j) -> p j l n", l=8, j=2)[:, half, :, :]
                        pos = posT[rows, (i // 2) * 16 + lo * 8:(i // 2) * 16 + lo * 8 + 8]
                        ins = V.tensor_tensor(xc[rows, i, lo * 8:lo * 8 + 8, :], win,
                                              pos.unsqueeze(2).broadcast_to([HD, 8, N_CMP]), ALU.add)
                        if half == 1 and lo == 1:
                            empties(ins, ("dupT", i))
                        else:
                            step(ins)
            wait_emptied(dve, ("dupT", 3))
            V.memset(small[:, 47:48], 0.0).then_inc(xc_done, 1)
            for b0, n in FT_PAIRS:
                if b0 not in FT_ON_ACT:
                    src = v3(result(dve, ("ft", b0))[:, 0:n * SEQ], n)
                    if b0 in FT_GAIN:
                        g = COL_QK + FT_GAIN[b0]
                        ins = V.tensor_scalar(ft[:, b0:b0 + n, :], src, cols[:, g:g + 1], None, ALU.mult)
                    else:
                        ins = V.tensor_copy(ft[:, b0:b0 + n, :], src)
                    empties(ins, ("ft", b0))

            bank = result(dve, "cmp")
            step(V.tensor_copy(ckd[:, :, 0:HD], v3(bank[0:N_CMP, 0:2 * HD], 2)))
            empties(V.tensor_copy(vcmp, v3(bank[0:N_CMP, 2 * HD:4 * HD], 2)), "cmp")
            settle()
            sq = v3(scr[0:N_CMP, 0:2 * HD], 2)
            step(V.tensor_tensor(sq, ckd[:, :, 0:HD], ckd[:, :, 0:HD], ALU.mult))
            settle()
            step(V.memset(small[:, 20:22], 1.0))
            settle()
            step(V.tensor_reduce(small[0:N_CMP, 20:22], sq, AX, ALU.add))
            settle()
            V.tensor_scalar(small[:, 24:26], small[:, 20:22], 1.0 / HD, RMS_EPS, ALU.mult, ALU.add)\
                .then_inc(var_done, 1)
            inverse_root()
            r = small[:, 32:34]
            step(V.tensor_tensor(ckd[:, :, 0:HD], ckd[:, :, 0:HD],
                                 r[0:N_CMP, :].unsqueeze(2).broadcast_to([N_CMP, 2, HD]), ALU.mult))
            settle()
            V.tensor_copy(ckd[:, :, HD:P], ckd[:, :, 0:HD]).then_inc(ckd_done, 1)
            bank = result(dve, "kcT")
            src = bank[:, 0:2 * P].rearrange("p (g n) -> p g n", g=2)[:, :, 0:N_CMP]
            empties(V.tensor_scalar(kcT, src, cols[:, COL_QK + 3:COL_QK + 4], None, ALU.mult), "kcT")

            dve.wait_ge(bias_landed, 16)
            for qt in range(TT):
                nk = (qt + 1) * P
                for h in range(4):
                    wait_emptied(dve, ("I", qt, h % 2))
                    settle()
                    ins = V.scalar_tensor_tensor(score[qt], rel[:, h, 0:nk], z[:, qt, IW + h:IW + h + 1],
                                                 causal[:, SEQ - nk:SEQ] if h == 0 else score[qt],
                                                 ALU.mult, ALU.add)
                    if h < 3:
                        step(ins)
                ins.then_inc(rel_used, 1)
                dve.wait_ge(rel_used, qt + 1)

            def top_keys(i):
                qt, it = divmod(i, TOPK // 8)
                src = score[qt] if it == 0 else work[qt]
                settle()
                step(V.max(small[:, 40:48], src))
                settle()
                step(V.match_replace(work[qt], small[:, 40:48], src, TAKEN))
                if it == TOPK // 8 - 1:
                    settle()
                    step(V.tensor_scalar(selmask[qt], work[qt], 0.5 * TAKEN, NEG, ALU.is_gt, ALU.mult))

            dve.wait_ge(gates_done, 2 * TT)

            def logits(u):
                kind, qt, h = UNITS2[u]
                nk = (qt + 1) * P
                L = lbuf[:, u % 4, :]
                o = 64 + 16 * (u % 4)
                segs = unit_segments(kind, h)
                v = u - AHEAD - 1
                if v >= 0:
                    kk, q2, h2 = UNITS2[v]
                    nb2 = (q2 + 1) * len(unit_segments(kk, h2))
                    result(dve, ("PT2", v, "c" if kk == "B" else (nb2 - 1) // 4))
                for s, (qb, kb, bh, _) in enumerate(segs):
                    idx = {"A": SS_AQ + h, "B": SS_BQ + h, "C": SS_CQ + 4 * s + h}[kind]
                    bank = result(dve, ("S2", u, s // 2))
                    ins = V.scalar_tensor_tensor(L[:, s * nk:(s + 1) * nk], bank[:, (s % 2) * 256:(s % 2) * 256 + nk],
                                                 rs[:, qt, idx:idx + 1], bias[:, bh, SEQ - nk:SEQ], ALU.mult, ALU.add)
                    if s % 2 == 1 or s == len(segs) - 1:
                        empties(ins, ("S2", u, s // 2))
                        wait_emptied(dve, ("S2", u, s // 2))
                    else:
                        step(ins)
                if kind == "A":
                    step(V.tensor_tensor(L[:, 0:nk], L[:, 0:nk], selmask[qt], ALU.add))
                    settle()
                if kind == "B":
                    end = 2 * nk + N_CMP
                    empties(V.scalar_tensor_tensor(L[:, 2 * nk:end], result(dve, ("S2", u, "c"))[:, 0:N_CMP],
                                                   rs[:, qt, SS_BQ + h:SS_BQ + h + 1], cmp_mask[:, qt, :],
                                                   ALU.mult, ALU.add), ("S2", u, "c"))
                    step(V.tensor_reduce(small[:, o + 8:o + 10], v3(L[:, 0:2 * nk], 2), AX, ALU.max))
                    wait_emptied(dve, ("S2", u, "c"))
                    step(V.tensor_reduce(small[:, o + 10:o + 11], L[:, 2 * nk:end], AX, ALU.max))
                    settle()
                    V.tensor_scalar(small[:, o:o + 3], small[:, o + 8:o + 11], 0.1 * NEG, -1.0, ALU.max, ALU.mult)\
                        .then_inc(l_done, 1)
                else:
                    step(V.tensor_reduce(small[:, o + 8:o + 9], L[:, 0:len(segs) * nk], AX, ALU.max))
                    settle()
                    V.tensor_scalar(small[:, o:o + 1], small[:, o + 8:o + 9], -1.0, None, ALU.mult).then_inc(l_done, 1)

            def inv_sum(u):
                kind, qt, h = UNITS2[u]
                return 48 + 8 * qt + h

            def weigh(u):
                kind, qt, h = UNITS2[u]
                nk = (qt + 1) * P
                L = lbuf[:, u % 4, :]
                o = 64 + 16 * (u % 4)
                dve.wait_ge(exp2_done, u + 1)
                if kind != "B":
                    V.reciprocal(small[:, inv_sum(u):inv_sum(u) + 1], small[:, o + 4:o + 5]).then_inc(p_done, 1)
                    return
                step(V.tensor_scalar(small[:, o + 12:o + 15], small[:, o + 4:o + 7], 1e-30, None, ALU.max))
                settle()
                step(V.reciprocal(small[:, o + 8:o + 11], small[:, o + 12:o + 15]))
                settle()
                step(V.tensor_tensor(small[:, o + 12:o + 15], small[:, o + 8:o + 11], gates[:, qt, h, :], ALU.mult))
                settle()
                step(V.tensor_scalar(L[:, 0:nk], L[:, 0:nk], small[:, o + 12:o + 13], None, ALU.mult))
                step(V.tensor_scalar(L[:, nk:2 * nk], L[:, nk:2 * nk], small[:, o + 13:o + 14], None, ALU.mult))
                V.tensor_scalar(L[:, 2 * nk:2 * nk + N_CMP], L[:, 2 * nk:2 * nk + N_CMP], small[:, o + 14:o + 15],
                                None, ALU.mult).then_inc(p_done, 1)

            def outputs(u):
                kind, qt, h = UNITS2[u]
                heads = h + 1
                bank = result(dve, ("O2", kind, qt))
                src, dst = v3(bank[:, 0:heads * HD], heads), v3(o2_tok(kind, qt), heads)
                if kind == "B":
                    empties(V.tensor_copy(dst, src), ("O2", kind, qt))
                else:
                    r0 = inv_sum(u - h)
                    empties(V.tensor_tensor(dst, src, small[:, r0:r0 + heads].unsqueeze(2)
                                            .broadcast_to([P, heads, HD]), ALU.mult), ("O2", kind, qt))

            for u in range(AHEAD):
                logits(u)
            weigh(0)
            for u, (kind, qt, h) in enumerate(UNITS2):
                if u + 1 < len(UNITS2):
                    weigh(u + 1)
                if u + AHEAD < len(UNITS2):
                    logits(u + AHEAD)
                if u < TT * TOPK // 8:
                    top_keys(u)
                if u and UNITS2[u - 1][0:2] != (kind, qt):
                    outputs(u - 1)
            outputs(len(UNITS2) - 1)

            i = 0
            for nb in range(2):
                for br in range(3):
                    for tt in range(TT):
                        y = y_tok[:, tt, nb * NB:nb * NB + NB]
                        dve.wait_ge(sig_done, i + 1)
                        bank = result(dve, (f"branch{br}", nb, tt))
                        if i == 0:
                            wait_emptied(dve, ("oT2", "C", 1))
                        g = tmp[:, i % 2, :]
                        if br == 0:
                            empties(V.tensor_tensor(y, g, bank[:, :], ALU.mult), (f"branch{br}", nb, tt))
                            wait_emptied(dve, (f"branch{br}", nb, tt))
                        else:
                            t = lbuf[:, tt, 0:NB]
                            settle()
                            empties(V.tensor_tensor(t, g, bank[:, :], ALU.mult), (f"branch{br}", nb, tt))
                            wait_emptied(dve, (f"branch{br}", nb, tt))
                            ins = V.tensor_tensor(y, y, t, ALU.add)
                            if nb == 1 and br == 2 and tt == 1:
                                ins.then_inc(mix_done, 1)
                            else:
                                step(ins)
                        i += 1

            def residual(stage, signal=None):
                for nb in range(2):
                    split_to(last_panel(stage, nb) + (1 if nb else 2))
                    for tt in range(TT):
                        x = x_tok[:, tt, nb * NB:nb * NB + NB]
                        empties(V.tensor_tensor(x, x, result(dve, (stage, nb, tt))[:, :], ALU.add), (stage, nb, tt))
                        if nb == 1 and signal is not None:
                            wait_emptied(dve, (stage, 0, tt))
                            wait_emptied(dve, (stage, 1, tt))
                            V.memset(small[:, 47:48], 0.0).then_inc(signal, 1)

            split_to(last_panel("branch2", 1) + 2)
            lows("mixed", hT)
            residual("w_out", x_done)
            split_to(last_panel("w_out", 1) + 2)
            rms_input(2 * TT)
            lows("ffn2_h", hT, None, gain(COL_N2))
            ffn("ffn2")
            residual("ffn2_out")

        @block.gpsimd
        def _(pool):
            roots = [0]

            def pool_share(i):
                raw, hi, lo = raw_panel(i), panel_part(i, 0), panel_part(i, 1)
                wait_split(pool, i, hi_only=True)
                half = slice(0 if lo_by_pool[i] else panels[i][2] // 2, panels[i][2])
                nc.gpsimd.tensor_tensor(lo[:, half, :], raw[:, half, :], hi[:, half, :].bitcast(F32), ALU.subtract)\
                    .then_inc(w_pool, 1)

            split_to = splitter(pool_share)

            def inverse_root(src, dst, exponent):
                roots[0] += 1
                pool.wait_ge(var_done, roots[0])
                nc.gpsimd.tensor_tensor(dst, src, exponent, ALU.pow).then_inc(rstd_done, 1)

            def head_roots(lo, hi, tt):
                if tt == 0:
                    roots[0] += 1
                    pool.wait_ge(var_done, roots[0])
                ins = nc.gpsimd.tensor_tensor(rs[:, tt, lo:hi], ss[:, tt, lo:hi], neghalf[:, 0:hi - lo], ALU.pow)
                if tt == TT - 1:
                    ins.then_inc(rstd_done, 1)

            def token_root(dst=small[:, 32:34]):
                inverse_root(small[:, 24:26], dst, neghalf[:, 0:2])

            split_to(last_panel("qkv", 5) + 2)
            pool.wait_ge(consts_done, 1)
            for _ in range(4):
                inverse_root(small[:, 40:44], small[:, 32:36], neghalf[:, 0:4])
            for stage, nb in (("wo", 1), ("ffn0_out", 1), ("pool", 0), ("ffn1_out", 1)):
                split_to(last_panel(stage, nb) + 1)
                token_root()
                split_to(last_panel(stage, nb) + 2)
            split_to(last_panel("z", 0) + 1)
            token_root(rms_z)
            for (lo, hi), nb in zip(SS_PARTS, (6, 8, 9)):
                for tt in range(TT):
                    split_to(panel_at[("z", nb, tt)])
                    head_roots(lo, hi, tt)
            split_to(last_panel("z", 9) + 2)
            token_root()
            split_to(last_panel("w_out", 1) + 1)
            token_root()
            split_to(len(panels))

        @block.sync
        def _(sp):
            def row_load(dst, src, sem_):
                sp.dma_start(dst, src.partition_broadcast(P)).then_inc(sem_, 16)

            mod_panel(sp, 0)
            mod_panel(sp, 1)
            n1 = 48 * DEPTH
            small_loads = [
                (colsrc[0:n1, :], a["b_mod"].rearrange("l (n p) -> (l n) p", p=P)),
                (colsrc[COL_N1:COL_N1 + KC, :], a["norm1_g_2"].rearrange("l (n p) -> (l n) p", p=P)),
                (colsrc[COL_N2:COL_N2 + KC, :], a["norm2_g_2"].rearrange("l (n p) -> (l n) p", p=P)),
                (colsrc[COL_SUB:COL_SUB + 1, :], a["attn_subln_g"]),
                (colsrc[COL_QK:COL_QK + 6, 0:HD], a["qk_norm_g_2"][0]),
                (colsrc[COL_QK:COL_QK + 6, HD:P], a["qk_norm_g_2"][0]),
                (possrc, a["nsa_cmp_pos_2"][0].rearrange("v (l j) d -> (v l) (j d)", j=2)),
                (oh_sb, a["const_onehot"]),
                (rm_sb, a["const_rowmask"]),
                (rel_sb, a["rel_bias_2"]),
            ] + [(lnsrc[(2 * l + i) * KC:(2 * l + i + 1) * KC, :], a[w][l, 0, :].rearrange("(n p) -> n p", p=P))
                 for l in range(2) for i, w in enumerate(("ln_g", "ln_b"))] + \
                [(lnsrc[(4 + i) * KC:(5 + i) * KC, :], a[w][1, 1, :].rearrange("(n p) -> n p", p=P))
                 for i, w in enumerate(("ln_g", "ln_b"))]
            assert len(small_loads) == N_SMALL_LOADS
            for dst, src in small_loads:
                sp.dma_start(dst, src).then_inc(cols_landed, 16)
            sp.dma_start(table[:, :], a["const_table"]).then_inc(table_landed, 16)
            sp.dma_start(x_tok, a["x"][0].rearrange("(t p) d -> p t d", p=P)).then_inc(x_landed, 16)
            sp.dma_start(y_tok, a["ctx"][0].rearrange("(t p) d -> p t d", p=P)).then_inc(ctx_landed, 16)
            row_load(lam_in, a["attn_lambda"][0], lam_landed)
            mod_panel(sp, 2)
            mod_panel(sp, 3)
            mods_before = {RING: [4, 5], 5: [6], 6: [7]}
            for e in range(8, N_EVENTS):
                at = min(event_panel[e - 4] + (5 if e < 16 else 7), event_panel[e - 2] + 3)
                mods_before.setdefault(at, []).append(e)
            for i, (key, srcs, chunks, width) in enumerate(panels):
                for e in mods_before.get(i, []):
                    mod_panel(sp, e)
                if i >= RING:
                    sp.wait_ge(*done[i - RING])
                slot = raw_panel(i)
                for src, lo, n in srcs:
                    sp.dma_start(slot[:, :, lo:lo + n], src).then_inc(w_landed[i % RING], 16)
                if i == RING:
                    for comp, row in ((2, g1row), (5, g2row)):
                        row_load(row, a["b_mod"][0, comp * D:(comp + 1) * D], g_landed[comp])
                    for r, w in enumerate(("ln_g", "ln_b")):
                        row_load(ln_rows[:, r, :], a[w][0, 0, :], ln_landed)
                if key == ("ffn1_in", 2, 0):
                    sp.wait_ge(srow_stored, 16)
                    sp.wait_ge(mod_acc, N_EVENTS - FIRST_DVE_EVENT)
                    sp.dma_start(bias, bass.AP(scratch.tensor, P - 1, [[SROW - 1, P], [P * SROW, REL_HEADS], [1, SEQ]]))\
                        .then_inc(bias_landed, 16)
            for tt in range(TT):
                wait_emptied(sp, ("ffn2_out", 1, tt))
                sp.dma_start(out[0, tt * P:(tt + 1) * P, :], x_tok[:, tt, :]).then_inc(out_stored, 16)
            sp.wait_ge(out_stored, 16 * TT)


_INS = ["x", "c", "ctx", "c_ctx", "w_mod", "b_mod", "ln_g", "ln_b", "attn_w_qkv", "attn_lambda",
        "attn_subln_g", "attn_w_o", "pool_w", "pool_scale", "ffn_w_in", "ffn_w_out", "norm1_g_2",
        "norm2_g_2", "w_in_2", "qk_norm_g_2", "nsa_cmp_pos_2", "nsa_cmp_w_2", "w_branch_a_2",
        "w_branch_b_2", "w_branch_c_2", "w_out_2", "w_ffn_in_2", "w_ffn_out_2", "rel_bias_2"]


def kernel(**inputs):
    import concourse.bacc as _bacc
    from concourse.bass_utils import run_bass_kernel_spmd as _run

    nc = _bacc.Bacc("TRN2", target_bir_lowering=False, num_devices=1)
    arrays = {f"in_{n}": np.ascontiguousarray(inputs[n]) for n in _INS}
    arrays.update(shape_constants())
    args = {n.removeprefix("in_"): nc.dram_tensor(n, v.shape, F32, kind="ExternalInput").ap()
            for n, v in arrays.items()}
    out = nc.dram_tensor("out", (1, SEQ, D), F32, kind="ExternalOutput").ap()
    scratch = nc.dram_tensor("bias_rows", (REL_HEADS, P, SROW), F32, kind="Internal").ap()
    build(nc, args, out, scratch)
    return _run(nc, [arrays], core_ids=[0]).results[0]["out"]
```
